# Optimizing a Trainium2 kernel written in Bass

```python
import jax
import jax.numpy as jnp
from jax import lax
import numpy as np

D_MODEL = 2048
BATCH = 1
SEQ = 512
DEPTH = 1
DEC_BATCH = 8
DEC_SEQ = 1
PAST_LEN = 1024
PAGE_SIZE = 128

N_META = 16
N_Q_HEADS = 8
N_KV_HEADS = 4
HEAD_DIM = 128
GROUP = N_Q_HEADS // N_KV_HEADS
ATTN_WIDTH = N_Q_HEADS * HEAD_DIM
KV_WIDTH = N_KV_HEADS * HEAD_DIM
N_IDX_HEADS = 8
IDX_DIM = 64
TOPK_MAX = 256
N_HG_HEADS = 8
HG_DK = 128
HG_DV = 128
HG_WIDTH = N_HG_HEADS * HG_DV
MIX_WIDTH = ATTN_WIDTH + HG_WIDTH
BLOCK = 128
D_FF = -(-8 * D_MODEL // (3 * 256)) * 256
IN_WIDTHS = (ATTN_WIDTH, KV_WIDTH, KV_WIDTH, N_IDX_HEADS * IDX_DIM, N_IDX_HEADS, IDX_DIM,
             N_HG_HEADS * HG_DK, N_HG_HEADS * HG_DK, HG_WIDTH, HG_WIDTH)
IN_WIDTH = sum(IN_WIDTHS)
ATTN_SCALE = HEAD_DIM ** -0.5
IDX_SCALE = IDX_DIM ** -0.5
IDX_W_SCALE = N_IDX_HEADS ** -0.5
LN_EPS = 1e-5
NORM_EPS = 1e-6
ALPHA = (2 * DEPTH) ** 0.25
BETA = (8 * DEPTH) ** -0.25

kernel_name = 'hymba_dsa_hgrn2_decode_step'

def layer_norm(x, g, b):
    xf = x.astype(jnp.float32)
    mu = jnp.mean(xf, -1, keepdims=True)
    var = jnp.mean(jnp.square(xf - mu), -1, keepdims=True)
    y = (xf - mu) * lax.rsqrt(var + LN_EPS) * g.astype(jnp.float32) + b.astype(jnp.float32)
    return y.astype(x.dtype)

def split_points():
    return [int(s) for s in np.cumsum(IN_WIDTHS)[:-1]]

def project(h, w_in, lb):
    B, T, _ = h.shape
    f32 = jnp.float32
    z = h @ w_in
    q, k, v, qi, wi, ki, hq, hf, hi, hg = jnp.split(z, split_points(), axis=-1)
    q = q.reshape(B, T, N_Q_HEADS, HEAD_DIM)
    k = k.reshape(B, T, N_KV_HEADS, HEAD_DIM)
    v = v.reshape(B, T, N_KV_HEADS, HEAD_DIM)
    qi = qi.reshape(B, T, N_IDX_HEADS, IDX_DIM)
    wi = wi.astype(f32) * IDX_W_SCALE
    fg = lb + (1.0 - lb) * jax.nn.sigmoid(hf.astype(f32))
    log_f = jnp.log(fg).reshape(B, T, N_HG_HEADS, HG_DK)
    kf = (1.0 - fg).reshape(B, T, N_HG_HEADS, HG_DK)
    hq = jax.nn.silu(hq.astype(f32)).reshape(B, T, N_HG_HEADS, HG_DK)
    hi = hi.astype(f32).reshape(B, T, N_HG_HEADS, HG_DV)
    return q, k, v, qi, wi, ki, hq, kf, hi, log_f, hg

def indexer_topk(qi, wi, q_pos, ki, n_keep):
    s = jnp.einsum('bqhd,bld->bqhl', qi, ki).astype(jnp.float32) * IDX_SCALE
    s = jnp.einsum('bqhl,bqh->bql', jax.nn.relu(s), wi)
    key_pos = jnp.arange(ki.shape[1])
    s = jnp.where(key_pos[None, None, :] <= q_pos[None, :, None], s, -jnp.inf)
    return lax.top_k(s, n_keep)[1]

def alibi_slopes():
    return jnp.exp2(-8.0 * jnp.arange(1, N_Q_HEADS + 1, dtype=jnp.float32) / N_Q_HEADS)

def attend(q, k_sel, v_sel, idx, q_pos):
    B, Q = q.shape[:2]
    qg = q.reshape(B, Q, N_KV_HEADS, GROUP, HEAD_DIM)
    logits = jnp.einsum('bqkgd,bqnkd->bqkgn', qg, k_sel).astype(jnp.float32) * ATTN_SCALE
    dist = (q_pos[None, :, None] - idx).astype(jnp.float32)[:, :, None, None, :]
    slopes = alibi_slopes().reshape(1, 1, N_KV_HEADS, GROUP, 1)
    logits = jnp.where(dist >= 0, logits - slopes * dist, -jnp.inf)
    p = jax.nn.softmax(logits, axis=-1).astype(v_sel.dtype)
    o = jnp.einsum('bqkgn,bqnkd->bqkgd', p, v_sel)
    return o.reshape(B, Q, ATTN_WIDTH)

def take_rows(rows, idx):
    return jax.vmap(lambda r, i: r[i])(rows, idx)

def gather_paged(pool, layer, page_table, new_rows, idx):
    is_past = idx < PAST_LEN
    ip = jnp.where(is_past, idx, 0)
    phys = page_table[jnp.arange(idx.shape[0])[:, None, None], ip // PAGE_SIZE]
    rows_past = pool[layer, phys, ip % PAGE_SIZE]
    rows_new = take_rows(new_rows, jnp.where(is_past, 0, idx - PAST_LEN))
    mask = is_past.reshape(is_past.shape + (1,) * (rows_past.ndim - is_past.ndim))
    return jnp.where(mask, rows_past, rows_new.astype(rows_past.dtype))

def hgrn2_chunk(S0, q, kf, i, log_f):
    C = q.shape[1]
    b = jnp.cumsum(log_f, axis=1)
    causal = jnp.tril(jnp.ones((C, C), dtype=bool))[None, :, :, None, None]
    decay = jnp.exp(jnp.where(causal, b[:, :, None] - b[:, None, :], -jnp.inf))
    a = jnp.einsum('btshd,bshd->bhts', q[:, :, None] * decay, kf)
    o = jnp.einsum('bhts,bshv->bthv', a, i) + jnp.einsum('bthd,bhdv->bthv', q * jnp.exp(b), S0)
    b_end = b[:, -1]
    S = S0 * jnp.exp(b_end)[..., None] + jnp.einsum('bshd,bshv->bhdv', kf * jnp.exp(b_end[:, None] - b), i)
    return S, o

def merge_heads(attn_o, hg_o, hg_gate, norm_g, w_out):
    B, T = attn_o.shape[:2]
    o = hg_o * lax.rsqrt(jnp.mean(jnp.square(hg_o), -1, keepdims=True) + NORM_EPS) * norm_g.astype(jnp.float32)
    o = o.reshape(B, T, HG_WIDTH) * jax.nn.silu(hg_gate.astype(jnp.float32))
    return jnp.concatenate([attn_o, o.astype(attn_o.dtype)], axis=-1) @ w_out

def swiglu(h, wg, wu, wd):
    return (jax.nn.silu(h @ wg) * (h @ wu)) @ wd

def to_blocks(a):
    r = a[:, N_META:]
    nb = r.shape[1] // BLOCK
    return jnp.moveaxis(r.reshape((r.shape[0], nb, BLOCK) + r.shape[2:]), 1, 0)

def from_blocks(a):
    a = jnp.moveaxis(a, 0, 1)
    return a.reshape((a.shape[0], a.shape[1] * a.shape[2]) + a.shape[3:])

def setup_inputs(seed: int = 0) -> dict:
    key = jax.random.key(seed)
    ks = jax.random.split(key, 24)
    n_pages = PAST_LEN // PAGE_SIZE
    n_pool = (DEC_BATCH * n_pages * 5 + 3) // 4
    f32 = jnp.float32

    def nrm(k, shape, scale):
        return jax.random.normal(k, shape, f32) * scale

    page_table = jax.random.permutation(ks[6], n_pool)[:DEC_BATCH * n_pages]
    page_table = page_table.reshape(DEC_BATCH, n_pages).astype(jnp.int32)
    return {
        'x_prompt': nrm(ks[0], (BATCH, SEQ, D_MODEL), 1.0),
        'x_sample': nrm(ks[1], (DEC_BATCH, DEC_SEQ, D_MODEL), 1.0),
        'cache_k': nrm(ks[2], (DEPTH, n_pool, PAGE_SIZE, N_KV_HEADS, HEAD_DIM), 1.0),
        'cache_v': nrm(ks[3], (DEPTH, n_pool, PAGE_SIZE, N_KV_HEADS, HEAD_DIM), 1.0),
        'cache_kidx': nrm(ks[4], (DEPTH, n_pool, PAGE_SIZE, IDX_DIM), 1.0),
        'state_hgrn': nrm(ks[5], (DEPTH, DEC_BATCH, N_HG_HEADS, HG_DK, HG_DV), 0.5),
        'page_table': page_table,
        'meta_tokens': nrm(ks[7], (N_META, D_MODEL), 1.0),
        'ln_in_g': 1.0 + nrm(ks[8], (D_MODEL,), 0.02),
        'ln_in_b': nrm(ks[9], (D_MODEL,), 0.02),
        'w_in': nrm(ks[10], (DEPTH, D_MODEL, IN_WIDTH), D_MODEL ** -0.5),
        'hg_lb_logits': nrm(ks[11], (DEPTH + 1, N_HG_HEADS * HG_DK), 0.5),
        'hg_norm_g': 1.0 + nrm(ks[12], (DEPTH, HG_DV), 0.02),
        'w_out': nrm(ks[13], (DEPTH, MIX_WIDTH, D_MODEL), MIX_WIDTH ** -0.5 * BETA),
        'ln1_g': 1.0 + nrm(ks[14], (DEPTH, D_MODEL), 0.02),
        'ln1_b': nrm(ks[15], (DEPTH, D_MODEL), 0.02),
        'w_gate': nrm(ks[16], (DEPTH, D_MODEL, D_FF), D_MODEL ** -0.5),
        'w_up': nrm(ks[17], (DEPTH, D_MODEL, D_FF), D_MODEL ** -0.5),
        'w_down': nrm(ks[18], (DEPTH, D_FF, D_MODEL), D_FF ** -0.5 * BETA),
        'ln2_g': 1.0 + nrm(ks[19], (DEPTH, D_MODEL), 0.02),
        'ln2_b': nrm(ks[20], (DEPTH, D_MODEL), 0.02),
    }

def reference(x_prompt, x_sample, cache_k, cache_v, cache_kidx, state_hgrn, page_table,
              meta_tokens, ln_in_g, ln_in_b, w_in, hg_lb_logits, hg_norm_g, w_out,
              ln1_g, ln1_b, w_gate, w_up, w_down, ln2_g, ln2_b):
    f32 = jnp.float32
    lb_all = jnp.cumsum(jax.nn.softmax(hg_lb_logits.astype(f32), axis=0), axis=0)

    B = x_prompt.shape[0]
    T = N_META + x_prompt.shape[1]
    meta = jnp.broadcast_to(meta_tokens[None], (B, N_META, D_MODEL)).astype(x_prompt.dtype)
    x = layer_norm(jnp.concatenate([meta, x_prompt], axis=1), ln_in_g, ln_in_b)
    n_keep_p = min(TOPK_MAX, T // 4)
    pos_p = jnp.arange(T)
    real_pos = pos_p[N_META:].reshape(-1, BLOCK)
    k_p, v_p, ki_p, s_p = [], [], [], []
    for l in range(DEPTH):
        q, k, v, qi, wi, ki, hq, kf, hi, log_f, hg = project(x, w_in[l], lb_all[l])

        def attn_block(args):
            qb, qib, wib, posb = args
            idx = indexer_topk(qib, wib, posb, ki, n_keep_p)
            return attend(qb, take_rows(k, idx), take_rows(v, idx), idx, posb)

        o_meta = attn_block((q[:, :N_META], qi[:, :N_META], wi[:, :N_META], pos_p[:N_META]))
        o_real = from_blocks(lax.map(attn_block, (to_blocks(q), to_blocks(qi), to_blocks(wi), real_pos)))
        attn_o = jnp.concatenate([o_meta, o_real], axis=1)

        S = jnp.zeros((B, N_HG_HEADS, HG_DK, HG_DV), f32)
        S, h_meta = hgrn2_chunk(S, hq[:, :N_META], kf[:, :N_META], hi[:, :N_META], log_f[:, :N_META])
        S, h_real = lax.scan(lambda c, a: hgrn2_chunk(c, *a), S,
                             (to_blocks(hq), to_blocks(kf), to_blocks(hi), to_blocks(log_f)))
        hg_o = jnp.concatenate([h_meta, from_blocks(h_real)], axis=1)

        mix = merge_heads(attn_o, hg_o, hg, hg_norm_g[l], w_out[l])
        x = layer_norm(ALPHA * x + mix, ln1_g[l], ln1_b[l])
        x = layer_norm(ALPHA * x + swiglu(x, w_gate[l], w_up[l], w_down[l]), ln2_g[l], ln2_b[l])
        k_p.append(k)
        v_p.append(v)
        ki_p.append(ki)
        s_p.append(S.astype(x_prompt.dtype))
    y_prompt = x[:, N_META:]

    xs = layer_norm(x_sample, ln_in_g, ln_in_b)
    DB, SQ = x_sample.shape[:2]
    n_keep_s = min(TOPK_MAX, (PAST_LEN + SQ) // 4)
    pos_s = PAST_LEN + jnp.arange(SQ)
    k_s, v_s, ki_s, s_s = [], [], [], []
    for l in range(DEPTH):
        q, k, v, qi, wi, ki, hq, kf, hi, log_f, hg = project(xs, w_in[l], lb_all[l])
        ki_past = cache_kidx[l, page_table].reshape(DB, PAST_LEN, IDX_DIM)
        ki_all = jnp.concatenate([ki_past, ki.astype(ki_past.dtype)], axis=1)
        idx = indexer_topk(qi, wi, pos_s, ki_all, n_keep_s)
        k_sel = gather_paged(cache_k, l, page_table, k, idx)
        v_sel = gather_paged(cache_v, l, page_table, v, idx)
        attn_o = attend(q, k_sel, v_sel, idx, pos_s)

        S, hg_o = hgrn2_chunk(state_hgrn[l].astype(f32), hq, kf, hi, log_f)

        mix = merge_heads(attn_o, hg_o, hg, hg_norm_g[l], w_out[l])
        xs = layer_norm(ALPHA * xs + mix, ln1_g[l], ln1_b[l])
        xs = layer_norm(ALPHA * xs + swiglu(xs, w_gate[l], w_up[l], w_down[l]), ln2_g[l], ln2_b[l])
        k_s.append(k)
        v_s.append(v)
        ki_s.append(ki)
        s_s.append(S.astype(state_hgrn.dtype))
    y_sample = xs

    return (y_prompt, y_sample,
            jnp.stack(k_p), jnp.stack(v_p), jnp.stack(ki_p), jnp.stack(s_p),
            jnp.stack(k_s), jnp.stack(v_s), jnp.stack(ki_s), jnp.stack(s_s))


_drawn_inputs = setup_inputs


def setup_inputs(seed=0):
    import zlib

    import numpy as np

    out = dict(_drawn_inputs(seed))
    spreads = {}
    factors = {}
    for name, (base, spread) in spreads.items():
        noise = np.random.default_rng([zlib.crc32(name.encode()), seed]).standard_normal(out[name].shape)
        drawn = base * np.exp(spread * noise) if base else spread * noise
        out[name] = jnp.asarray(drawn.astype(out[name].dtype))
    for name, factor in factors.items():
        out[name] = (out[name] * factor).astype(out[name].dtype)
    return out
```

```python
from contextlib import ExitStack

import concourse.bass as bass
from concourse import mybir

ALU = mybir.AluOpType
ACT = mybir.ActivationFunctionType
AX = mybir.AxisListType.X
F32 = mybir.dt.float32
F32R = mybir.dt.float32r
BF16 = mybir.dt.bfloat16
I32 = mybir.dt.int32
U32 = mybir.dt.uint32

P = 128
D = 2048
KD = D // P
NS = 8
NM = 16
NR = 512
NB = NR // P
M0 = NS
R0 = NS + NM
NT = NS + NM + NR
HALF = NT // 2
HD = 128
NG = 4
NH = 8
PAST = 1024
KEEP_P = (NM + NR) // 4
KEEP_S = 256
NBLK = KEEP_S // P
FF = 5632
FC = 4
NC = FF // (FC * P)
ALPHA = 2.0 ** 0.25
ATTN_SCALE = HD ** -0.5
IDX_SCALE = 64 ** -0.5
IDX_W_SCALE = NH ** -0.5
LN_EPS = 1e-5
NORM_EPS = 1e-6
INADMISSIBLE = -3.0e38
TAKEN = -3.4e38
OFF = -1.0e30
SIG_CAP = 1.0e18
SUB = 32
W_COLS = {"q": 0, "k": 1024, "v": 1536, "qi": 2048, "wk": 2560, "hq": 2632, "hf": 3656, "hi": 4680, "hg": 5704}
WIDE = [NM + P * i for i in range(1, NB + 1)]
WOFF = [sum(WIDE[:i]) for i in range(NB)]
S_C = 5
S_B = S_C + 4 * NH
S_D1 = S_B + 4 * NG
S_D2 = S_D1 + 8
S_E = S_D2 + 8
T_D1, T_D2 = S_D1, S_D1 + 16
T_E = T_D2 + 16


class At:

    def __init__(self, const, coef=0, reg=None):
        self.const, self.coef, self.reg = const, coef, reg

    def __add__(self, k):
        return At(self.const + k, self.coef, self.reg)

    def __sub__(self, k):
        return self + (-k)

    def half(self):
        return At(self.const // 2, self.coef // 2, self.reg)

    def times(self, k):
        return At(self.const * k, self.coef * k, self.reg)

    @property
    def odd(self):
        return self.const % 2

    @property
    def v(self):
        return self.const if self.reg is None else self.reg * self.coef + self.const


class Chain:

    def __init__(self, eng, sem, start=0):
        self.eng, self.sem, self.start, self.n = eng, sem, start, 0

    def __call__(self, ins):
        self.n += 1
        ins.then_inc(self.sem, 1)
        self.eng.wait_ge(self.sem, self.start + self.n)


def wait_apart(eng, sem, value, seen):
    eng.wait_ge(sem, value)
    eng.sem_inc(seen, 1)


def hymba_kernel(nc, *arrays):
    with ExitStack() as ctx:
        program(ctx, nc, *arrays)


def program(
    ctx, nc: bass.Bass, x_prompt, x_sample, cache_k, cache_v, cache_kidx, state_hgrn, page_table, meta_tokens,
    ln_in_g, ln_in_b, w_in, hg_lb_logits, hg_norm_g, w_out, ln1_g, ln1_b, w_gate, w_up, w_down, ln2_g, ln2_b,
    y_prompt, y_sample, k_prompt, v_prompt, kidx_prompt, hgrn_prompt, k_sample, v_sample, kidx_sample, hgrn_sample,
):
    sems = {}

    def sem(name):
        if name not in sems:
            sems[name] = ctx.enter_context(nc.semaphore(name))
        return sems[name]

    BASE = 16512

    def at(name, shape, dt, off):
        return nc.alloc_sbuf_tensor_at(name, shape, dt, offset=BASE + off)

    class Region:

        def __init__(self, start, size):
            self.pos, self.end = start, start + size

        def take(self, name, shape, dt=F32):
            n = 2 if dt == BF16 else 4
            for d in shape[1:]:
                n *= d
            n = (n + 31) // 32 * 32
            t = at(name, shape, dt, self.pos)
            self.pos += n
            assert self.pos <= self.end, (name, self.pos, self.end)
            return t

    TILE = NT * 4
    O_RAW = 2 * KD * TILE
    O_WH = O_RAW + 16384
    O_WL = O_WH + 16384
    O_SACC = O_WL + 16384
    O_ATT = O_SACC + KD * TILE
    O_R = O_ATT + NH * TILE
    TOP = 229344 - BASE

    xh = at("xh", [P, KD, NT], F32R, 0)
    xl = at("xl", [P, KD, NT], F32R, KD * TILE)
    raw = at("raw", [P, 2, 2048], F32, O_RAW)
    wh = at("wh", [P, 2, 2048], F32R, O_WH)
    wl = at("wl", [P, 2, 2048], F32R, O_WL)
    sacc = at("sacc", [P, KD, NT], F32, O_SACC)
    attn_o = at("attn_o", [P, NH, NT], F32, O_ATT)

    rr_ = Region(O_R, TOP - O_R)
    ident = rr_.take("ident", [P, P])
    ones = rr_.take("ones", [P, P])
    dist = rr_.take("dist", [P, 528])
    tri = rr_.take("tri", [P, P])
    causal = rr_.take("causal", [P, P])
    vec = rr_.take("vec", [P, 113])
    lb = rr_.take("lb", [P, 24])
    keepmask = rr_.take("keepmask", [P, sum(WIDE)], BF16)
    halfsel = rr_.take("halfsel", [P, 2])
    pageof = rr_.take("pageof", [8, P])
    pmod = rr_.take("pmod", [P, 8])
    ptT = rr_.take("ptT", [8, 8])
    ptB = rr_.take("ptB", [8, 8])
    pt_i = rr_.take("pt_i", [8, 2, 8], I32)
    grow = rr_.take("grow", [P, NBLK, NS], U32)
    slope8 = rr_.take("slope8", [8, NH])
    zt = rr_.take("zt", [8, 2 * NS - 1])
    R_START = rr_.pos
    mid = O_SACC + NH * TILE

    xtok = at("xtok", [P, NB, D], F32, O_SACC)
    xtok_s = at("xtok_s", [R0, D], F32, O_ATT)
    r0 = Region(R_START, TOP - R_START)
    vrows = r0.take("vrows", [113, P])
    bn = r0.take("bn", [P, 5, 4, 6])
    mv = r0.take("mv", [P, 5, 2])
    lnt = r0.take("lnt", [P, 2, NT])

    ra = Region(O_SACC, NH * TILE)
    rb = Region(R_START, TOP - R_START)
    qT = [ra.take("q0T", [P, 2, NT]), rb.take("q1T", [P, 2, NT])]
    kT = [ra.take("k0T", [P, NT]), rb.take("k1T", [P, NT])]
    vtok = [ra.take("v0tok", [P, 6, P]), rb.take("v1tok", [P, 6, P])]
    vT = ra.take("vT", [P, NT])
    ktok = ra.take("ktok", [P, 6, P])
    lg = rb.take("lg", [P, 2, 528])
    pT = rb.take("pT", [P, 2, NR])
    pTm = rb.take("pTm", [NM, 2 * P + 2 * NM])
    lgm = rb.take("lgm", [NM, 2, NM])
    nmx = rb.take("nmx", [P, 2, 2])
    nmxm = rb.take("nmxm", [NM, 2, 2])
    distS = rb.take("distS", [NS, KEEP_S + 1])
    maskS = rb.take("maskS", [NS, KEEP_S + 1])
    nsl = rb.take("nsl", [NS, NS, NH])
    tmp = rb.take("tmp", [P, 2, NT])
    work = rb.take("work", [NS, 4, KEEP_S])
    vnew = rb.take("vnew", [NS, NG, P])
    assert rb.pos <= R_START + 33408
    qpad = at("qpad", [P, NG, NS, NH], F32, R_START + 33408)
    knew = at("knew", [P, NG, NS], F32, R_START + 34432)
    assert R_START + 34432 + 128 <= TOP
    kgs = at("kgs", [P, 2, NBLK, NG * P], F32, 0)
    vgs = at("vgs", [P, 2, NBLK, NG * P], F32, 8192)
    kgT = at("kgT", [P, NBLK, NG, P], F32, KD * TILE)
    ps = at("ps", [NH, KEEP_S + 1], F32, KD * TILE + 4096)
    pz = at("pz", [NH, 2 * NS - 1], F32, KD * TILE + 5152)
    pTs = at("pTs", [P, 24], F32, KD * TILE + 5216)
    snm = at("snm", [NH, 2], F32, KD * TILE + 5344)

    rc = Region(O_ATT, NH * TILE)
    bcum = rc.take("bcum", [P, NT])
    kf = rc.take("kf", [P, NT])
    hq = rc.take("hq", [P, NT])
    gate = rc.take("gate", [P, NT])
    hiT = rc.take("hiT", [P, NT])
    qd = rc.take("qd", [P, NT])
    qe = rc.take("qe", [P, NT])
    ke = rc.take("ke", [P, NT])
    rd = Region(R_START, TOP - R_START)
    t1 = rd.take("t1", [P, NT])
    t2 = rd.take("t2", [P, NT])
    et = rd.take("et", [P, 4 * (32 + 64 + 96 + 128) + NM])
    itok = rd.take("itok", [P, 6, P])
    ketok = rd.take("ketok", [P, 5, P])
    aT = rd.take("aT", [P, NB, P])
    aTm = rd.take("aTm", [NM, NM])
    st = rd.take("st", [P, NB + 1, P])
    ss = rd.take("ss", [P, NS, P])
    cur = rd.take("cur", [P, sum(WIDE)])
    curs = rd.take("curs", [NS, PAST + 1])
    idx = at("idx", [NS, KEEP_S], U32, ra.pos)
    fs = at("fs", [P, NS], F32, ra.pos + 1024)
    eb = at("eb", [P, NB], F32, ra.pos + 1056)
    top8 = at("top8", [P, NB, 8], F32, ra.pos + 1088)
    tops = at("tops", [NS, 8], F32, ra.pos + 1216)
    topi = at("topi", [NS, 8], U32, ra.pos + 1248)
    assert ra.pos + 1280 <= O_SACC + NH * TILE

    ri = Region(mid, NH * TILE)
    qiT = ri.take("qiT", [P, 4, NT])
    wikiT = ri.take("wikiT", [72, NT])
    kiT = ri.take("kiT", [P, NT])
    wk = ri.take("wk", [P, 6, 136])
    ri2 = Region(O_SACC, NH * TILE - 2432)
    rel = ri2.take("rel", [P, 2, 528])
    kx = ri2.take("kx", [P, 2, 512])
    kxT = ri2.take("kxT", [P, 2, 512])
    qS = ri.take("qS", [P, NS, NH])
    wsel = ri.take("wsel", [NS, NS, NH])
    wbc = ri.take("wbc", [P, NS, NH])
    prod = rd.take("prod", [P, 4, NS])
    isc = rd.take("isc", [P, 2, NS, 4])
    krow = rd.take("krow", [P, NS], U32)
    rsc = ri2.take("rsc", [P, 2, 256])
    nsc = rd.take("nsc", [NS, NH])

    re_ = Region(O_ATT, TOP - O_ATT)
    hh = re_.take("hh", [P, FC, NT], F32R)
    hl = re_.take("hl", [P, FC, NT], F32R)
    rf = Region(R_START, TOP - R_START)
    ssum = rf.take("ssum", [P, 2, NT])
    sq = rf.take("sq", [P, 2, NT])
    mu = rf.take("mu", [P, NT])
    rstd = rf.take("rstd", [P, NT])
    lnd = rf.take("lnd", [P, 2, NT])
    gbuf = rf.take("gbuf", [P, 2, NT])
    hbuf = rf.take("hbuf", [P, 2, NT])
    ytok = at("ytok", [P, NB + 1, D], F32, 0)

    acc = ctx.enter_context(nc.psum_tensor("acc", [P, 2, 2, 512], F32))
    b4 = ctx.enter_context(nc.psum_tensor("b4", [P, 512], F32))
    b5 = ctx.enter_context(nc.psum_tensor("b5", [P, 512], F32))
    b6 = ctx.enter_context(nc.psum_tensor("b6", [P, 512], F32))
    b7 = ctx.enter_context(nc.psum_tensor("b7", [P, 512], F32))

    def whole(t):
        return acc[:, t.odd, :, 0:HALF]

    def cut(ap):
        return ap.rearrange("p (a n) -> p a n", a=2)

    def fr(ap):
        return ap.bitcast(F32)

    def mts(s):
        if s.reg is None and s.const >= S_D1:
            return At(T_D1 + 2 * (s.const - S_D1 + 1))
        assert s.const < S_D1
        return s + 1

    w_in3 = w_in[0].rearrange("(k p) n -> p k n", p=P)
    wo3 = w_out[0].rearrange("(k p) n -> p k n", p=P)

    def sC(h, j):
        return h + (S_C + j)

    HG = ("hf", "hq", "hi", "hg")

    Y_ACT = [len([u for u in range(5 * q + 5) if u % 2 == 0]) for q in range(4)]
    Y_DVE = [len([u for u in range(5 * q + 5) if u % 2 == 1]) for q in range(4)]

    def y_bank(u):
        u %= 8
        return (b4, b5, b6, b7)[u][:, :] if u < 4 else acc[:, (u - 4) // 2, u % 2, :]

    def e_used(n, c):
        return At(T_E + (n + 1 if n < 8 else 8 + 4 * (n - 7)), 24, c) if not isinstance(c, int) \
            else At(T_E + 24 * c + (n + 1 if n < 8 else 8 + 4 * (n - 7)))

    def e_tile(n, c):
        return At(S_E + n, 12, c) if not isinstance(c, int) else At(S_E + n + 12 * c)

    def e_result(n, i, c):
        k = n if n < 8 else 8 + 4 * (n - 8) + i
        return At(T_E + k, 24, c) if not isinstance(c, int) else At(T_E + k + 24 * c)

    def e_before(n, c):
        if n >= 2:
            return e_used(n - 2, c)
        if isinstance(c, int) and c == 0:
            return At(T_E - 2 * (1 - n))
        return e_used(n + 10, c) - 24

    def d2_before(n, n2):
        return At(T_D2 + 2 * (n - 1) , 4, n2) if not isinstance(n2, int) else At(T_D2 + 2 * (n - 1) + 4 * n2)

    block = ctx.enter_context(nc.Block())

    @block.sync
    def _(sp):
        def load(s, dst, src):
            if s.reg is not None or s.const >= 2:
                sp.wait_ge(sem("l_split"), (s - 1).v)
            sp.dma_start(dst, src).then_inc(sem(f"w_in{s.odd}"), 16)

        def raw_at(s, k, n):
            return raw[:, s.odd, 0:k * n].rearrange("p (k n) -> p k n", k=k)

        sp.dma_start(xtok_s[0:NS, :], x_sample[:, 0, :]).then_inc(sem("x_in4"), 16)
        sp.dma_start(xtok_s[M0:R0, :], meta_tokens).then_inc(sem("x_in4"), 16)
        for c in range(NB):
            sp.dma_start(xtok[:, c, :], x_prompt[0, P * c:P * c + P, :]).then_inc(sem(f"x_in{c}"), 16)
        for i in range(4):
            load(At(i), raw_at(At(i), KD, P), w_in3[:, :, W_COLS["qi"] + P * i:W_COLS["qi"] + P * i + P])
        load(At(4), raw_at(At(4), KD, 72), w_in3[:, :, W_COLS["wk"]:W_COLS["wk"] + 72])

        def head_loads(h4, reg):
            for j in range(4):
                c = W_COLS[HG[j]]
                src = w_in3[:, :, c:c + P] if reg is None else w_in3[:, :, bass.ds(reg * P + c, P)]
                load(h4 + S_C + j, raw_at(h4 + S_C + j, KD, P), src)

        head_loads(At(0), None)
        with sp.Fori(1, NH, 1) as h:
            head_loads(At(0, 4, h), h)
        for g in range(NG):
            for j, c in enumerate((W_COLS["k"] + P * g, W_COLS["v"] + P * g, 2 * P * g, 2 * P * g + P)):
                s = At(S_B + 4 * g + j)
                load(s, raw_at(s, KD, P), w_in3[:, :, c:c + P])
        for n in range(8):
            s = At(S_D1 + n)
            c = (n * 256 + 1024) % D
            load(s, raw_at(s, 8, 256), wo3[:, 8:16, c:c + 256])
        with sp.Fori(0, 4, 1) as n2:
            for i in range(2):
                s = At(S_D2 + i, 2, n2)
                load(s, raw_at(s, 8, 256), wo3[:, 0:8, bass.ds(n2 * 512 + 256 * i, 256)])
        wg3, wu3 = (w[0].rearrange("(k p) n -> p k n", p=P) for w in (w_gate, w_up))
        with sp.Fori(0, NC, 1) as c:
            for n in range(2 * FC):
                s = At(S_E + n, 12, c)
                w = (wg3, wu3)[n % 2]
                load(s, raw_at(s, KD, P), w[:, :, bass.ds(c * (FC * P) + (n // 2) * P, P)])
            wd3 = w_down[0, bass.ds(c * (FC * P), FC * P), :].rearrange("(k p) n -> p k n", p=P)
            for n in range(4):
                s = At(S_E + 2 * FC + n, 12, c)
                load(s, raw_at(s, FC, 512), wd3[:, :, n * 512:n * 512 + 512])
        for q in range(4):
            sp.wait_ge(sem("y_act"), Y_ACT[q])
            sp.wait_ge(sem("y_dve"), Y_DVE[q])
            sp.dma_start(y_prompt[0, :, 512 * q:512 * q + 512].rearrange("(c p) d -> p c d", p=P),
                         ytok[:, 0:NB, 512 * q:512 * q + 512]).then_inc(sem("y_out"), 16)
            sp.dma_start(y_sample[:, 0, 512 * q:512 * q + 512], ytok[0:NS, NB, 512 * q:512 * q + 512])\
                .then_inc(sem("y_out"), 16)
        sp.wait_ge(sem("y_out"), 128)

    @block.gpsimd
    def _(pool):
        ch = Chain(pool, sem("pool_step"))

        def mask(ap, value, **kw):
            ch(pool.affine_select(out=ap, in_=ap, fill=value, **kw))

        for name in ("ho_done", "mixed", "state_left"):
            pool.sem_inc(sem(name), 1)
        for r, src in ((0, ln_in_g), (16, ln_in_b), (32, ln1_g[0]), (48, ln1_b[0])):
            pool.dma_start(vrows[r:r + 16, :], src.rearrange("(k p) -> k p", p=P)).then_inc(sem("vec_in"), 16)
        pool.dma_start(vrows[64:80, :], hg_lb_logits.rearrange("l (h p) -> (l h) p", p=P)).then_inc(sem("vec_in"), 16)
        pool.dma_start(vrows[80:81, :], hg_norm_g).then_inc(sem("vec_in"), 16)
        for r, src in ((81, ln2_g[0]), (97, ln2_b[0])):
            pool.dma_start(vrows[r:r + 16, :], src.rearrange("(k p) -> k p", p=P)).then_inc(sem("vec_in"), 16)
        pool.dma_start(pt_i[:, 0, :], page_table.rearrange("b p -> p b"), allow_slow_non_contiguous=True).then_inc(sem("pt_in"), 16)
        pool.dma_start(pt_i[:, 1, :], page_table).then_inc(sem("pt_in"), 16)
        ch(pool.memset(ones[:], 1.0))
        ch(pool.memset(ident[:], 0.0))
        mask(ident[:], 1.0, compare_op=ALU.not_equal, base=0, pattern=[[-1, P]], channel_multiplier=1)
        ch(pool.memset(tri[:], 1.0))
        mask(tri[:], 0.0, compare_op=ALU.is_ge, base=0, pattern=[[1, P]], channel_multiplier=-1)
        ch(pool.memset(causal[:], 0.0))
        mask(causal[:], INADMISSIBLE, compare_op=ALU.is_ge, base=0, pattern=[[-1, P]], channel_multiplier=1)
        ch(pool.iota(dist[:], pattern=[[-1, 528]], base=400, channel_multiplier=1,
                     allow_small_or_imprecise_dtypes=True))
        ch(pool.memset(halfsel[:], 1.0))
        mask(halfsel[:, 0:1], 0.0, compare_op=ALU.is_ge, base=63, pattern=[[0, 1]], channel_multiplier=-1)
        mask(halfsel[:, 1:2], 0.0, compare_op=ALU.is_ge, base=-64, pattern=[[0, 1]], channel_multiplier=1)
        ch(pool.memset(pageof[:], 16.0))
        mask(pageof[:], 0.0, compare_op=ALU.is_ge, base=0, pattern=[[1, P]], channel_multiplier=-16)
        mask(pageof[:], 0.0, compare_op=ALU.is_ge, base=15, pattern=[[-1, P]], channel_multiplier=16)
        ch(pool.iota(pmod[:].bitcast(I32), pattern=[[0, 8]], base=0, channel_multiplier=1))
        for h in range(NH):
            ch(pool.memset(slope8[:, h:h + 1], -(2.0 ** -(h + 1))))
        ch(pool.memset(zt[:], 0.0))
        ch(pool.memset(zt[:, NS - 1:NS], 1.0))
        pool.sem_inc(sem("consts"), 1)

        kidx_rows = cache_kidx[0].rearrange("n (j r) d -> (n j) (r d)", r=8)
        pool.wait_ge(sem("krow_ready"), 1)
        for b in range(NS):
            if b >= 2:
                pool.wait_ge(sem("kx_turned"), b - 1)
            pool.indirect_dma_start(kx[:, b % 2, :], None, kidx_rows,
                                    bass.IndirectOffsetOnAxis(ap=krow[:, b:b + 1], axis=0)).then_inc(sem(f"kx_in{b % 2}"), 16)
        pool.wait_ge(sem("wk_ready"), 1)
        ki_rows = kidx_prompt[0, 0]
        pool.dma_start(ki_rows[NM:NM + NR, :].rearrange("(c p) d -> p c d", p=P), wk[:, 0:4, 8:72]).then_inc(sem("out_ki"), 16)
        pool.dma_start(ki_rows[0:NM, :], wk[0:NM, 4, 8:72]).then_inc(sem("out_ki"), 16)
        pool.dma_start(kidx_sample[0, :, 0, :], wk[0:NS, 5, 8:72]).then_inc(sem("out_ki"), 16)

        state_in = state_hgrn[0].rearrange("b h d v -> h d b v")
        state_out = hgrn_sample[0].rearrange("b h d v -> h d b v")

        def load_state(h):
            pool.dma_start(ss[:], state_in[h] if isinstance(h, int) else state_in[bass.ds(h, 1)].rearrange("o d b v -> (o d) b v")
                           ).then_inc(sem("state_in"), 16)

        def store_states(h, n):
            wait_apart(pool, sem("sstate_ready"), n + 1, sem("pool_seen"))
            dst = state_out[h] if isinstance(h, int) else state_out[bass.ds(h, 1)].rearrange("o d b v -> (o d) b v")
            pool.dma_start(dst, ss[:]).then_inc(sem("sstate_out"), 16)
            wait_apart(pool, sem("st_ready"), n + 1, sem("pool_seen"))
            dst = hgrn_prompt[0, 0, h] if isinstance(h, int) else hgrn_prompt[0, 0, bass.ds(h, 1)].rearrange("o d v -> (o d) v")
            pool.dma_start(dst, st[:, NB, :]).then_inc(sem("state_out"), 16)

        load_state(0)
        with pool.Fori(1, NH, 1) as h:
            store_states(h - 1, h - 1)
            pool.wait_ge(sem("ho_done"), h + 1)
            pool.wait_ge(sem("state_out"), h * 16)
            pool.sem_inc(sem("state_left"), 1)
            wait_apart(pool, sem("sstate_out"), h * 16, sem("pool_seen"))
            load_state(h)
        store_states(NH - 1, NH - 1)

        def store_rows(g, src, to_prompt, to_sample, name):
            rows = to_prompt[0, 0, :, g, :]
            pool.dma_start(rows[NM:NM + NR, :].rearrange("(c p) d -> p c d", p=P), src[:, 0:4, :]).then_inc(sem(name), 16)
            pool.dma_start(rows[0:NM, :], src[0:NM, 4, :]).then_inc(sem(name), 16)
            pool.dma_start(to_sample[0, :, 0, g, :], src[0:NS, 5, :]).then_inc(sem(name), 16)

        for g in range(NG):
            pool.wait_ge(sem("kv_tok"), 4 * g + 2)
            store_rows(g, ktok, k_prompt, k_sample, "k_out")
            pool.wait_ge(sem("kv_tok"), 4 * g + 4)
            store_rows(g, vtok[g % 2], v_prompt, v_sample, "v_out")
        pool.wait_ge(sem("resid_lo"), 8)
        pool.wait_ge(sem("grow_ready"), 1)
        for b in range(NS):
            for name, dst, src, used in (("gk", kgs, cache_k, "sg_turned"), ("gv", vgs, cache_v, "so_done")):
                if b >= 2:
                    pool.wait_ge(sem(used), b - 1)
                for blk in range(NBLK):
                    pool.indirect_dma_start(dst[:, b % 2, blk, :], None, src[0].rearrange("n s k d -> (n s) (k d)"),
                                            bass.IndirectOffsetOnAxis(ap=grow[:, blk, b:b + 1], axis=0))\
                        .then_inc(sem(f"{name}{b % 2}"), 16)
        pool.wait_ge(sem("k_out"), 48 * NG)
        pool.wait_ge(sem("v_out"), 48 * NG)
        pool.wait_ge(sem("sstate_out"), 16 * NH)
        pool.wait_ge(sem("state_out"), 16 * NH)
        pool.wait_ge(sem("out_ki"), 48)

    @block.scalar
    def _(act):
        nc.scalar.preload_act_table_set("natural_log_exp_and_others")
        ch = Chain(act, sem("act_step"))

        def split(s, used=None):
            act.wait_ge(sem(f"w_in{s.odd}"), (s.half() + 1).times(16).v)
            if used is None and (s.reg is not None or s.const >= 2):
                used = mts(s - 2)
            if used is not None:
                act.wait_ge(sem("mm"), used.v)
            act.activation(wh[:, s.odd, :], raw[:, s.odd, :], ACT.Copy).then_inc(sem("h_split"), 1)

        def split_wk(s):
            act.wait_ge(sem(f"w_in{s.odd}"), (s.half() + 1).times(16).v)
            act.wait_ge(sem("mm"), mts(s - 2).v)
            act.activation(wh[:, s.odd, 0:KD * 72], raw[:, s.odd, 0:KD * 72], ACT.Copy).then_inc(sem("h_split"), 1)

        def sigmoid_tail(u):
            act.wait_ge(sem("sig_capped"), u + 1)
            act.activation(t1[:, :], t1[:, :], ACT.Ln, bias=1.0).then_inc(sem("sig_ln"), 1)
            act.wait_ge(sem("sig_ln"), u + 1)
            act.activation(t1[:, :], t1[:, :], ACT.Exp, scale=-1.0).then_inc(sem("sigmoid"), 1)

        split(At(0))
        split(At(1))
        act.wait_ge(sem("vec_turned"), 1)
        ch(act.activation(vec[:], b4[:, 0:113], ACT.Copy))
        act.wait_ge(sem("lb_shifted"), 1)
        act.activation(lb[:, 0:16], lb[:, 0:16], ACT.Exp).then_inc(sem("lb_exp"), 1)
        for c in range(5):
            n = R0 if c == NB else P
            act.wait_ge(sem("var"), c + 1)
            ch(act.activation(mv[0:n, c, 1:2], mv[0:n, c, 1:2], ACT.Ln, bias=LN_EPS))
            act.activation(mv[0:n, c, 1:2], mv[0:n, c, 1:2], ACT.Exp, scale=-0.5).then_inc(sem("rstd"), 1)
        for k in range(KD):
            act.wait_ge(sem("x_lin"), k + 1)
            act.activation(xh[:, k, :], lnt[:, k % 2, :], ACT.Copy).then_inc(sem("xh_ready"), 1)

        for i in range(4):
            if i == 3:
                split_wk(At(i + 1))
            elif i >= 1:
                split(At(i + 1))
            act.wait_ge(sem("mm"), i + 1)
            if i == 0:
                act.wait_ge(sem("x_turned"), KD)
            act.activation(cut(qiT[:, i, :]), whole(At(i)), ACT.Copy).then_inc(sem(f"acc_read{i % 2}"), 1)
        split(At(S_C))
        act.wait_ge(sem("mm"), 5)
        ch(act.activation(cut(wikiT[:, :]), acc[0:72, 0, :, 0:HALF], ACT.Copy))
        act.sem_inc(sem("acc_read0"), 1)
        act.sem_inc(sem("wiki_ready"), 1)

        def idx_setup():
            act.wait_ge(sem("wk_turned"), 1)
            for lo in (0, 72):
                n = 72 if lo == 0 else 64
                f = 0 if lo == 0 else 8
                src = b4[:, 0:288].rearrange("p (c f) -> p c f", c=4)
                act.activation(wk[:, 0:4, lo:lo + n], src[:, :, f:72], ACT.Copy).then_inc(sem("act_step"), 1)
                act.activation(wk[0:NM, 4, lo:lo + n], b5[0:NM, f:72], ACT.Copy).then_inc(sem("act_step"), 1)
                act.activation(wk[0:NS, 5, lo:lo + n], b5[0:NS, 72 + f:144], ACT.Copy).then_inc(sem("act_step"), 1)
            ch.n += 6
            act.wait_ge(sem("act_step"), ch.n)
            act.sem_inc(sem("wk_ready"), 1)
            act.wait_ge(sem("ki_back"), 1)
            act.activation(kiT[:, R0:NT], b6[:, :], ACT.Copy).then_inc(sem("act_step"), 1)
            act.activation(kiT[:, 0:R0], b7[:, 0:R0], ACT.Copy).then_inc(sem("act_step"), 1)
            q4 = qiT[:, :, 0:NS].rearrange("p m b -> p b m")
            for dst in (0, 64):
                for src in (0, 64):
                    out = qS[dst:dst + 64, :, :].rearrange("p b (m e) -> p b m e", e=2)[:, :, :, src // 64]
                    act.activation(out, q4[src:src + 64], ACT.Copy).then_inc(sem("act_step"), 1)
            ch.n += 6
            act.wait_ge(sem("act_step"), ch.n)
            act.sem_inc(sem("ki_ready"), 1)

        def idx_relu(i, m):
            n = 4 * i + m
            act.wait_ge(sem("idx_scores"), n + 1)
            if n >= 1:
                act.wait_ge(sem("idx_summed"), n)
            w = P * (i + 1)
            for e, (real, meta) in enumerate(((b4, b6), (b5, b7))):
                act.activation(rel[:, e, NM:NM + w], real[:, 0:w], ACT.Relu, scale=IDX_SCALE)
                act.activation(rel[:, e, 0:NM], meta[:, 0:NM], ACT.Relu, scale=IDX_SCALE)\
                   .then_inc(sem("idx_relu"), 1)

        def idx_sample(b):
            act.wait_ge(sem("kx_turned"), b + 1)
            if b >= 2:
                act.wait_ge(sem("sidx_scores"), b - 1)
            act.activation(kxT[:, b % 2, :], (b4, b5)[b % 2][:, :], ACT.Copy).then_inc(sem("kxT_ready"), 1)

        def idx_sample_relu():
            act.wait_ge(sem("sidx_scores"), NS)
            act.activation(rsc[:, 0, :], b6[:, 0:256], ACT.Relu, scale=IDX_SCALE)
            act.activation(rsc[:, 1, :], b7[:, 0:256], ACT.Relu, scale=IDX_SCALE).then_inc(sem("sidx_relu"), 1)
            act.wait_ge(sem("nsc_scores"), 1)
            act.activation(nsc[:], b5[0:NS, 0:NH], ACT.Relu, scale=IDX_SCALE).then_inc(sem("nsc_relu"), 1)

        def t_of(h4, j):
            return h4 + (S_C + j)

        def forget(h4, n):
            t = t_of(h4, 0)
            act.wait_ge(sem("mm"), (t + 1).v)
            act.wait_ge(sem("gate_ready"), n)
            act.activation(cut(t1[:, :]), whole(t), ACT.Exp, scale=-1.0).then_inc(sem("sig_exp"), 1)
            sigmoid_tail(3 * n)
            act.wait_ge(sem("sigmoid"), 3 * n + 1)
            if not isinstance(n, int):
                act.wait_ge(sem("mixed"), n)
            act.activation(t2[:, :], t1[:, :], ACT.Ln, scale=lbcol(h4, n, 1), bias=lbcol(h4, n, 0))\
               .then_inc(sem("logf"), 1)

        def lbcol(h4, n, which):
            return lb[:, 8 * which + n:8 * which + n + 1] if isinstance(n, int) else lb[:, bass.ds(n + 8 * which, 1)]

        def query(h4, n):
            t = t_of(h4, 1)
            act.wait_ge(sem("mm"), (t + 1).v)
            act.wait_ge(sem("kf_ready"), n + 1)
            act.activation(cut(t1[:, :]), whole(t), ACT.Exp, scale=-1.0).then_inc(sem("sig_exp"), 1)
            sigmoid_tail(3 * n + 1)

        def decays(h4, n):
            act.wait_ge(sem("b_ready"), n + 1)
            act.wait_ge(sem("intra_done"), n)
            off = 0
            for i in range(4):
                w = SUB * (i + 1)
                for c in range(NB):
                    lo = R0 + P * c
                    mid_ = lo + SUB * i + SUB // 2 - 1
                    act.activation(et[:, off + c * w:off + c * w + w], bcum[:, lo:lo + w], ACT.Exp, scale=-1.0,
                                   bias=bcum[:, mid_:mid_ + 1])
                off += NB * w
            act.activation(et[:, off:off + NM], bcum[:, M0:R0], ACT.Exp, scale=-1.0,
                           bias=bcum[:, M0 + 7:M0 + 8]).then_inc(sem("et_exp"), 1)
            for c in range(NB):
                lo = R0 + P * c
                act.activation(ke[:, lo:lo + P], bcum[:, lo:lo + P], ACT.Exp, scale=-1.0, bias=bcum[:, lo + P - 1:lo + P])
            act.activation(ke[:, M0:R0], bcum[:, M0:R0], ACT.Exp, scale=-1.0, bias=bcum[:, R0 - 1:R0])\
               .then_inc(sem("ke_exp"), 1)
            act.wait_ge(sem("ho_done"), n + 1)
            act.activation(qe[:, :], bcum[:, :], ACT.Exp).then_inc(sem("qe_exp"), 1)
            act.wait_ge(sem("st_ready"), n)
            act.activation(eb[:, :], bcum[:, R0 + P - 1:NT:P], ACT.Exp)
            act.wait_ge(sem("sstate_ready"), n)
            act.activation(fs[:, :], bcum[:, 0:NS], ACT.Exp).then_inc(sem("ends_exp"), 1)
            act.wait_ge(sem("qd_arg"), n + 1)
            act.activation(qd[:, M0:NT], qd[:, M0:NT], ACT.Exp).then_inc(sem("qd_exp"), 1)

        def inputs(h4, n):
            t = t_of(h4, 2)
            act.wait_ge(sem("mm"), (t + 1).v)
            act.wait_ge(sem("head_turned"), n)
            act.activation(cut(hiT[:, :]), whole(t), ACT.Copy).then_inc(sem(f"acc_read{t.odd}"), 1)

        def turned(h4, n):
            act.wait_ge(sem("head_turned"), n + 1)
            act.wait_ge(sem("ho_done"), n + 1)
            act.activation(itok[:, 0:4, :], b4[:, :].rearrange("p (c v) -> p c v", c=4), ACT.Copy)
            act.activation(ketok[:, 0:4, :], b6[:, :].rearrange("p (c v) -> p c v", c=4), ACT.Copy)
            act.activation(itok[0:NM, 4, :], b5[0:NM, 0:P], ACT.Copy)
            act.activation(itok[0:NS, 5, :], b5[0:NS, P:2 * P], ACT.Copy)
            act.activation(ketok[0:NM, 4, :], b5[0:NM, 2 * P:3 * P], ACT.Copy).then_inc(sem("tok_ready"), 1)

        def gating(h4, n):
            t = t_of(h4, 3)
            act.wait_ge(sem("mm"), (t + 1).v)
            act.wait_ge(sem("q_ready"), n + 1)
            act.activation(cut(t1[:, :]), whole(t), ACT.Exp, scale=-1.0).then_inc(sem("sig_exp"), 1)
            sigmoid_tail(3 * n + 2)

        def squares(n):
            act.wait_ge(sem("ho_done"), n + 2)
            act.wait_ge(sem("b_ready"), n + 1) if isinstance(n, int) and n == NH - 1 else act.wait_ge(sem("b_ready"), n + 2)
            act.activation(t2[:, R0:NT], b4[:, :], ACT.Square)
            act.activation(t2[:, 0:R0], b5[:, 0:R0], ACT.Square).then_inc(sem("squared"), 1)

        def norm_scale(n):
            act.wait_ge(sem("norm_sum"), n + 1)
            act.activation(t2[:, R0:NT], b6[:, :], ACT.Ln, scale=1.0 / P, bias=NORM_EPS)
            act.activation(t2[:, 0:R0], b7[:, 0:R0], ACT.Ln, scale=1.0 / P, bias=NORM_EPS).then_inc(sem("norm_ln"), 1)
            act.wait_ge(sem("norm_ln"), n + 1)
            act.activation(t2[:, :], t2[:, :], ACT.Exp, scale=-0.5).then_inc(sem("norm_scale"), 1)

        def early(h4, n, j):
            if j == 1:
                forget(h4, n)
            if j == 2:
                query(h4, n)
                decays(h4, n)
            if j == 3:
                inputs(h4, n)

        def late(h4, n, j):
            if j == 0:
                turned(h4, n)
                gating(h4, n)
            if j == 2:
                squares(n)
            if j == 3:
                norm_scale(n)

        idx_setup()
        for j in range(4):
            split(At(S_C + j + 1))
            early(At(0), 0, j)
            if j == 0:
                for b in range(NS):
                    idx_sample(b)
                idx_sample_relu()
            for m in range(4):
                idx_relu(j, m)
        with act.Fori(1, NH, 1) as h:
            for j in range(4):
                split(At(S_C + j + 1, 4, h))
                late(At(-4, 4, h), h - 1, j)
                early(At(0, 4, h), h, j)
        def take(g, j):
            t = At(S_B + 4 * g + j)
            act.wait_ge(sem("mm"), (t + 1).v)
            src = whole(t)
            dst = (kT[g % 2][:, :], vT[:, :], qT[g % 2][:, 0, :], qT[g % 2][:, 1, :])[j]
            if j == 0:
                ch(act.activation(knew[:, g, :], src[:, 0, 0:NS], ACT.Copy))
            if j >= 2:
                if j == 2 and g == 0:
                    act.wait_ge(sem("qpad_clear"), 1)
                ch(act.activation(qpad[:, g, :, 2 * g + j - 2], src[:, 0, 0:NS], ACT.Copy, scale=ATTN_SCALE))
            ch(act.activation(cut(dst), src, ACT.Copy))
            act.sem_inc(sem(f"acc_read{t.odd}"), 1)
            act.sem_inc(sem("qkv_in"), 1)

        def kv_rows(g, j):
            dst = ktok if j == 0 else vtok[g % 2]
            act.wait_ge(sem("kv_turned"), 4 * g + 2 * j + 1)
            if j == 0 and g >= 1:
                act.wait_ge(sem("k_out"), 48 * g)
            if j == 1 and g >= 2:
                act.wait_ge(sem("v_out"), 48 * (g - 1))
            act.activation(dst[:, 0:4, :], b7[:, :].rearrange("p (c d) -> p c d", c=4), ACT.Copy).then_inc(sem("kv_tok"), 1)
            act.wait_ge(sem("kv_turned"), 4 * g + 2 * j + 2)
            act.activation(dst[0:NM, 4, :], b7[0:NM, 0:P], ACT.Copy)
            act.activation(dst[0:NS, 5, :], b7[0:NS, P:2 * P], ACT.Copy).then_inc(sem("kv_tok"), 1)

        def att_exp(n):
            i = n % NB
            act.wait_ge(sem("att_max"), n + 1)
            for hd in range(2):
                last = act.activation(lg[:, hd, 0:WIDE[i]], lg[:, hd, 0:WIDE[i]], ACT.Exp, bias=nmx[:, 0, hd:hd + 1],
                                      accum_out=nmx[:, 1, hd:hd + 1])
                if i == 0:
                    last = act.activation(lgm[:, hd, :], lgm[:, hd, :], ACT.Exp, bias=nmxm[:, 0, hd:hd + 1],
                                   accum_out=nmxm[:, 1, hd:hd + 1])
            last.then_inc(sem("att_exp"), 1)

        def att_probs(n):
            i = n % NB
            act.wait_ge(sem("p_turned"), n + 1)
            w = P * (i + 1)
            act.activation(pT[:, 0, 0:w], b4[:, 0:w], ACT.Copy)
            act.activation(pT[:, 1, 0:w], b5[:, 0:w], ACT.Copy)
            m = 2 * P + (2 * NM if i == 0 else 0)
            act.activation(pTm[:, 0:m], b6[0:NM, 0:m], ACT.Copy).then_inc(sem("pT_out"), 1)

        def att_take(n):
            g, i = n // NB, n % NB
            act.wait_ge(sem("pv_done"), n + 1)
            if i == 0:
                ch(act.activation(attn_o[:, 2 * g:2 * g + 2, M0:R0],
                                  b7[:, 2 * P:2 * P + 2 * NM].rearrange("p (h q) -> p h q", h=2), ACT.Copy))
            act.activation(attn_o[:, 2 * g:2 * g + 2, R0 + P * i:R0 + P * i + P],
                           b7[:, 0:2 * P].rearrange("p (h q) -> p h q", h=2), ACT.Copy).then_inc(sem("pv_out"), 1)

        def keep_new(g):
            act.activation(vnew[:, g, :], vtok[g % 2][0:NS, 5, :], ACT.Copy).then_inc(sem("vnew_in"), 1)

        for g in range(NG):
            for j in range(4):
                split(At(S_B + 4 * g + j + 1))
                if j >= 1:
                    take(g, j - 1)
                elif g >= 1:
                    take(g - 1, 3)
                if g == 0:
                    late(At(28), 7, j) if j != 2 else None
                    if j == 2:
                        kv_rows(0, 0)
                        squares(7)
                    if j == 3:
                        kv_rows(0, 1)
                else:
                    n = 4 * (g - 1) + j
                    if n >= 1:
                        att_take(n - 1)
                    att_exp(n)
                    if j == 0:
                        keep_new(g - 1)
                    if j in (1, 2):
                        kv_rows(g, j - 1)
                    att_probs(n)

        def mix_round(k):
            act.wait_ge(sem("x_sum"), k + 1)
            act.activation(xh[:, 8 + k, :], sacc[:, 8 + k, :], ACT.Copy).then_inc(sem("mix_h"), 1)

        def mix_resid(k):
            act.wait_ge(sem("mix_in"), k + 1)
            act.activation(sacc[:, 8 + k, :], tmp[:, k % 2, :], ACT.Copy, scale=ALPHA).then_inc(sem("resid"), 1)

        def sample_att(b):
            act.wait_ge(sem("sg_turned"), b + 1)
            act.wait_ge(sem("slog"), b)
            act.activation(kgT[:, 0], b4[:, :].rearrange("p (g k) -> p g k", g=NG), ACT.Copy)
            act.activation(kgT[:, 1], b5[:, :].rearrange("p (g k) -> p g k", g=NG), ACT.Copy).then_inc(sem("sgT"), 1)
            act.wait_ge(sem("smax"), b + 1)
            act.activation(ps[:, :], b6[0:NH, 0:KEEP_S + 1], ACT.Exp, bias=snm[:, 0:1], accum_out=snm[:, 1:2])\
               .then_inc(sem("sexp"), 1)
            act.wait_ge(sem("sp_turned"), b + 1)
            act.activation(pTs[:, 0:16], b7[:, 0:16], ACT.Copy)
            act.activation(pTs[0:NS, 16:24], b7[0:NS, 16:24], ACT.Copy).then_inc(sem("spT"), 1)
            act.wait_ge(sem("so_done"), b + 1)
            act.activation(attn_o[:, :, b], b7[:, 32:32 + NH], ACT.Copy).then_inc(sem("so_out"), 1)

        for n in range(8):
            split(At(S_D1 + n + 1))
            if n == 0:
                take(3, 3)
                mix_round(0)
                for k in range(1, 9):
                    if k < 8:
                        mix_round(k)
                    mix_resid(k - 1)
            if n <= 4:
                att_take(11 + n)
            if n == 1:
                act.wait_ge(sem("k_out"), 48 * NG)
                act.wait_ge(sem("v_out"), 48 * NG)
                for k in range(8):
                    act.activation(sacc[:, k, :], fr(xh[:, k, :]), ACT.Copy, scale=ALPHA).then_inc(sem("resid_h"), 1)
            if n < 4:
                att_exp(12 + n)
                if n == 0:
                    keep_new(3)
                att_probs(12 + n)
            else:
                sample_att(2 * (n - 4))
                sample_att(2 * (n - 4) + 1)

        def stat_square(m):
            k = m.const % KD
            act.wait_ge(sem("s_done"), (m + 1).v)
            if m.reg is not None or m.const >= 2:
                act.wait_ge(sem("q_sum"), (m - 1).v)
            src = sacc[:, k, :] if m.reg is None else sacc[:, bass.ds(m.v, 1), :].rearrange("p o n -> p (o n)")
            act.activation(sq[:, k % 2, :], src, ACT.Square).then_inc(sem("sq_done"), 1)

        act.wait_ge(sem("so_out"), NS)
        for k in range(NH):
            act.activation(xh[:, k, :], attn_o[:, k, :], ACT.Copy).then_inc(sem("att_h"), 1)

        def d2(n2):
            for i in range(2):
                last = isinstance(n2, int) and False
                s = At(S_D2 + i + 1, 2, n2) if not isinstance(n2, int) else At(S_D2 + i + 1 + 2 * n2)
                split(s, d2_before(i + 1, n2))
                for e in range(2):
                    stat_square(At(2 * i + e, 4, n2) if not isinstance(n2, int) else At(2 * i + e + 4 * n2))

        d2(0)
        with act.Fori(1, 4, 1) as n2:
            d2(n2)

        def scale_of(n):
            act.wait_ge(sem("ln_var"), n)
            ch(act.activation(rstd[:, :], rstd[:, :], ACT.Ln, bias=LN_EPS))
            act.activation(rstd[:, :], rstd[:, :], ACT.Exp, scale=-0.5).then_inc(sem("ln_rstd"), 1)

        scale_of(1)
        for k in range(KD):
            act.wait_ge(sem("ln_norm"), k + 1)
            ch(act.activation(sacc[:, k, :], lnd[:, k % 2, :], ACT.Identity, scale=vec[:, 32 + k:33 + k],
                              bias=vec[:, 48 + k:49 + k]))
            act.activation(xh[:, k, :], sacc[:, k, :], ACT.Copy).then_inc(sem("x1_h"), 1)
        nc.scalar.preload_act_table_set("silu_and_others")
        split(At(S_E + 1), e_before(1, 0))
        act.wait_ge(sem("x1_in"), KD)
        for k in range(KD):
            act.activation(sacc[:, k, :], sacc[:, k, :], ACT.Copy, scale=ALPHA).then_inc(sem("x1_resid"), 1)

        def mlp(c, last=False):
            for n in range(12):
                if not (isinstance(c, int) and c == 0 and n == 0) and not (last and n == 11):
                    nn, cc = (n + 1, c) if n < 11 else (0, c + 1)
                    split(e_tile(nn, cc), e_before(nn, cc))
                if n in (1, 3, 5, 7):
                    t = e_result(n - 1, 0, c)
                    f = (n - 1) // 2
                    act.wait_ge(sem("mm"), (t + 1).v)
                    if f >= 2 or not isinstance(c, int) or c >= 1:
                        act.wait_ge(sem("gated"), 4 * c + f - 1)
                    act.activation(cut(gbuf[:, f % 2, :]), whole(t), ACT.Silu).then_inc(sem("gate_done"), 1)
                    act.wait_ge(sem("gate_done"), 4 * c + f + 1)
                    act.sem_inc(sem(f"acc_read{t.odd}"), 1)
                if n in (2, 4, 6, 8):
                    f = n // 2 - 1
                    act.wait_ge(sem("gated"), 4 * c + f + 1)
                    act.activation(hh[:, f, :], hbuf[:, f % 2, :], ACT.Copy).then_inc(sem("hh_done"), 1)
                if last and n >= 8:
                    for i in range(4):
                        stat_square(At(16 + 4 * (n - 8) + i))

        mlp(0)
        with act.Fori(1, NC - 1, 1) as c:
            mlp(c)
        mlp(NC - 1, last=True)
        nc.scalar.preload_act_table_set("natural_log_exp_and_others")
        scale_of(2)
        for k in range(KD + 1):
            if k < KD:
                act.wait_ge(sem("ln_norm"), KD + k + 1)
                act.activation(sacc[:, k, :], lnd[:, k % 2, :], ACT.Identity, scale=vec[:, 81 + k:82 + k],
                               bias=vec[:, 97 + k:98 + k]).then_inc(sem("y_ready"), 1)
            if k >= 4 and k % 4 == 0:
                q = k // 4 - 1
                for u in range(5 * q, 5 * q + 5):
                    if u % 2 == 0:
                        act.wait_ge(sem("y_turned"), u + 1)
                        r = P if u % 5 < 4 else NS
                        act.activation(ytok[0:r, u % 5, 512 * q:512 * q + 512], y_bank(u)[0:r], ACT.Copy)\
                           .then_inc(sem("y_act"), 1)

    @block.tensor
    def _(pe):
        mm = nc.tensor.matmul

        def turn(out, in_):
            k = in_.shape[0]
            b = in_.start_partition()
            return nc.tensor.transpose(out, in_, ident[b:b + k, b:b + k])

        def product(s, t, kt, width, sub, x, between, rows=P, kx0=0, last=None):
            if sub == 0:
                pe.wait_ge(sem("l_split"), (s + 1).v)
            if t.reg is not None or t.const >= 2:
                pe.wait_ge(sem(f"acc_read{t.odd}"), t.half().v)
            for k in range(kt):
                at_ = k * width + sub * P
                a_h, a_l = (w[:, s.odd, at_:at_ + rows] for w in (wh, wl))
                for n, (a, b) in enumerate(((a_h, x[0]), (a_h, x[1]), (a_l, x[0]))):
                    for half in range(2):
                        ins = mm(acc[0:rows, t.odd, half, 0:HALF], a, b[:, kx0 + k, half * HALF:half * HALF + HALF],
                                 start=(k == 0 and n == 0), stop=(k == kt - 1 and n == 2))
                if k == kt - 1:
                    ins.then_inc(sem("mm"), 1)
                for f in between.get(k, ()):
                    f()

        X = (xh, xl)

        pe.wait_ge(sem("consts"), 1)
        pe.wait_ge(sem("vec_in"), 128)
        turn(b4[:, 0:113], vrows[0:113, :]).then_inc(sem("vec_turned"), 1)
        pe.wait_ge(sem("act_step"), 1)
        real, small = (b4, b6), (b5, b7)
        for k in range(KD):
            if k == 0:
                pe.wait_ge(sem("x_norm"), NB + 1)
            if k >= 2:
                pe.wait_ge(sem("x_lin"), k - 1)
            for c in range(NB):
                turn(real[k % 2][:, c * P:c * P + P], xtok[:, c, k * P:k * P + P])
            turn(small[k % 2][:, 0:R0], xtok_s[:, k * P:k * P + P]).then_inc(sem("x_turned"), 1)

        def x_ready(k):
            return lambda: pe.wait_ge(sem("xl_ready"), k + 1)

        x_ready(0)()
        product(At(0), At(0), KD, P, 0, X, {k: (x_ready(k + 1),) for k in range(KD - 1)})
        for i in range(1, 4):
            product(At(i), At(i), KD, P, 0, X, {})
        product(At(4), At(4), KD, 72, 0, X, {}, rows=72)

        def wk_turn():
            pe.wait_ge(sem("wiki_ready"), 1)
            for c in range(NB):
                turn(b4[:, 72 * c:72 * c + 72], wikiT[:, R0 + P * c:R0 + P * c + P])
            turn(b5[0:NM, 0:72], wikiT[:, M0:R0])
            turn(b5[0:NS, 72:144], wikiT[:, 0:NS]).then_inc(sem("wk_turned"), 1)
            pe.wait_ge(sem("pt_ready"), 1)
            mm(b7[:, 64:72], pageof[:], ptT[:], start=True, stop=True).then_inc(sem("krow_sum"), 1)

        def ki_back():
            pe.wait_ge(sem("wk_ready"), 1)
            pe.wait_ge(sem("krow_ready"), 1)
            for c in range(NB):
                turn(b6[:, P * c:P * c + P], wk[:, c, 8:136])
            turn(b7[:, M0:R0], wk[0:NM, 4, 8:136])
            turn(b7[:, 0:NS], wk[0:NS, 5, 8:136]).then_inc(sem("ki_back"), 1)

        def kx_turn(b):
            pe.wait_ge(sem(f"kx_in{b % 2}"), 16 * (b // 2 + 1))
            if b >= 2:
                pe.wait_ge(sem("kxT_ready"), b - 1)
            else:
                pe.wait_ge(sem("wk_ready"), 1)
            for r in range(4):
                last = turn((b4, b5)[b % 2][:, P * r:P * r + P], kx[:, b % 2, P * r:P * r + P])
            last.then_inc(sem("kx_turned"), 1)

        def kx_scores(b):
            pe.wait_ge(sem("kxT_ready"), b + 1)
            pe.wait_ge(sem("ki_ready"), 1)
            for r in range(4):
                for e in range(2):
                    at_ = (b * 4 + r) * NH
                    last = mm((b6, b7)[e][:, at_:at_ + NH], kxT[64 * e:64 * e + 64, b % 2, P * r:P * r + P],
                              qS[64 * e:64 * e + 64, b, :], start=True, stop=True)
            last.then_inc(sem("sidx_scores"), 1)

        def kx_new():
            pe.wait_ge(sem("prod_ready"), 1)
            pe.wait_ge(sem("kxT_ready"), NS)
            for m in range(4):
                last = mm(b5[0:NS, 2 * m:2 * m + 2], prod[:, m, :], halfsel[:], start=True, stop=True)
            last.then_inc(sem("nsc_scores"), 1)
            mm(b4[:, 0:64], ones[0:NS, :], wsel[:].rearrange("k b h -> k (b h)"), start=True, stop=True)\
                .then_inc(sem("wbc_sum"), 1)

        def is_turn():
            pe.wait_ge(sem("isc_ready"), 1)
            pe.wait_ge(sem("nsc_relu"), 1)
            for e in range(2):
                for r in range(4):
                    last = turn((b4, b5)[e][0:NS, P * r:P * r + P], isc[:, e, :, r])
            last.then_inc(sem("isc_turned"), 1)

        def idx_scores(i, m):
            n = 4 * i + m
            if n == 0:
                pe.wait_ge(sem("isc_read"), 2)
            else:
                pe.wait_ge(sem("idx_relu"), 2 * n)
            w = P * (i + 1)
            lo = R0 + P * i
            for e, (real_, meta) in enumerate(((b4, b6), (b5, b7))):
                a = qiT[64 * e:64 * e + 64, m, lo:lo + P]
                mm(real_[:, 0:w], a, kiT[64 * e:64 * e + 64, R0:R0 + w], start=True, stop=True)
                last = mm(meta[:, 0:NM], a, kiT[64 * e:64 * e + 64, M0:R0], start=True, stop=True)
            last.then_inc(sem("idx_scores"), 1)

        def head_turn(h4, n):
            t = h4 + (S_C + 2)
            if h4.reg is None:
                pe.wait_ge(sem("idx_relu"), 32)
            pe.wait_ge(sem(f"acc_read{t.odd}"), (t.half() + 1).v)
            pe.wait_ge(sem("qd_ready"), n + 1)
            for c in range(NB):
                lo = R0 + P * c
                turn(b4[:, P * c:P * c + P], hiT[:, lo:lo + P])
                turn(b6[:, P * c:P * c + P], ke[:, lo:lo + P])
            turn(b5[0:NM, 0:P], hiT[:, M0:R0])
            turn(b5[0:NS, P:2 * P], hiT[:, 0:NS])
            turn(b5[0:NM, 2 * P:3 * P], ke[:, M0:R0])
            off = NB * (32 + 64 + 96 + 128)
            mm(b5[0:NM, 3 * P:3 * P + NM], et[:, off:off + NM], qd[:, M0:R0], start=True, stop=True)\
                .then_inc(sem("head_turned"), 1)
            off = 0
            for i in range(4):
                w = SUB * (i + 1)
                for c in range(NB):
                    last = mm(b7[0:w, P * c + SUB * i:P * c + SUB * i + SUB], et[:, off + c * w:off + c * w + w],
                              qd[:, R0 + P * c + SUB * i:R0 + P * c + SUB * i + SUB], start=True, stop=True)
                off += NB * w
            last.then_inc(sem("intra_done"), 1)

        def outer(n):
            pe.wait_ge(sem("tok_ready"), n + 1)
            pe.wait_ge(sem("aT_ready"), n + 1)
            for c in range(NB):
                mm(b4[:, P * c:P * c + P], ketok[:, c, :], itok[:, c, :], start=True, stop=True)
            mm(b5[:, 0:P], ketok[0:NM, 4, :], itok[0:NM, 4, :], start=True, stop=True).then_inc(sem("outer_done"), 1)

        def spread(n):
            for b in range(NS):
                last = mm((b6, b7)[b // 4][:, P * (b % 4):P * (b % 4) + P], ident[0:NS, b:b + 1].to_broadcast([NS, P]),
                          itok[0:NS, 5, :], start=True, stop=True)
            last.then_inc(sem("spread_done"), 1)

        def head_out(n):
            pe.wait_ge(sem("st_ready"), n + 1)
            for c in range(NB):
                lo = R0 + P * c
                mm(b4[:, P * c:P * c + P], itok[:, c, :], aT[:, c, :], start=True, stop=False)
                mm(b4[:, P * c:P * c + P], st[:, c, :], qe[:, lo:lo + P], start=False, stop=True)
            mm(b5[:, M0:R0], itok[0:NM, 4, :], aTm[:], start=True, stop=True)
            pe.wait_ge(sem("sstate_ready"), n + 1)
            for b in range(NS):
                last = mm(b5[:, b:b + 1], ss[:, b, :], hq[:, b:b + 1], start=True, stop=True)
            last.then_inc(sem("ho_done"), 1)

        def norm_sum(n):
            pe.wait_ge(sem("squared"), n + 1)
            mm(b6[:, :], ones[:], t2[:, R0:NT], start=True, stop=True)
            mm(b7[:, 0:R0], ones[:], t2[:, 0:R0], start=True, stop=True).then_inc(sem("norm_sum"), 1)

        def late(n, j):
            if j == 0:
                return {11: (lambda: outer(n),), 15: (lambda: spread(n),)}
            if j == 1:
                return {11: (lambda: head_out(n),)}
            if j == 2:
                return {11: (lambda: norm_sum(n),)}
            return {}

        def merged(*maps):
            out = {}
            for m_ in maps:
                for k, v in m_.items():
                    out[k] = out.get(k, ()) + tuple(v)
            return out

        def early(h4, n, j):
            return {15: (lambda: head_turn(h4, n),)} if j == 3 else {}

        for j in range(4):
            side = {}
            if j == 0:
                side = {1: (wk_turn,), 4: (ki_back,), 15: (lambda: [idx_scores(0, m) for m in range(4)],)}
                for b in range(NS):
                    side.setdefault(5 + b, ())
                    side[5 + b] += (lambda b=b: kx_turn(b),)
                    side.setdefault(6 + b, ())
                    side[6 + b] += (lambda b=b: kx_scores(b),)
                side[14] = (kx_new,) + side.get(14, ())
                side[15] = (is_turn,) + side[15]
            else:
                side = {3 + 3 * m: (lambda m=m: idx_scores(j, m),) for m in range(4)}
            product(At(S_C + j), At(S_C + j), KD, P, 0, X, merged(side, early(At(0), 0, j)))
        with pe.Fori(1, NH, 1) as h:
            for j in range(4):
                s = At(S_C + j, 4, h)
                product(s, s, KD, P, 0, X, merged(late(h - 1, j), early(At(0, 4, h), h, j)))

        def kv_turn(g, j, small):
            c = 4 * g + 2 * j + small
            src = (kT[g % 2], vT)[j]
            pe.wait_ge(sem("qkv_in"), 4 * g + j + 1)
            if g == 0:
                pe.wait_ge(sem("sstate_ready"), NH) if j == 0 else pe.wait_ge(sem("norm_ln"), NH)
            else:
                pe.wait_ge(sem("pv_out"), 4 * (g - 1) + j + 1)
            if c >= 1:
                pe.wait_ge(sem("kv_tok"), c)
            if small:
                turn(b7[0:NM, 0:P], src[:, M0:R0])
                last = turn(b7[0:NS, P:2 * P], src[:, 0:NS])
            else:
                for q in range(NB):
                    last = turn(b7[:, P * q:P * q + P], src[:, R0 + P * q:R0 + P * q + P])
            last.then_inc(sem("kv_turned"), 1)

        def att_scores(n):
            g, i = n // NB, n % NB
            pe.wait_ge(sem("qkv_in"), 4 * g + 4)
            if n == 0:
                pe.wait_ge(sem("mixed"), NH + 1)
            else:
                pe.wait_ge(sem("pT_out"), n)
            q, k = qT[g % 2], kT[g % 2]
            w, lo = P * (i + 1), R0 + P * i
            for hd in range(2):
                mm((b4, b5)[hd][:, 0:w], q[:, hd, lo:lo + P], k[:, R0:R0 + w], start=True, stop=True)
                last = mm(b6[:, NM * hd:NM * hd + NM], q[:, hd, lo:lo + P], k[:, M0:R0], start=True, stop=True)
                if i == 0:
                    last = mm(b6[0:NM, 2 * NM + NM * hd:3 * NM + NM * hd], q[:, hd, M0:R0], k[:, M0:R0],
                              start=True, stop=True)
            last.then_inc(sem("att_scores"), 1)

        def p_turn(n):
            i = n % NB
            pe.wait_ge(sem("att_p"), n + 1)
            for hd in range(2):
                for c in range(i + 1):
                    turn((b4, b5)[hd][:, P * c:P * c + P], lg[:, hd, NM + P * c:NM + P * c + P])
                last = turn(b6[0:NM, P * hd:P * hd + P], lg[:, hd, 0:NM])
                if i == 0:
                    last = turn(b6[0:NM, 2 * P + NM * hd:2 * P + NM * hd + NM], lgm[:, hd, :])
            last.then_inc(sem("p_turned"), 1)

        def pv(n):
            g, i = n // NB, n % NB
            v = vtok[g % 2]
            pe.wait_ge(sem("pT_out"), n + 1)
            pe.wait_ge(sem("kv_tok"), min(16, 4 * g + 4 + (0, 2, 4, 4)[i]))
            if n == 3:
                pe.wait_ge(sem("grow_ready"), 1)
            for hd in range(2):
                out = b7[:, P * hd:P * hd + P]
                for c in range(i + 1):
                    mm(out, v[:, c, :], pT[:, hd, P * c:P * c + P], start=(c == 0), stop=False)
                last = mm(out, v[0:NM, 4, :], pTm[:, P * hd:P * hd + P], start=False, stop=True)
            if i == 0:
                for hd in range(2):
                    last = mm(b7[:, 2 * P + NM * hd:2 * P + NM * hd + NM], v[0:NM, 4, :],
                              pTm[:, 2 * P + NM * hd:2 * P + NM * hd + NM], start=True, stop=True)
            last.then_inc(sem("pv_done"), 1)

        def row_turn():
            pe.wait_ge(sem("rows_ready"), 1)
            pe.wait_ge(sem("pv_out"), 3)
            for blk in range(NBLK):
                last = turn(b7[:, NS * blk:NS * blk + NS], work[:, 3, P * blk:P * blk + P])
            last.then_inc(sem("rows_turned"), 1)

        for g in range(NG):
            for j in range(4):
                side = {}
                if g == 0:
                    side = late(7, j)
                    if j == 2:
                        side = {2: (lambda: kv_turn(0, 0, 0),), 5: (lambda: kv_turn(0, 0, 1),), 11: side[11]}
                    if j == 3:
                        side = {12: (lambda: kv_turn(0, 1, 0),), 15: (lambda: kv_turn(0, 1, 1),)}
                else:
                    n = 4 * (g - 1) + j
                    if n >= 1:
                        side[3] = (lambda n=n: pv(n - 1),)
                    side[5] = (lambda n=n: att_scores(n),)
                    if j in (1, 2):
                        side[8] = (lambda g=g, j=j: kv_turn(g, j - 1, 0),)
                        side[11] = (lambda g=g, j=j: kv_turn(g, j - 1, 1),)
                    if n == 3:
                        side[8] = (row_turn,)
                    side[15] = (lambda n=n: p_turn(n),)
                s = At(S_B + 4 * g + j)
                product(s, s, KD, P, 0, X, side)

        def mix_in(k):
            return lambda: pe.wait_ge(sem("mix_in"), k + 1)

        def sg_turn(b):
            pe.wait_ge(sem(f"gk{b % 2}"), 16 * NBLK * (b // 2 + 1))
            pe.wait_ge(sem("sgT"), b) if b >= 1 else pe.wait_ge(sem("pT_out"), 16)
            for blk in range(NBLK):
                for g in range(NG):
                    last = turn((b4, b5)[blk][:, P * g:P * g + P], kgs[:, b % 2, blk, P * g:P * g + P])
            last.then_inc(sem("sg_turned"), 1)

        def s_scores(b):
            pe.wait_ge(sem("sgT"), b + 1)
            if b >= 1:
                pe.wait_ge(sem("sexp"), b)
            out = b6[0:NH, 0:KEEP_S + 1]
            mm(out, ident[0:NS, b:b + 1].to_broadcast([NS, NH]), maskS[:], start=True, stop=False)
            mm(out, nsl[:, b, :], distS[:], start=False, stop=False)
            for g in range(NG):
                mm(b6[0:NH, 0:KEEP_S], qpad[:, g, b, :], kgT[:, :, g, :], start=False, stop=False)
            for g in range(NG):
                last = mm(b6[0:NH, KEEP_S:KEEP_S + 1], qpad[:, g, b, :], knew[:, g, b:b + 1], start=False, stop=(g == NG - 1))
            last.then_inc(sem("slog"), 1)

        def sp_turn(b):
            pe.wait_ge(sem("sp_ready"), b + 1)
            pe.wait_ge(sem("so_out"), b) if b >= 1 else pe.wait_ge(sem("pv_out"), 16)
            for blk in range(NBLK):
                turn(b7[:, 8 * blk:8 * blk + 8], ps[:, P * blk:P * blk + P])
            mm(b7[0:NS, 16:24], pz[:, NS - 1 - b:2 * NS - 1 - b], ident[0:NH, 0:NH], start=True, stop=True)\
                .then_inc(sem("sp_turned"), 1)

        def s_pv(b):
            pe.wait_ge(sem("spT"), b + 1)
            pe.wait_ge(sem(f"gv{b % 2}"), 16 * NBLK * (b // 2 + 1))
            if b == 0:
                pe.wait_ge(sem("vnew_in"), NG)
            for g in range(NG):
                out = b7[:, 32 + 2 * g:34 + 2 * g]
                for blk in range(NBLK):
                    mm(out, vgs[:, b % 2, blk, P * g:P * g + P], pTs[:, 8 * blk + 2 * g:8 * blk + 2 * g + 2],
                       start=(blk == 0), stop=False)
                last = mm(out, vnew[:, g, :], pTs[0:NS, 16 + 2 * g:18 + 2 * g], start=False, stop=True)
            last.then_inc(sem("so_done"), 1)

        mix_in(0)()
        for n in range(8):
            for i in range(2):
                side = {}
                if n == 0 and i == 0:
                    side = {k: (mix_in(k + 1),) for k in range(7)}
                if n <= 3:
                    if i == 0:
                        side[3] = side.get(3, ()) + (lambda n=n: pv(11 + n),)
                        side[5] = side.get(5, ()) + (lambda n=n: att_scores(12 + n),)
                    else:
                        side[7] = (lambda n=n: p_turn(12 + n),)
                else:
                    b = 2 * (n - 4) + i
                    side = {0: (lambda b=b: sg_turn(b),), 2: (lambda b=b: s_scores(b),),
                            6: (lambda b=b: sp_turn(b),), 7: (lambda b=b: s_pv(b),)}
                    if b == 0:
                        side[0] = (lambda: pv(15),) + side[0]
                product(At(S_D1 + n), At(T_D1 + 2 * n + i), 8, 256, i, X, side, kx0=8)

        def att_in(k):
            return lambda: pe.wait_ge(sem("att_in"), k + 1)

        def d2(n2):
            for i in range(2):
                for e in range(2):
                    if isinstance(n2, int):
                        s, t = At(S_D2 + i + 2 * n2), At(T_D2 + 2 * i + e + 4 * n2)
                    else:
                        s, t = At(S_D2 + i, 2, n2), At(T_D2 + 2 * i + e, 4, n2)
                    side = {k: (att_in(k + 1),) for k in range(7)} if isinstance(n2, int) and i == e == 0 else {}
                    product(s, t, 8, 256, e, X, side)

        att_in(0)()
        d2(0)
        with pe.Fori(1, 4, 1) as n2:
            d2(n2)

        def ln_sums(n):
            pe.wait_ge(sem("s_sum"), 16 * n)
            pe.wait_ge(sem("q_sum"), 16 * n)
            if n == 1:
                pe.wait_ge(sem("so_out"), NS)
            mm(b4[:, :], ones[:], ssum[:, 0, R0:NT], start=True, stop=True)
            mm(b5[:, 0:R0], ones[:], ssum[:, 0, 0:R0], start=True, stop=True)
            mm(b6[:, :], ones[:], ssum[:, 1, R0:NT], start=True, stop=True)
            mm(b7[:, 0:R0], ones[:], ssum[:, 1, 0:R0], start=True, stop=True).then_inc(sem("ln_sums"), 1)

        ln_sums(1)

        def x1_in(k):
            return lambda: pe.wait_ge(sem("x1_in"), k + 1)

        def mlp(c):
            first = isinstance(c, int) and c == 0
            for n in range(8):
                side = {k: (x1_in(k + 1),) for k in range(KD - 1)} if first and n == 0 else {}
                product(e_tile(n, c), e_result(n, 0, c), KD, P, 0, X, side)
            for n in range(8, 12):
                for i in range(4):
                    side = {k: (lambda k=k: pe.wait_ge(sem("hl_done"), 4 * c + k + 2),) for k in range(3)} \
                        if n == 8 and i == 0 else {}
                    if n == 8 and i == 0:
                        pe.wait_ge(sem("hl_done"), 4 * c + 1)
                    product(e_tile(n, c), e_result(n, i, c), FC, 512, i, (hh, hl), side)

        x1_in(0)()
        mlp(0)
        with pe.Fori(1, NC - 1, 1) as c:
            mlp(c)
        mlp(NC - 1)
        ln_sums(2)
        for q in range(4):
            pe.wait_ge(sem("y_ready"), 4 * q + 4)
            if q == 0:
                pe.wait_ge(sem("s_done"), 32)
            for c in range(NB + 1):
                u = 5 * q + c
                if u >= 8:
                    v = u - 7
                    pe.wait_ge(sem(("y_act", "y_dve")[u % 2]), (v + 1) // 2 if u % 2 == 0 else v // 2)
                for k in range(4):
                    out = y_bank(u)[:, P * k:P * k + P]
                    if c < NB:
                        last = turn(out, sacc[:, 4 * q + k, R0 + P * c:R0 + P * c + P])
                    else:
                        last = turn(out[0:NS], sacc[:, 4 * q + k, 0:NS])
                last.then_inc(sem("y_turned"), 1)

    @block.vector
    def _(dve):
        V = nc.vector
        ch = Chain(dve, sem("dve_step"))

        def split(s, n=2048):
            dve.wait_ge(sem("h_split"), (s + 1).v)
            V.tensor_tensor(wl[:, s.odd, 0:n], raw[:, s.odd, 0:n], fr(wh[:, s.odd, 0:n]), ALU.subtract)\
                .then_inc(sem("l_split"), 1)

        split(At(0))
        split(At(1))
        dve.wait_ge(sem("act_step"), 1)
        ch(V.tensor_tensor(lb[:, 16:24], vec[:, 64:72], vec[:, 72:80], ALU.max))
        V.tensor_tensor(lb[:, 8:16], vec[:, 72:80], lb[:, 16:24], ALU.subtract)
        V.tensor_tensor(lb[:, 0:8], vec[:, 64:72], lb[:, 16:24], ALU.subtract).then_inc(sem("lb_shifted"), 1)
        for c in range(5):
            n, src = (R0, xtok_s) if c == NB else (P, xtok[:, c, :])
            dve.wait_ge(sem(f"x_in{c}"), 32 if c == NB else 16)
            for q in range(4):
                last = V.bn_stats(bn[0:n, c, q, :], src[0:n, q * 512:q * 512 + 512])
            ch(last)
            V.bn_aggr(mv[0:n, c, :], bn[0:n, c, :, :].rearrange("p a b -> p (a b)")).then_inc(sem("var"), 1)
            dve.wait_ge(sem("rstd"), c + 1)
            V.tensor_scalar(src[0:n, :], src[0:n, :], mv[0:n, c, 0:1], mv[0:n, c, 1:2], ALU.subtract, ALU.mult)\
                .then_inc(sem("x_norm"), 1)
        dve.wait_ge(sem("lb_exp"), 1)
        ch(V.tensor_tensor(lb[:, 16:24], lb[:, 0:8], lb[:, 8:16], ALU.add))
        ch(V.reciprocal(lb[:, 16:24], lb[:, 16:24]))
        ch(V.tensor_tensor(lb[:, 0:8], lb[:, 0:8], lb[:, 16:24], ALU.mult))
        V.tensor_scalar(lb[:, 16:24], lb[:, 0:8], 1.0, None, ALU.subtract)
        ch(V.tensor_scalar(lb[:, 8:16], lb[:, 0:8], -1.0, 1.0, ALU.mult, ALU.add))
        real, small = (b4, b6), (b5, b7)
        for k in range(KD):
            dve.wait_ge(sem("x_turned"), k + 1)
            if k >= 2:
                dve.wait_ge(sem("xl_ready"), k - 1)
            g, b = vec[:, k:k + 1], vec[:, 16 + k:17 + k]
            V.tensor_scalar(lnt[:, k % 2, R0:NT], real[k % 2][:, :], g, b, ALU.mult, ALU.add)
            V.tensor_scalar(lnt[:, k % 2, 0:R0], small[k % 2][:, 0:R0], g, b, ALU.mult, ALU.add).then_inc(sem("x_lin"), 1)
            dve.wait_ge(sem("xh_ready"), k + 1)
            V.tensor_tensor(xl[:, k, :], lnt[:, k % 2, :], fr(xh[:, k, :]), ALU.subtract).then_inc(sem("xl_ready"), 1)
        for i in range(2, 5):
            split(At(i), KD * 72 if i == 4 else 2048)
        split(At(S_C))
        dve.wait_ge(sem("pt_in"), 32)
        V.tensor_copy(ptT[:], pt_i[:, 0, :])
        V.tensor_copy(ptB[:], pt_i[:, 1, :]).then_inc(sem("pt_ready"), 1)
        dve.wait_ge(sem("consts"), 1)
        ch(V.tensor_scalar(pmod[:].bitcast(I32), pmod[:].bitcast(I32), 15, None, ALU.bitwise_and))
        ch(V.tensor_copy(pmod[:], pmod[:].bitcast(I32)))
        dve.wait_ge(sem("krow_sum"), 1)
        V.tensor_tensor(krow[:], b7[:, 64:72], pmod[:], ALU.add).then_inc(sem("krow_ready"), 1)

        def idx_setup():
            dve.wait_ge(sem("wk_ready"), 1)
            ch(V.tensor_scalar(wk[:, 0:4, 0:8], wk[:, 0:4, 0:8], IDX_W_SCALE, None, ALU.mult))
            ch(V.tensor_scalar(wk[0:NS, 5, 0:8], wk[0:NS, 5, 0:8], IDX_W_SCALE, None, ALU.mult))
            ch(V.tensor_tensor(wsel[:], wk[0:NS, 5, 0:8].unsqueeze(1).to_broadcast([NS, NS, NH]),
                               ident[0:NS, 0:NS].unsqueeze(2).to_broadcast([NS, NS, NH]), ALU.mult))
            dve.wait_ge(sem("ki_ready"), 1)
            V.tensor_tensor(prod[:], qiT[:, :, 0:NS], kiT[:, 0:NS].unsqueeze(1).to_broadcast([P, 4, NS]), ALU.mult)\
                .then_inc(sem("prod_ready"), 1)

        def idx_samples():
            dve.wait_ge(sem("wbc_sum"), 1)
            ch(V.tensor_copy(wbc[:], b4[:, 0:64].rearrange("p (b h) -> p b h", b=NS)))
            dve.wait_ge(sem("sidx_relu"), 1)
            for e in range(2):
                v = rsc[:, e, :].rearrange("p (b r h) -> p b r h", b=NS, r=4)
                ch(V.tensor_tensor(v, v, wbc[:].unsqueeze(2).to_broadcast([P, NS, 4, NH]), ALU.mult))
                ch(V.tensor_reduce(isc[:, e, :, :], v, AX, ALU.add))
            dve.sem_inc(sem("isc_ready"), 1)
            dve.wait_ge(sem("nsc_relu"), 1)
            ch(V.tensor_tensor(nsc[:], nsc[:], wk[0:NS, 5, 0:8], ALU.mult))
            ch(V.tensor_reduce(curs[:, PAST:PAST + 1], nsc[:], AX, ALU.add))
            dve.wait_ge(sem("isc_turned"), 1)
            rows = curs[:, 0:PAST].rearrange("b (p r e) -> b e r p", r=4, e=2)
            for e in range(2):
                V.tensor_copy(rows[:, e], (b4, b5)[e][0:NS, :].rearrange("b (r p) -> b r p", r=4))\
                    .then_inc(sem("isc_read"), 1)
            dve.wait_ge(sem("isc_read"), 2)

        def idx_sum(i, m):
            n = 4 * i + m
            out = cur[:, WOFF[i]:WOFF[i] + WIDE[i]]
            for e in range(2):
                w = wk[:, i, 2 * m + e:2 * m + e + 1]
                dve.wait_ge(sem("idx_relu"), 2 * n + e + 1)
                if m == 0 and e == 0:
                    ch(V.tensor_scalar(out, rel[:, e, 0:WIDE[i]], w, None, ALU.mult))
                else:
                    ch(V.scalar_tensor_tensor(out=out, in0=rel[:, e, 0:WIDE[i]], scalar=w, in1=out,
                                              op0=ALU.mult, op1=ALU.add))
            dve.sem_inc(sem("idx_summed"), 1)
            if m == 3:
                ch(V.tensor_tensor(out[:, WIDE[i] - P:WIDE[i]], out[:, WIDE[i] - P:WIDE[i]], causal[:], ALU.add))

        def take_prompt(c2):
            for i in range(NB):
                V.max(top8[:, i, :], cur[:, WOFF[i]:WOFF[i] + WIDE[i]]).then_inc(sem("dve_top"), 1)
            wait_apart(dve, sem("dve_top"), c2 + 4, sem("dve_seen"))
            for i in range(NB):
                row = cur[:, WOFF[i]:WOFF[i] + WIDE[i]]
                V.match_replace(row, top8[:, i, :], row, TAKEN).then_inc(sem("dve_top"), 1)
            wait_apart(dve, sem("dve_top"), c2 + 8, sem("dve_seen"))

        def take_sample(c3, slot):
            V.max(tops[:], curs[:]).then_inc(sem("dve_tops"), 1)
            wait_apart(dve, sem("dve_tops"), c3 + 1, sem("dve_seen"))
            V.max_index(topi[:], tops[:], curs[:]).then_inc(sem("dve_tops"), 1)
            V.match_replace(curs[:], tops[:], curs[:], TAKEN).then_inc(sem("dve_tops"), 1)
            dve.wait_ge(sem("dve_tops"), c3 + 3)
            V.tensor_copy(slot, topi[:]).then_inc(sem("dve_tops"), 1)
            dve.wait_ge(sem("dve_tops"), c3 + 4)

        def t_of(h4, j):
            return h4 + (S_C + j)

        def lbcol(n, which):
            return lb[:, 8 * which + n:8 * which + n + 1] if isinstance(n, int) else lb[:, bass.ds(n + 8 * which, 1)]

        def cap(u):
            dve.wait_ge(sem("sig_exp"), u + 1)
            V.tensor_scalar(t1[:, :], t1[:, :], SIG_CAP, None, ALU.min).then_inc(sem("sig_capped"), 1)

        SCAN = 8

        def forget(h4, n):
            t = t_of(h4, 0)
            cap(3 * n)
            V.sem_inc(sem(f"acc_read{t.odd}"), 1)
            dve.wait_ge(sem("sigmoid"), 3 * n + 1)
            dve.wait_ge(sem("head_turned"), n)
            V.tensor_scalar(kf[:, :], t1[:, :], lbcol(n, 2), lbcol(n, 1), ALU.mult, ALU.add).then_inc(sem("kf_ready"), 1)
            dve.wait_ge(sem("logf"), n + 1)
            for c in range(NB):
                lo = R0 + P * c
                V.tensor_tensor_scan(bcum[:, lo:lo + P], ones[:], t2[:, lo:lo + P], 0.0, ALU.mult, ALU.add)
            V.tensor_tensor_scan(bcum[:, M0:R0], ones[:, 0:NM], t2[:, M0:R0], 0.0, ALU.mult, ALU.add)
            V.tensor_copy(bcum[:, 0:NS], t2[:, 0:NS]).then_inc(sem("b_ready"), 1)

        def query(h4, n):
            t = t_of(h4, 1)
            cap(3 * n + 1)
            dve.wait_ge(sem("sigmoid"), 3 * n + 2)
            dve.wait_ge(sem("ho_done"), n + 1)
            V.tensor_tensor(cut(hq[:, :]), whole(t), cut(t1[:, :]), ALU.mult).then_inc(sem("q_ready"), 1)
            dve.wait_ge(sem("q_ready"), n + 1)
            V.sem_inc(sem(f"acc_read{t.odd}"), 1)
            dve.wait_ge(sem("b_ready"), n + 1)
            dve.wait_ge(sem("intra_done"), n)
            v = bcum[:, R0:NT].rearrange("p (s x) -> p s x", x=SUB)
            V.tensor_tensor(qd[:, R0:NT].rearrange("p (s x) -> p s x", x=SUB), v,
                            v[:, :, SUB // 2 - 1:SUB // 2].to_broadcast([P, NR // SUB, SUB]), ALU.subtract)
            V.tensor_scalar(qd[:, M0:R0], bcum[:, M0:R0], bcum[:, M0 + 7:M0 + 8], None, ALU.subtract).then_inc(sem("qd_arg"), 1)

        def decays(h4, n):
            dve.wait_ge(sem("et_exp"), n + 1)
            off = 0
            kr = kf[:, R0:NT].rearrange("p (c x) -> p c x", c=NB)
            for i in range(4):
                w = SUB * (i + 1)
                v = et[:, off:off + NB * w].rearrange("p (c x) -> p c x", c=NB)
                V.tensor_tensor(v, v, kr[:, :, 0:w], ALU.mult)
                off += NB * w
            V.tensor_tensor(et[:, off:off + NM], et[:, off:off + NM], kf[:, M0:R0], ALU.mult)
            dve.wait_ge(sem("ke_exp"), n + 1)
            V.tensor_tensor(ke[:, M0:NT], ke[:, M0:NT], kf[:, M0:NT], ALU.mult)
            dve.wait_ge(sem("qe_exp"), n + 1)
            V.tensor_tensor(qe[:, M0:NT], qe[:, M0:NT], hq[:, M0:NT], ALU.mult)
            dve.wait_ge(sem("qd_exp"), n + 1)
            V.tensor_tensor(qd[:, M0:NT], qd[:, M0:NT], hq[:, M0:NT], ALU.mult).then_inc(sem("qd_ready"), 1)

        def triangle(n):
            dve.wait_ge(sem("intra_done"), n + 1)
            dve.wait_ge(sem("ho_done"), n + 1)
            v = b7[:, :].rearrange("p (c x) -> p c x", c=NB)
            for i in range(4):
                w, lo = SUB * (i + 1), SUB * i
                V.tensor_tensor(aT[0:w, :, lo:lo + SUB], v[0:w, :, lo:lo + SUB],
                                tri[0:w, lo:lo + SUB].unsqueeze(1).to_broadcast([w, NB, SUB]), ALU.mult)
            dve.wait_ge(sem("tok_ready"), n + 1)
            V.tensor_tensor(aTm[:], b5[0:NM, 3 * P:3 * P + NM], tri[0:NM, 0:NM], ALU.mult).then_inc(sem("aT_ready"), 1)

        def gating(h4, n):
            t = t_of(h4, 3)
            cap(3 * n + 2)
            dve.wait_ge(sem("sigmoid"), 3 * n + 3)
            dve.wait_ge(sem("mixed"), n + 1)
            V.tensor_tensor(cut(gate[:, :]), whole(t), cut(t1[:, :]), ALU.mult).then_inc(sem("gate_ready"), 1)
            dve.wait_ge(sem("gate_ready"), n + 1)
            V.sem_inc(sem(f"acc_read{t.odd}"), 1)

        def states(n, cst):
            dve.wait_ge(sem("outer_done"), n + 1)
            dve.wait_ge(sem("ends_exp"), n + 1)
            dve.wait_ge(sem("ho_done"), n + 1)
            dve.wait_ge(sem("state_left"), n + 1)
            V.tensor_copy(st[:, 0, :], b5[:, 0:P]).then_inc(sem("dve_st"), 1)
            for c in range(NB):
                dve.wait_ge(sem("dve_st"), cst + c + 1)
                ins = V.scalar_tensor_tensor(out=st[:, c + 1, :], in0=st[:, c, :], scalar=eb[:, c:c + 1],
                                             in1=b4[:, P * c:P * c + P], op0=ALU.mult, op1=ALU.add)
                ins.then_inc(sem("dve_st"), 1)
            dve.wait_ge(sem("dve_st"), cst + 5)
            dve.sem_inc(sem("st_ready"), 1)
            dve.wait_ge(sem("spread_done"), n + 1)
            dve.wait_ge(sem("state_in"), (n + 1) * 16)
            for b in range(NS):
                V.tensor_scalar(ss[:, b, :], ss[:, b, :], fs[:, b:b + 1], None, ALU.mult).then_inc(sem("dve_st"), 1)
            dve.wait_ge(sem("dve_st"), cst + 5 + NS)
            for b in range(NS):
                ins = V.scalar_tensor_tensor(out=ss[:, b, :], in0=(b6, b7)[b // 4][:, P * (b % 4):P * (b % 4) + P],
                                             scalar=kf[:, b:b + 1], in1=ss[:, b, :], op0=ALU.mult, op1=ALU.add)
            ins.then_inc(sem("sstate_ready"), 1)
            return 5 + NS

        def mix(n, cm):
            dve.wait_ge(sem("norm_scale"), n + 1)
            V.tensor_tensor(t2[:, R0:NT], b4[:, :], t2[:, R0:NT], ALU.mult).then_inc(sem("dve_mix"), 1)
            V.tensor_tensor(t2[:, 0:R0], b5[:, 0:R0], t2[:, 0:R0], ALU.mult).then_inc(sem("dve_mix"), 1)
            dve.wait_ge(sem("dve_mix"), cm + 2)
            dst = sacc[:, NH + n, :] if isinstance(n, int) else sacc[:, bass.ds(n + NH, 1), :].rearrange("p o n -> p (o n)")
            V.scalar_tensor_tensor(out=dst, in0=t2[:, :], scalar=vec[:, 80:81], in1=gate[:, :],
                                   op0=ALU.mult, op1=ALU.mult).then_inc(sem("mixed"), 1)

        def early(h4, n, j):
            if j == 1:
                forget(h4, n)
            if j == 2:
                query(h4, n)
            if j == 3:
                decays(h4, n)

        def late(h4, n, j):
            if j == 0:
                triangle(n)
                gating(h4, n)
            if j == 1:
                states(n, n * (5 + NS))
            if j == 3:
                mix(n, n * 2)

        idx_setup()
        dve.wait_ge(sem("x_turned"), KD)
        V.memset(aT[:], 0.0)
        for j in range(4):
            split(At(S_C + j + 1))
            early(At(0), 0, j)
            if j == 0:
                idx_samples()
            for m in range(4):
                idx_sum(j, m)
        with dve.Fori(1, NH, 1) as h:
            for j in range(4):
                split(At(S_C + j + 1, 4, h))
                late(At(-4, 4, h), h - 1, j)
                early(At(0, 4, h), h, j)
                if j < 2:
                    take_prompt((h - 1) * 16 + 8 * j)
                take_sample((h - 1) * 16 + 4 * j, idx[:, bass.ds((h - 1) * 32 + 8 * j, 8)])

        def keep_prompt(i):
            row = cur[:, WOFF[i]:WOFF[i] + WIDE[i]]
            w = WIDE[i]
            eq, rank, cnt = et[:, 0:w], et[:, 528:528 + w], et[:, 1060:1064]
            km = keepmask[:, WOFF[i]:WOFF[i] + w]
            top = top8[:, i, :]
            ch(V.max(top, row))
            least = top8[:, i, 3:4]
            V.tensor_scalar(cnt[:, 0:3], top8[:, i, 0:3], least, None, ALU.is_gt)
            ch(V.tensor_scalar(eq, row, least, None, ALU.is_equal))
            V.tensor_tensor_scan(rank, eq, eq, 0.0, ALU.add, ALU.max)
            ch(V.tensor_reduce(cnt[:, 3:4], cnt[:, 0:3], AX, ALU.add))
            ch(V.tensor_scalar(cnt[:, 3:4], cnt[:, 3:4], -1.0, 4.0, ALU.mult, ALU.add))
            ch(V.scalar_tensor_tensor(out=rank, in0=rank, scalar=cnt[:, 3:4], in1=eq, op0=ALU.is_le, op1=ALU.mult))
            ch(V.scalar_tensor_tensor(out=rank, in0=row, scalar=least, in1=rank, op0=ALU.is_gt, op1=ALU.add))
            ch(V.scalar_tensor_tensor(out=rank, in0=row, scalar=TAKEN, in1=rank, op0=ALU.is_equal, op1=ALU.add))
            ch(V.tensor_scalar(km, rank, -OFF, OFF, ALU.mult, ALU.add))
            ch(V.tensor_tensor(km[:, w - P:w], km[:, w - P:w], causal[:], ALU.add))

        def sample_rows():
            page, pos, rows = work[:, 0, :], work[:, 1, :], work[:, 3, :]
            ch(V.tensor_scalar(page.bitcast(I32), idx[:].bitcast(I32), 7, None, ALU.logical_shift_right))
            ch(V.tensor_scalar(pos.bitcast(I32), idx[:].bitcast(I32), P - 1, None, ALU.bitwise_and))
            ch(V.tensor_copy(page, page.bitcast(I32)))
            ch(V.tensor_copy(rows, pos.bitcast(I32)))
            ch(V.tensor_copy(pos, idx[:].bitcast(I32)))
            ch(V.tensor_scalar(distS[:, 0:KEEP_S], pos, -1.0, float(PAST), ALU.mult, ALU.add))
            ch(V.memset(distS[:, KEEP_S:KEEP_S + 1], 0.0))
            ch(V.tensor_scalar(maskS[:, 0:KEEP_S], pos, float(PAST), None, ALU.is_ge))
            ch(V.tensor_reduce(maskS[:, KEEP_S:KEEP_S + 1], maskS[:, 0:KEEP_S], AX, ALU.add))
            ch(V.tensor_scalar(maskS[:, 0:KEEP_S], maskS[:, 0:KEEP_S], OFF, None, ALU.mult))
            ch(V.tensor_scalar(maskS[:, KEEP_S:KEEP_S + 1], maskS[:, KEEP_S:KEEP_S + 1], -OFF, OFF, ALU.mult, ALU.add))
            for q in range(PAST // P):
                ch(V.tensor_scalar(work[:, 2, :], page, float(q), ptB[:, q:q + 1], ALU.is_equal, ALU.mult))
                ch(V.scalar_tensor_tensor(out=rows, in0=work[:, 2, :], scalar=float(P), in1=rows,
                                          op0=ALU.mult, op1=ALU.add))
            V.tensor_tensor(nsl[:], ident[0:NS, 0:NS].unsqueeze(2).to_broadcast([NS, NS, NH]),
                            slope8[:].unsqueeze(1).to_broadcast([NS, NS, NH]), ALU.mult).then_inc(sem("rows_ready"), 1)

        def attend(n):
            g, i = n // NB, n % NB
            w = WIDE[i]
            if n >= 1:
                dve.wait_ge(sem("p_turned"), n)
            for hd in range(2):
                slope = -(2.0 ** -(2 * g + hd + 1))
                ch(V.scalar_tensor_tensor(out=lg[:, hd, 0:w], in0=dist[:, 384 - P * i:384 - P * i + w], scalar=slope,
                                          in1=keepmask[:, WOFF[i]:WOFF[i] + w], op0=ALU.mult, op1=ALU.add))
                if i == 0:
                    ch(V.scalar_tensor_tensor(out=lgm[:, hd, :], in0=dist[0:NM, 400:400 + NM], scalar=slope,
                                              in1=causal[0:NM, 0:NM], op0=ALU.mult, op1=ALU.add))
            dve.wait_ge(sem("att_scores"), n + 1)
            for hd in range(2):
                V.scalar_tensor_tensor(out=lg[:, hd, NM:w], in0=(b4, b5)[hd][:, 0:w - NM], scalar=ATTN_SCALE,
                                       in1=lg[:, hd, NM:w], op0=ALU.mult, op1=ALU.add)
                last = V.scalar_tensor_tensor(out=lg[:, hd, 0:NM], in0=b6[:, NM * hd:NM * hd + NM], scalar=ATTN_SCALE,
                                              in1=lg[:, hd, 0:NM], op0=ALU.mult, op1=ALU.add)
                if i == 0:
                    last = V.scalar_tensor_tensor(out=lgm[:, hd, :], in0=b6[0:NM, 2 * NM + NM * hd:3 * NM + NM * hd],
                                                  scalar=ATTN_SCALE, in1=lgm[:, hd, :], op0=ALU.mult, op1=ALU.add)
            ch(last)
            last = V.tensor_reduce(nmx[:, 0, :], lg[:, :, 0:w], AX, ALU.max)
            if i == 0:
                last = V.tensor_reduce(nmxm[:, 0, :], lgm[:], AX, ALU.max)
            ch(last)
            if i == 0:
                ch(V.tensor_scalar(nmxm[:, 0, :], nmxm[:, 0, :], -1.0, None, ALU.mult))
            V.tensor_scalar(nmx[:, 0, :], nmx[:, 0, :], -1.0, None, ALU.mult).then_inc(sem("att_max"), 1)
            dve.wait_ge(sem("att_exp"), n + 1)
            last = V.reciprocal(nmx[:, 1, :], nmx[:, 1, :])
            if i == 0:
                last = V.reciprocal(nmxm[:, 1, :], nmxm[:, 1, :])
            ch(last)
            for hd in range(2):
                if i == 0:
                    V.tensor_scalar(lgm[:, hd, :], lgm[:, hd, :], nmxm[:, 1, hd:hd + 1], None, ALU.mult)
                last = V.tensor_scalar(lg[:, hd, 0:w], lg[:, hd, 0:w], nmx[:, 1, hd:hd + 1], None, ALU.mult)
            last.then_inc(sem("att_p"), 1)

        for g in range(NG):
            for j in range(4):
                split(At(S_B + 4 * g + j + 1))
                if g == 0:
                    late(At(28), 7, j)
                    if j == 0:
                        V.memset(qpad[:], 0.0).then_inc(sem("qpad_clear"), 1)
                    if j < 2:
                        take_prompt(112 + 8 * j)
                    take_sample(112 + 4 * j, idx[:, 224 + 8 * j:232 + 8 * j])
                    if j >= 2:
                        keep_prompt(2 * j - 4)
                        keep_prompt(2 * j - 3)
                else:
                    attend(4 * (g - 1) + j)
                    if g == 1 and j == 0:
                        dve.wait_ge(sem("sstate_out"), 16 * NH)
                        dve.wait_ge(sem("state_out"), 16 * NH)
                        sample_rows()
                    if g == 1 and j == 3:
                        dve.wait_ge(sem("rows_turned"), 1)
                        V.tensor_copy(grow[:].rearrange("p k b -> p (k b)"), b7[:, 0:16]).then_inc(sem("grow_ready"), 1)

        def x_sum(k):
            if k >= 2:
                dve.wait_ge(sem("resid"), k - 1)
            V.tensor_tensor(tmp[:, k % 2, :], fr(xh[:, 8 + k, :]), fr(xl[:, 8 + k, :]), ALU.add).then_inc(sem("x_sum"), 1)

        def mix_rest(k):
            dve.wait_ge(sem("mix_h"), k + 1)
            V.tensor_tensor(xl[:, 8 + k, :], sacc[:, 8 + k, :], fr(xh[:, 8 + k, :]), ALU.subtract).then_inc(sem("mix_in"), 1)

        def add_mix(n, i):
            t = At(T_D1 + 2 * n + i)
            m = (2 * n + i + 8) % KD
            dve.wait_ge(sem("mm"), (t + 1).v)
            V.tensor_tensor(cut(sacc[:, m, :]), cut(sacc[:, m, :]), whole(t), ALU.add).then_inc(sem(f"acc_read{t.odd}"), 1)

        def sample_att(b):
            dve.wait_ge(sem("slog"), b + 1)
            ch(V.tensor_reduce(snm[:, 0:1], b6[0:NH, 0:KEEP_S + 1], AX, ALU.max))
            V.tensor_scalar(snm[:, 0:1], snm[:, 0:1], -1.0, None, ALU.mult).then_inc(sem("smax"), 1)
            dve.wait_ge(sem("sexp"), b + 1)
            ch(V.reciprocal(snm[:, 1:2], snm[:, 1:2]))
            ch(V.tensor_scalar(ps[:, :], ps[:, :], snm[:, 1:2], None, ALU.mult))
            V.tensor_scalar(pz[:], zt[:], ps[:, KEEP_S:KEEP_S + 1], None, ALU.mult).then_inc(sem("sp_ready"), 1)

        for n in range(8):
            split(At(S_D1 + n + 1))
            if n == 0:
                x_sum(0)
                for k in range(8):
                    if k < 7:
                        x_sum(k + 1)
                    mix_rest(k)
            if n >= 1:
                add_mix(n - 1, 1)
            if n == 1:
                for k in range(8):
                    dve.wait_ge(sem("resid_h"), k + 1)
                    V.scalar_tensor_tensor(out=sacc[:, k, :], in0=fr(xl[:, k, :]), scalar=ALPHA, in1=sacc[:, k, :],
                                           op0=ALU.mult, op1=ALU.add).then_inc(sem("resid_lo"), 1)
            if n < 4:
                attend(12 + n)
                add_mix(n, 0)
            else:
                sample_att(2 * (n - 4))
                add_mix(n, 0)
                sample_att(2 * (n - 4) + 1)

        dve.wait_ge(sem("so_out"), NS)
        for k in range(NH):
            dve.wait_ge(sem("att_h"), k + 1)
            V.tensor_tensor(xl[:, k, :], attn_o[:, k, :], fr(xh[:, k, :]), ALU.subtract).then_inc(sem("att_in"), 1)
        add_mix(7, 1)

        def tile_of(buf, m):
            k = m.const % KD
            return buf[:, k, :] if m.reg is None else buf[:, bass.ds(m.v, 1), :].rearrange("p o n -> p (o n)")

        def finish(m, t):
            dve.wait_ge(sem("mm"), (t + 1).v)
            dst = tile_of(sacc, m)
            V.tensor_tensor(cut(dst), cut(dst), whole(t), ALU.add).then_inc(sem("s_done"), 1)
            dve.wait_ge(sem("s_done"), (m + 1).v)
            dve.sem_inc(sem(f"acc_read{t.odd}"), 1)
            dve.wait_ge(sem("s_sum"), m.v)
            V.tensor_tensor(ssum[:, 0, :], ssum[:, 0, :], dst, ALU.add).then_inc(sem("s_sum"), 1)

        def finish_square(m):
            dve.wait_ge(sem("sq_done"), (m + 1).v)
            dve.wait_ge(sem("q_sum"), m.v)
            V.tensor_tensor(ssum[:, 1, :], ssum[:, 1, :], sq[:, m.const % 2, :], ALU.add).then_inc(sem("q_sum"), 1)

        ch(V.memset(ssum[:], 0.0))

        def d2(n2):
            for i in range(2):
                split(At(S_D2 + i + 1, 2, n2) if not isinstance(n2, int) else At(S_D2 + i + 1 + 2 * n2))
                for e in range(2):
                    m = At(2 * i + e, 4, n2) if not isinstance(n2, int) else At(2 * i + e + 4 * n2)
                    finish(m, m + T_D2)
                    finish_square(m)

        d2(0)
        with dve.Fori(1, 4, 1) as n2:
            d2(n2)

        def ln_stats(n):
            dve.wait_ge(sem("ln_sums"), n)
            for src, part in ((b4, slice(R0, NT)), (b5, slice(0, R0))):
                last = V.tensor_scalar(mu[:, part], src[:, 0:part.stop - part.start], 1.0 / D, None, ALU.mult)
            ch(last)
            ch(V.tensor_tensor(rstd[:, :], mu[:, :], mu[:, :], ALU.mult))
            for src, part in ((b6, slice(R0, NT)), (b7, slice(0, R0))):
                last = V.scalar_tensor_tensor(out=rstd[:, part], in0=src[:, 0:part.stop - part.start], scalar=1.0 / D,
                                              in1=rstd[:, part], op0=ALU.mult, op1=ALU.subtract)
            last.then_inc(sem("ln_var"), 1)

        def center(k):
            ch(V.tensor_tensor(lnd[:, k % 2, :], sacc[:, k, :], mu[:, :], ALU.subtract))

        ln_stats(1)
        for k in range(KD):
            if k >= 2:
                dve.wait_ge(sem("x1_h"), k - 1)
            center(k)
            if k == 0:
                dve.wait_ge(sem("ln_rstd"), 1)
            V.tensor_tensor(lnd[:, k % 2, :], lnd[:, k % 2, :], rstd[:, :], ALU.mult).then_inc(sem("ln_norm"), 1)
            if k >= 1:
                dve.wait_ge(sem("x1_h"), k)
                V.tensor_tensor(xl[:, k - 1, :], sacc[:, k - 1, :], fr(xh[:, k - 1, :]), ALU.subtract).then_inc(sem("x1_in"), 1)
        dve.wait_ge(sem("x1_h"), KD)
        V.tensor_tensor(xl[:, KD - 1, :], sacc[:, KD - 1, :], fr(xh[:, KD - 1, :]), ALU.subtract).then_inc(sem("x1_in"), 1)
        ch(V.memset(ssum[:], 0.0))

        def down(m, t):
            dve.wait_ge(sem("mm"), (t + 1).v)
            V.tensor_tensor(cut(sacc[:, m, :]), cut(sacc[:, m, :]), whole(t), ALU.add).then_inc(sem("down_done"), 1)

        def mlp(c, last=False):
            for n in range(12):
                if not (last and n == 11):
                    nn, cc = (n + 1, c) if n < 11 else (0, c + 1)
                    split(e_tile(nn, cc))
                if n in (2, 4, 6, 8):
                    f = n // 2 - 1
                    t = e_result(n - 1, 0, c)
                    dve.wait_ge(sem("mm"), (t + 1).v)
                    dve.wait_ge(sem("gate_done"), 4 * c + f + 1)
                    if f >= 2 or not isinstance(c, int) or c >= 1:
                        dve.wait_ge(sem("hl_done"), 4 * c + f - 1)
                    V.tensor_tensor(cut(hbuf[:, f % 2, :]), whole(t), cut(gbuf[:, f % 2, :]), ALU.mult).then_inc(sem("gated"), 1)
                    dve.wait_ge(sem("gated"), 4 * c + f + 1)
                    dve.sem_inc(sem(f"acc_read{t.odd}"), 1)
                    dve.wait_ge(sem("hh_done"), 4 * c + f + 1)
                    V.tensor_tensor(hl[:, f, :], hbuf[:, f % 2, :], fr(hh[:, f, :]), ALU.subtract).then_inc(sem("hl_done"), 1)
                if n >= 8:
                    for i in range(4):
                        m = 4 * (n - 8) + i
                        t = e_result(n, i, c)
                        if last:
                            finish(At(16 + m), t)
                            finish_square(At(16 + m))
                        else:
                            dve.wait_ge(sem("mm"), (t + 1).v)
                            if isinstance(c, int):
                                dve.wait_ge(sem("x1_resid"), m + 1)
                            V.tensor_tensor(cut(sacc[:, m, :]), cut(sacc[:, m, :]), whole(t), ALU.add)\
                                .then_inc(sem(f"acc_read{t.odd}"), 1)

        mlp(0)
        with dve.Fori(1, NC - 1, 1) as c:
            mlp(c)
        mlp(NC - 1, last=True)
        ln_stats(2)
        for k in range(KD + 1):
            if k < KD:
                if k >= 2:
                    dve.wait_ge(sem("y_ready"), k - 1)
                center(k)
                if k == 0:
                    dve.wait_ge(sem("ln_rstd"), 2)
                V.tensor_tensor(lnd[:, k % 2, :], lnd[:, k % 2, :], rstd[:, :], ALU.mult).then_inc(sem("ln_norm"), 1)
            if k >= 4 and k % 4 == 0:
                q = k // 4 - 1
                for u in range(5 * q, 5 * q + 5):
                    if u % 2 == 1:
                        dve.wait_ge(sem("y_turned"), u + 1)
                        r = P if u % 5 < 4 else NS
                        V.tensor_copy(ytok[0:r, u % 5, 512 * q:512 * q + 512], y_bank(u)[0:r]).then_inc(sem("y_dve"), 1)


OUTPUTS = (
    (1, NR, D), (NS, 1, D),
    (1, 1, NM + NR, NG, HD), (1, 1, NM + NR, NG, HD), (1, 1, NM + NR, 64), (1, 1, NH, HD, HD),
    (1, NS, 1, NG, HD), (1, NS, 1, NG, HD), (1, NS, 1, 64), (1, NS, NH, HD, HD),
)
INPUTS = (
    "x_prompt", "x_sample", "cache_k", "cache_v", "cache_kidx", "state_hgrn", "page_table", "meta_tokens",
    "ln_in_g", "ln_in_b", "w_in", "hg_lb_logits", "hg_norm_g", "w_out", "ln1_g", "ln1_b",
    "w_gate", "w_up", "w_down", "ln2_g", "ln2_b",
)


def kernel(**inputs):
    import numpy as _np
    import concourse.bacc as _bacc
    from concourse import mybir as _mybir
    from concourse.bass_utils import run_bass_kernel_spmd as _run

    nc = _bacc.Bacc("TRN2", target_bir_lowering=False, num_devices=1)
    arrays, args = {}, []
    for name in INPUTS:
        a = _np.ascontiguousarray(inputs[name])
        arrays[f"in_{name}_dram"] = a
        args.append(nc.dram_tensor(f"in_{name}_dram", a.shape, _mybir.dt.from_np(a.dtype), kind="ExternalInput").ap())
    for i, shape in enumerate(OUTPUTS):
        args.append(nc.dram_tensor(f"out_{i}_dram", shape, _mybir.dt.float32, kind="ExternalOutput").ap())
    hymba_kernel(nc, *args)
    r = _run(nc, [arrays], core_ids=[0])
    return tuple(r.results[0][f"out_{i}_dram"] for i in range(len(OUTPUTS)))
```

```python
from contextlib import ExitStack

import concourse.bass as bass
from concourse import mybir

ALU = mybir.AluOpType
ACT = mybir.ActivationFunctionType
AX = mybir.AxisListType.X
F32 = mybir.dt.float32
F32R = mybir.dt.float32r
BF16 = mybir.dt.bfloat16
I32 = mybir.dt.int32
U32 = mybir.dt.uint32

P = 128
D = 2048
KD = D // P
NS = 8
NM = 16
NR = 512
NB = NR // P
M0 = NS
R0 = NS + NM
NT = NS + NM + NR
HALF = NT // 2
HD = 128
NG = 4
NH = 8
PAST = 1024
KEEP_P = (NM + NR) // 4
KEEP_S = 256
NBLK = KEEP_S // P
FF = 5632
FC = 4
NC = FF // (FC * P)
ALPHA = 2.0 ** 0.25
ATTN_SCALE = HD ** -0.5
IDX_SCALE = 64 ** -0.5
IDX_W_SCALE = NH ** -0.5
LN_EPS = 1e-5
NORM_EPS = 1e-6
INADMISSIBLE = -3.0e38
TAKEN = -3.4e38
OFF = -1.0e30
SIG_CAP = 1.0e18
SUB = 32
W_COLS = {"q": 0, "k": 1024, "v": 1536, "qi": 2048, "wk": 2560, "hq": 2632, "hf": 3656, "hi": 4680, "hg": 5704}
WIDE = [NM + P * i for i in range(1, NB + 1)]
WOFF = [sum(WIDE[:i]) for i in range(NB)]
S_C = 5
S_B = S_C + 4 * NH
S_D1 = S_B + 4 * NG
S_D2 = S_D1 + 8
S_E = S_D2 + 8
T_D1, T_D2 = S_D1, S_D1 + 16
T_E = T_D2 + 16


class At:

    def __init__(self, const, coef=0, reg=None):
        self.const, self.coef, self.reg = const, coef, reg

    def __add__(self, k):
        return At(self.const + k, self.coef, self.reg)

    def __sub__(self, k):
        return self + (-k)

    def half(self):
        return At(self.const // 2, self.coef // 2, self.reg)

    def times(self, k):
        return At(self.const * k, self.coef * k, self.reg)

    @property
    def odd(self):
        return self.const % 2

    @property
    def v(self):
        return self.const if self.reg is None else self.reg * self.coef + self.const


class Chain:

    def __init__(self, eng, sem, start=0):
        self.eng, self.sem, self.start, self.n = eng, sem, start, 0

    def __call__(self, ins):
        self.n += 1
        ins.then_inc(self.sem, 1)
        self.eng.wait_ge(self.sem, self.start + self.n)


def wait_apart(eng, sem, value, seen):
    eng.wait_ge(sem, value)
    eng.sem_inc(seen, 1)


def hymba_kernel(nc, *arrays):
    with ExitStack() as ctx:
        program(ctx, nc, *arrays)


def program(
    ctx, nc: bass.Bass, x_prompt, x_sample, cache_k, cache_v, cache_kidx, state_hgrn, page_table, meta_tokens,
    ln_in_g, ln_in_b, w_in, hg_lb_logits, hg_norm_g, w_out, ln1_g, ln1_b, w_gate, w_up, w_down, ln2_g, ln2_b,
    y_prompt, y_sample, k_prompt, v_prompt, kidx_prompt, hgrn_prompt, k_sample, v_sample, kidx_sample, hgrn_sample,
):
    sems = {}

    def sem(name):
        if name not in sems:
            sems[name] = ctx.enter_context(nc.semaphore(name))
        return sems[name]

    BASE = 16512

    def at(name, shape, dt, off):
        return nc.alloc_sbuf_tensor_at(name, shape, dt, offset=BASE + off)

    class Region:

        def __init__(self, start, size):
            self.pos, self.end = start, start + size

        def take(self, name, shape, dt=F32):
            n = 2 if dt == BF16 else 4
            for d in shape[1:]:
                n *= d
            n = (n + 31) // 32 * 32
            t = at(name, shape, dt, self.pos)
            self.pos += n
            assert self.pos <= self.end, (name, self.pos, self.end)
            return t

    TILE = NT * 4
    O_RAW = 2 * KD * TILE
    O_WH = O_RAW + 16384
    O_WL = O_WH + 16384
    O_SACC = O_WL + 16384
    O_ATT = O_SACC + KD * TILE
    O_R = O_ATT + NH * TILE
    TOP = 229344 - BASE

    xh = at("xh", [P, KD, NT], F32R, 0)
    xl = at("xl", [P, KD, NT], F32R, KD * TILE)
    raw = at("raw", [P, 2, 2048], F32, O_RAW)
    wh = at("wh", [P, 2, 2048], F32R, O_WH)
    wl = at("wl", [P, 2, 2048], F32R, O_WL)
    sacc = at("sacc", [P, KD, NT], F32, O_SACC)
    attn_o = at("attn_o", [P, NH, NT], F32, O_ATT)

    rr_ = Region(O_R, TOP - O_R)
    ident = rr_.take("ident", [P, P])
    ones = rr_.take("ones", [P, P])
    dist = rr_.take("dist", [P, 528])
    tri = rr_.take("tri", [P, P])
    causal = rr_.take("causal", [P, P])
    vec = rr_.take("vec", [P, 113])
    lb = rr_.take("lb", [P, 24])
    keepmask = rr_.take("keepmask", [P, sum(WIDE)], BF16)
    halfsel = rr_.take("halfsel", [P, 2])
    pageof = rr_.take("pageof", [8, P])
    pmod = rr_.take("pmod", [P, 8])
    ptT = rr_.take("ptT", [8, 8])
    ptB = rr_.take("ptB", [8, 8])
    pt_i = rr_.take("pt_i", [8, 2, 8], I32)
    grow = rr_.take("grow", [P, NBLK, NS], U32)
    slope8 = rr_.take("slope8", [8, NH])
    zt = rr_.take("zt", [8, 2 * NS - 1])
    R_START = rr_.pos
    mid = O_SACC + NH * TILE

    xtok = at("xtok", [P, NB, D], F32, O_SACC)
    xtok_s = at("xtok_s", [R0, D], F32, O_ATT)
    r0 = Region(R_START, TOP - R_START)
    vrows = r0.take("vrows", [113, P])
    bn = r0.take("bn", [P, 5, 4, 6])
    mv = r0.take("mv", [P, 5, 4])
    lnt = r0.take("lnt", [P, 2, NT])

    ra = Region(O_SACC, NH * TILE)
    rb = Region(R_START, TOP - R_START)
    qT = [ra.take("q0T", [P, 2, NT]), rb.take("q1T", [P, 2, NT])]
    kT = [ra.take("k0T", [P, NT]), rb.take("k1T", [P, NT])]
    vtok = [ra.take("v0tok", [P, 6, P]), rb.take("v1tok", [P, 6, P])]
    vT = ra.take("vT", [P, NT])
    ktok = ra.take("ktok", [P, 6, P])
    lg = rb.take("lg", [P, 2, 528])
    pT = rb.take("pT", [P, 2, NR])
    pTm = rb.take("pTm", [NM, 2 * P + 2 * NM])
    lgm = rb.take("lgm", [NM, 2, NM])
    nmx = rb.take("nmx", [P, 2, 2])
    nmxm = rb.take("nmxm", [NM, 2, 2])
    distS = rb.take("distS", [NS, KEEP_S + 1])
    maskS = rb.take("maskS", [NS, KEEP_S + 1])
    nsl = rb.take("nsl", [NS, NS, NH])
    work = rb.take("work", [NS, 4, KEEP_S])
    vnew = rb.take("vnew", [NS, NG, P])
    assert rb.pos <= R_START + 29248
    tmp = rb.take("tmp", [P, 2, NT])
    assert rb.pos <= R_START + 33408
    qpad = at("qpad", [P, NG, NS, NH], F32, R_START + 33408)
    knew = at("knew", [P, NG, NS], F32, R_START + 34432)
    assert R_START + 34432 + 128 <= TOP
    kgs = at("kgs", [P, 2, NBLK, NG * P], F32, 0)
    vgs = at("vgs", [P, 2, NBLK, NG * P], F32, 8192)
    kgT = at("kgT", [P, NBLK, NG, P], F32, KD * TILE)
    ps = at("ps", [NH, KEEP_S + 1], F32, KD * TILE + 4096)
    pz = at("pz", [NH, 2 * NS - 1], F32, KD * TILE + 5152)
    pTs = at("pTs", [P, 24], F32, KD * TILE + 5216)
    snm = at("snm", [NH, 2], F32, KD * TILE + 5344)

    rc = Region(O_ATT, NH * TILE)
    bcum = rc.take("bcum", [P, NT])
    kf = rc.take("kf", [P, NT])
    hq = rc.take("hq", [P, NT])
    gate = rc.take("gate", [P, NT])
    hiT = rc.take("hiT", [P, NT])
    qd = rc.take("qd", [P, NT])
    qe = rc.take("qe", [P, NT])
    ke = rc.take("ke", [P, NT])
    rd = Region(R_START, TOP - R_START)
    t1 = rd.take("t1", [P, NT])
    t2 = rd.take("t2", [P, NT])
    et = rd.take("et", [P, 4 * (32 + 64 + 96 + 128) + NM])
    itok = rd.take("itok", [P, 6, P])
    ketok = rd.take("ketok", [P, 5, P])
    aT = rd.take("aT", [P, NB, P])
    aTm = rd.take("aTm", [NM, NM])
    st = rd.take("st", [P, NB + 1, P])
    ss = rd.take("ss", [P, NS, P])
    cur = rd.take("cur", [P, sum(WIDE)])
    curs = rd.take("curs", [NS, PAST + 1])
    idx = at("idx", [NS, KEEP_S], U32, ra.pos)
    fs = at("fs", [P, NS], F32, ra.pos + 1024)
    eb = at("eb", [P, NB], F32, ra.pos + 1056)
    top8 = at("top8", [P, NB, 8], F32, ra.pos + 1088)
    tops = at("tops", [NS, 8], F32, ra.pos + 1216)
    topi = at("topi", [NS, 8], U32, ra.pos + 1248)
    assert ra.pos + 1280 <= O_SACC + NH * TILE

    ri = Region(mid, NH * TILE)
    qiT = ri.take("qiT", [P, 4, NT])
    wikiT = ri.take("wikiT", [72, NT])
    kiT = ri.take("kiT", [P, NT])
    wk = ri.take("wk", [P, 6, 136])
    ri2 = Region(O_SACC, NH * TILE - 2432)
    rel = ri2.take("rel", [P, 2, 528])
    kx = ri2.take("kx", [P, 2, 512])
    kxT = at("kxT", [P, NS, 512], F32, R_START + 7488)
    qS = ri.take("qS", [P, NS, 2, NH])
    wsel = ri.take("wsel", [NS, NS, NH])
    wbc = ri.take("wbc", [P, NS, NH])
    prod = rd.take("prod", [P, 4, NS])
    isc = rd.take("isc", [P, NS, 8])
    krow = rd.take("krow", [P, NS], U32)
    rsc = ri2.take("rsc", [P, 512])
    nsc = rd.take("nsc", [NS, NH])

    re_ = Region(O_ATT, TOP - O_ATT)
    hh = re_.take("hh", [P, FC, NT], F32R)
    hl = re_.take("hl", [P, FC, NT], F32R)
    rf = Region(R_START, TOP - R_START)
    ssum = rf.take("ssum", [P, 2, NT])
    sq = rf.take("sq", [P, 2, NT])
    mu = rf.take("mu", [P, NT])
    rstd = rf.take("rstd", [P, NT])
    lnd = rf.take("lnd", [P, 4, NT])
    gbuf = rf.take("gbuf", [P, 2, NT])
    hbuf = rf.take("hbuf", [P, 2, NT])
    ytok = at("ytok", [P, NB + 1, D], F32, 0)

    acc = ctx.enter_context(nc.psum_tensor("acc", [P, 2, 2, 512], F32))
    b4 = ctx.enter_context(nc.psum_tensor("b4", [P, 512], F32))
    b5 = ctx.enter_context(nc.psum_tensor("b5", [P, 512], F32))
    b6 = ctx.enter_context(nc.psum_tensor("b6", [P, 512], F32))
    b7 = ctx.enter_context(nc.psum_tensor("b7", [P, 512], F32))

    def whole(t):
        return acc[:, t.odd, :, 0:HALF]

    def cut(ap):
        return ap.rearrange("p (a n) -> p a n", a=2)

    def fr(ap):
        return ap.bitcast(F32)

    def mts(s):
        if s.reg is None and s.const >= S_D1:
            return At(T_D1 + 2 * (s.const - S_D1 + 1))
        assert s.const < S_D1
        return s + 1

    w_in3 = w_in[0].rearrange("(k p) n -> p k n", p=P)
    wo3 = w_out[0].rearrange("(k p) n -> p k n", p=P)

    def sC(h, j):
        return h + (S_C + j)

    HG = ("hf", "hq", "hi", "hg")
    IDX_BLOCKS = ((), (0, 1), (), (2, 3))

    def y_on_act(u):
        return u % 5 % 2 == 0

    def y_after(k):
        q, r = (k - 6) // 4, (k - 6) % 4
        if q < 0 or r > 1:
            return []
        return [5 * q + r, 5 * q + r + 2] + ([5 * q + 4] if r == 1 else [])

    def y_copied(u):
        return "y_act" if y_on_act(u) else "y_dve", len([v for v in range(u + 1) if y_on_act(v) == y_on_act(u)])

    def y_bank(u):
        u %= 8
        return (b4, b5, b6, b7)[u][:, :] if u < 4 else acc[:, (u - 4) // 2, u % 2, :]

    MLP_BODY = (("gate", 0), ("down", 0), ("down", 1), ("down", 2), ("down", 3), ("up", 0), ("gate", 1), ("up", 1),
                ("gate", 2), ("up", 2), ("gate", 3), ("up", 3))

    def mlp_plan(c):
        whole_body = not isinstance(c, int) or 1 <= c < NC
        if whole_body:
            s, t = (At(S_E - 4, 12, c), At(T_E - 16, 24, c)) if not isinstance(c, int) else \
                (At(S_E - 4 + 12 * c), At(T_E - 16 + 24 * c))
            body = MLP_BODY
        else:
            s, t = (At(S_E), At(T_E)) if c == 0 else (At(S_E - 4 + 12 * NC), At(T_E - 16 + 24 * NC))
            body = [e for e in MLP_BODY if (e[0] == "down") == (c == NC)]
        plan = []
        for kind, f in body:
            plan.append((kind, f, s, t))
            s, t = s + 1, t + (4 if kind == "down" else 1)
        return plan

    def d2_before(n, n2):
        return At(T_D2 + 2 * (n - 1) , 4, n2) if not isinstance(n2, int) else At(T_D2 + 2 * (n - 1) + 4 * n2)

    block = ctx.enter_context(nc.Block())

    @block.sync
    def _(sp):
        def load(s, dst, src):
            if s.reg is not None or s.const >= 2:
                sp.wait_ge(sem("l_split"), (s - 1).v)
            sp.dma_start(dst, src).then_inc(sem(f"w_in{s.odd}"), 16)

        def raw_at(s, k, n):
            return raw[:, s.odd, 0:k * n].rearrange("p (k n) -> p k n", k=k)

        sp.dma_start(xtok_s[0:NS, :], x_sample[:, 0, :]).then_inc(sem("x_in4"), 16)
        sp.dma_start(xtok_s[M0:R0, :], meta_tokens).then_inc(sem("x_in4"), 16)
        for c in range(NB):
            sp.dma_start(xtok[:, c, :], x_prompt[0, P * c:P * c + P, :]).then_inc(sem(f"x_in{c}"), 16)
        for i in range(4):
            load(At(i), raw_at(At(i), KD, P), w_in3[:, :, W_COLS["qi"] + P * i:W_COLS["qi"] + P * i + P])
        load(At(4), raw_at(At(4), KD, 72), w_in3[:, :, W_COLS["wk"]:W_COLS["wk"] + 72])

        def head_loads(h4, reg):
            for j in range(4):
                c = W_COLS[HG[j]]
                src = w_in3[:, :, c:c + P] if reg is None else w_in3[:, :, bass.ds(reg * P + c, P)]
                load(h4 + S_C + j, raw_at(h4 + S_C + j, KD, P), src)

        head_loads(At(0), None)
        with sp.Fori(1, NH, 1) as h:
            head_loads(At(0, 4, h), h)
        for g in range(NG):
            for j, c in enumerate((W_COLS["k"] + P * g, W_COLS["v"] + P * g, 2 * P * g, 2 * P * g + P)):
                s = At(S_B + 4 * g + j)
                load(s, raw_at(s, KD, P), w_in3[:, :, c:c + P])
        for n in range(8):
            s = At(S_D1 + n)
            c = (n * 256 + 1024) % D
            load(s, raw_at(s, 8, 256), wo3[:, 8:16, c:c + 256])
        with sp.Fori(0, 4, 1) as n2:
            for i in range(2):
                s = At(S_D2 + i, 2, n2)
                load(s, raw_at(s, 8, 256), wo3[:, 0:8, bass.ds(n2 * 512 + 256 * i, 256)])
        wg3, wu3 = (w[0].rearrange("(k p) n -> p k n", p=P) for w in (w_gate, w_up))
        def mlp_loads(c):
            for kind, n, s, t in mlp_plan(c):
                if kind == "down":
                    rows = w_down[0, (c - 1) * FC * P:c * FC * P, :] if isinstance(c, int) else \
                        w_down[0, bass.ds(c * (FC * P) - FC * P, FC * P), :]
                    load(s, raw_at(s, FC, 512), rows.rearrange("(k p) n -> p k n", p=P)[:, :, n * 512:n * 512 + 512])
                else:
                    w = wg3 if kind == "gate" else wu3
                    at_ = c * (FC * P) + n * P
                    load(s, raw_at(s, KD, P), w[:, :, at_:at_ + P] if isinstance(c, int) else w[:, :, bass.ds(at_, P)])

        mlp_loads(0)
        with sp.Fori(1, NC, 1) as c:
            mlp_loads(c)
        mlp_loads(NC)
        for q in range(4):
            for u in (5 * q + 3, 5 * q + 4):
                name, n = y_copied(u)
                sp.wait_ge(sem(name), n)
            sp.dma_start(y_prompt[0, :, 512 * q:512 * q + 512].rearrange("(c p) d -> p c d", p=P),
                         ytok[:, 0:NB, 512 * q:512 * q + 512]).then_inc(sem("y_out"), 16)
            sp.dma_start(y_sample[:, 0, 512 * q:512 * q + 512], ytok[0:NS, NB, 512 * q:512 * q + 512])\
                .then_inc(sem("y_out"), 16)
        sp.wait_ge(sem("y_out"), 128)

    @block.gpsimd
    def _(pool):
        ch = Chain(pool, sem("pool_step"))

        def mask(ap, value, **kw):
            ch(pool.affine_select(out=ap, in_=ap, fill=value, **kw))

        for name in ("ho_done", "mixed", "state_left"):
            pool.sem_inc(sem(name), 1)
        for r, src in ((0, ln_in_g), (16, ln_in_b), (32, ln1_g[0]), (48, ln1_b[0])):
            pool.dma_start(vrows[r:r + 16, :], src.rearrange("(k p) -> k p", p=P)).then_inc(sem("vec_in"), 16)
        pool.dma_start(vrows[64:80, :], hg_lb_logits.rearrange("l (h p) -> (l h) p", p=P)).then_inc(sem("vec_in"), 16)
        pool.dma_start(vrows[80:81, :], hg_norm_g).then_inc(sem("vec_in"), 16)
        for r, src in ((81, ln2_g[0]), (97, ln2_b[0])):
            pool.dma_start(vrows[r:r + 16, :], src.rearrange("(k p) -> k p", p=P)).then_inc(sem("vec_in"), 16)
        pool.dma_start(pt_i[:, 0, :], page_table.rearrange("b p -> p b"), allow_slow_non_contiguous=True).then_inc(sem("pt_in"), 16)
        pool.dma_start(pt_i[:, 1, :], page_table).then_inc(sem("pt_in"), 16)
        ch(pool.memset(ones[:], 1.0))
        ch(pool.memset(ident[:], 0.0))
        mask(ident[:], 1.0, compare_op=ALU.not_equal, base=0, pattern=[[-1, P]], channel_multiplier=1)
        ch(pool.memset(tri[:], 1.0))
        mask(tri[:], 0.0, compare_op=ALU.is_ge, base=0, pattern=[[1, P]], channel_multiplier=-1)
        ch(pool.memset(causal[:], 0.0))
        mask(causal[:], INADMISSIBLE, compare_op=ALU.is_ge, base=0, pattern=[[-1, P]], channel_multiplier=1)
        ch(pool.iota(dist[:], pattern=[[-1, 528]], base=400, channel_multiplier=1,
                     allow_small_or_imprecise_dtypes=True))
        ch(pool.memset(halfsel[:], 1.0))
        mask(halfsel[:, 0:1], 0.0, compare_op=ALU.is_ge, base=63, pattern=[[0, 1]], channel_multiplier=-1)
        mask(halfsel[:, 1:2], 0.0, compare_op=ALU.is_ge, base=-64, pattern=[[0, 1]], channel_multiplier=1)
        ch(pool.memset(pageof[:], 16.0))
        mask(pageof[:], 0.0, compare_op=ALU.is_ge, base=0, pattern=[[1, P]], channel_multiplier=-16)
        mask(pageof[:], 0.0, compare_op=ALU.is_ge, base=15, pattern=[[-1, P]], channel_multiplier=16)
        ch(pool.iota(pmod[:].bitcast(I32), pattern=[[0, 8]], base=0, channel_multiplier=1))
        for h in range(NH):
            ch(pool.memset(slope8[:, h:h + 1], -(2.0 ** -(h + 1))))
        ch(pool.memset(zt[:], 0.0))
        ch(pool.memset(zt[:, NS - 1:NS], 1.0))
        pool.sem_inc(sem("consts"), 1)

        kidx_rows = cache_kidx[0].rearrange("n (j r) d -> (n j) (r d)", r=8)
        pool.wait_ge(sem("krow_ready"), 1)
        pool.wait_ge(sem("x_turned"), KD)
        for b in range(NS):
            if b >= 2:
                pool.wait_ge(sem("kx_turned"), b - 1)
            pool.indirect_dma_start(kx[:, b % 2, :], None, kidx_rows,
                                    bass.IndirectOffsetOnAxis(ap=krow[:, b:b + 1], axis=0)).then_inc(sem(f"kx_in{b % 2}"), 16)
        pool.wait_ge(sem("wk_ready"), 1)
        ki_rows = kidx_prompt[0, 0]
        pool.dma_start(ki_rows[NM:NM + NR, :].rearrange("(c p) d -> p c d", p=P), wk[:, 0:4, 8:72]).then_inc(sem("out_ki"), 16)
        pool.dma_start(ki_rows[0:NM, :], wk[0:NM, 4, 8:72]).then_inc(sem("out_ki"), 16)
        pool.dma_start(kidx_sample[0, :, 0, :], wk[0:NS, 5, 8:72]).then_inc(sem("out_ki"), 16)

        state_in = state_hgrn[0].rearrange("b h d v -> h d b v")
        state_out = hgrn_sample[0].rearrange("b h d v -> h d b v")

        def load_state(h):
            pool.dma_start(ss[:], state_in[h] if isinstance(h, int) else state_in[bass.ds(h, 1)].rearrange("o d b v -> (o d) b v")
                           ).then_inc(sem("state_in"), 16)

        def store_states(h, n):
            wait_apart(pool, sem("sstate_ready"), n + 1, sem("seen"))
            dst = state_out[h] if isinstance(h, int) else state_out[bass.ds(h, 1)].rearrange("o d b v -> (o d) b v")
            pool.dma_start(dst, ss[:]).then_inc(sem("sstate_out"), 16)
            wait_apart(pool, sem("st_ready"), n + 1, sem("seen"))
            dst = hgrn_prompt[0, 0, h] if isinstance(h, int) else hgrn_prompt[0, 0, bass.ds(h, 1)].rearrange("o d v -> (o d) v")
            pool.dma_start(dst, st[:, NB, :]).then_inc(sem("state_out"), 16)

        def decays(n):
            pt = nc.gpsimd.tensor_tensor
            pool.wait_ge(sem("kf_ready"), n + 1)
            pool.wait_ge(sem("et_exp"), n + 1)
            off = 0
            kr = kf[:, R0:NT].rearrange("p (c x) -> p c x", c=NB)
            for i in range(4):
                w = SUB * (i + 1)
                v = et[:, off:off + NB * w].rearrange("p (c x) -> p c x", c=NB)
                pt(v, v, kr[:, :, 0:w], ALU.mult)
                off += NB * w
            pt(et[:, off:off + NM], et[:, off:off + NM], kf[:, M0:R0], ALU.mult)
            pool.wait_ge(sem("ke_exp"), n + 1)
            pt(ke[:, M0:NT], ke[:, M0:NT], kf[:, M0:NT], ALU.mult)
            pool.wait_ge(sem("q_ready"), n + 1)
            pool.wait_ge(sem("qe_exp"), n + 1)
            pt(qe[:, M0:NT], qe[:, M0:NT], hq[:, M0:NT], ALU.mult).then_inc(sem("decayed"), 1)

        pool.wait_ge(sem("sidx_scores"), NS)
        load_state(0)
        decays(0)
        with pool.Fori(1, NH, 1) as h:
            store_states(h - 1, h - 1)
            pool.wait_ge(sem("ho_done"), h + 1)
            pool.wait_ge(sem("state_out"), h * 16)
            pool.sem_inc(sem("state_left"), 1)
            wait_apart(pool, sem("sstate_out"), h * 16, sem("seen"))
            load_state(h)
            decays(h)
        store_states(NH - 1, NH - 1)

        def store_rows(g, src, to_prompt, to_sample, name):
            rows = to_prompt[0, 0, :, g, :]
            pool.dma_start(rows[NM:NM + NR, :].rearrange("(c p) d -> p c d", p=P), src[:, 0:4, :]).then_inc(sem(name), 16)
            pool.dma_start(rows[0:NM, :], src[0:NM, 4, :]).then_inc(sem(name), 16)
            pool.dma_start(to_sample[0, :, 0, g, :], src[0:NS, 5, :]).then_inc(sem(name), 16)

        for g in range(NG):
            pool.wait_ge(sem("kv_tok"), 4 * g + 2)
            store_rows(g, ktok, k_prompt, k_sample, "k_out")
            pool.wait_ge(sem("kv_tok"), 4 * g + 4)
            store_rows(g, vtok[g % 2], v_prompt, v_sample, "v_out")
        pool.wait_ge(sem("resid_lo"), 8)
        pool.wait_ge(sem("grow_ready"), 1)
        for b in range(NS):
            for name, dst, src, used in (("gk", kgs, cache_k, "sg_turned"), ("gv", vgs, cache_v, "so_done")):
                if b >= 2:
                    pool.wait_ge(sem(used), b - 1)
                for blk in range(NBLK):
                    pool.indirect_dma_start(dst[:, b % 2, blk, :], None, src[0].rearrange("n s k d -> (n s) (k d)"),
                                            bass.IndirectOffsetOnAxis(ap=grow[:, blk, b:b + 1], axis=0))\
                        .then_inc(sem(f"{name}{b % 2}"), 16)
        for n, taken in ((0, "x1_h"), (1, "y_ready")):
            pool.wait_ge(sem("mu_ready"), n + 1)
            for k in range(KD):
                if n == 1 and k % 4 == 3:
                    continue
                if k >= 4:
                    pool.wait_ge(sem(taken), k - 3)
                nc.gpsimd.tensor_tensor(lnd[:, k % 4, :], sacc[:, k, :], mu[:, :], ALU.subtract).then_inc(sem("centered"), 1)
        pool.wait_ge(sem("k_out"), 48 * NG)
        pool.wait_ge(sem("v_out"), 48 * NG)
        pool.wait_ge(sem("sstate_out"), 16 * NH)
        pool.wait_ge(sem("state_out"), 16 * NH)
        pool.wait_ge(sem("out_ki"), 48)

    @block.scalar
    def _(act):
        nc.scalar.preload_act_table_set("natural_log_exp_and_others")
        ch = Chain(act, sem("act_step"))

        def split(s, used=None):
            act.wait_ge(sem(f"w_in{s.odd}"), (s.half() + 1).times(16).v)
            if used is None and (s.reg is not None or s.const >= 2):
                used = mts(s - 2)
            if used is not None:
                act.wait_ge(sem("mm"), used.v)
            act.activation(wh[:, s.odd, :], raw[:, s.odd, :], ACT.Copy).then_inc(sem("h_split"), 1)

        def split_wk(s):
            act.wait_ge(sem(f"w_in{s.odd}"), (s.half() + 1).times(16).v)
            act.wait_ge(sem("mm"), mts(s - 2).v)
            act.activation(wh[:, s.odd, 0:KD * 72], raw[:, s.odd, 0:KD * 72], ACT.Copy).then_inc(sem("h_split"), 1)

        def sigmoid_tail(u):
            act.wait_ge(sem("sig_capped"), u + 1)
            act.activation(t1[:, :], t1[:, :], ACT.Ln, bias=1.0).then_inc(sem("sig_ln"), 1)
            act.wait_ge(sem("sig_ln"), u + 1)
            act.activation(t1[:, :], t1[:, :], ACT.Exp, scale=-1.0).then_inc(sem("sigmoid"), 1)

        for q, c in enumerate((NB, 0, 1, 2, 3)):
            n, src = (R0, xtok_s) if c == NB else (P, xtok[:, c, :])
            act.wait_ge(sem("var"), q + 1)
            m_, r_ = mv[0:n, c, 0:1], mv[0:n, c, 1:2]
            act.activation(mv[0:n, c, 2:3], m_, ACT.Copy, scale=-1.0)
            ch(act.activation(r_, r_, ACT.Ln, bias=LN_EPS))
            ch(act.activation(r_, r_, ACT.Exp, scale=-0.5))
            ch(act.activation(mv[0:n, c, 3:4], mv[0:n, c, 2:3], ACT.Identity, scale=r_))
            act.activation(src[0:n, :], src[0:n, :], ACT.Identity, scale=r_, bias=mv[0:n, c, 3:4])\
               .then_inc(sem("x_norm"), 1)
        act.wait_ge(sem("vec_turned"), 1)
        act.activation(vec[:], b4[:, 0:113], ACT.Copy).then_inc(sem("vec_ready"), 1)
        act.wait_ge(sem("lb_shifted"), 1)
        act.activation(lb[:, 0:16], lb[:, 0:16], ACT.Exp).then_inc(sem("lb_exp"), 1)
        split(At(0))
        split(At(1))
        for k in range(KD):
            if k % 2:
                act.wait_ge(sem("x_turned"), k + 1)
                if k >= 2:
                    act.wait_ge(sem("xl_ready"), k - 1)
                g, b = vec[:, k:k + 1], vec[:, 16 + k:17 + k]
                act.activation(lnt[:, 1, R0:NT], b6[:, :], ACT.Identity, scale=g, bias=b)
                act.activation(lnt[:, 1, 0:R0], b7[:, 0:R0], ACT.Identity, scale=g, bias=b).then_inc(sem("x_lin1"), 1)
                act.wait_ge(sem("x_lin1"), k // 2 + 1)
            else:
                act.wait_ge(sem("x_lin0"), k // 2 + 1)
            act.activation(xh[:, k, :], lnt[:, k % 2, :], ACT.Copy).then_inc(sem("xh_ready"), 1)

        def kx_take(b):
            act.wait_ge(sem("kx_turned"), b + 1)
            act.activation(kxT[:, b, :], (b4, b5)[b % 2][:, :], ACT.Copy).then_inc(sem("kxT_ready"), 1)

        act.wait_ge(sem("x_turned"), KD)
        split(At(2))
        act.wait_ge(sem("mm"), 1)
        act.activation(cut(qiT[:, 0, :]), whole(At(0)), ACT.Copy).then_inc(sem("acc_read0"), 1)
        for i in range(1, 4):
            if i >= 2:
                for b in range(3 * i - 6, 3 * i - 3):
                    kx_take(b)
            split(At(i + 2)) if i != 2 else split_wk(At(4))
            act.wait_ge(sem("mm"), i + 1)
            act.activation(cut(qiT[:, i, :]), whole(At(i)), ACT.Copy).then_inc(sem(f"acc_read{i % 2}"), 1)
        kx_take(6)
        kx_take(7)
        act.wait_ge(sem("mm"), 5)
        ch(act.activation(cut(wikiT[:, :]), acc[0:72, 0, :, 0:HALF], ACT.Copy))
        act.sem_inc(sem("acc_read0"), 1)
        act.sem_inc(sem("wiki_ready"), 1)

        def idx_setup():
            act.wait_ge(sem("idx_turned"), 1)
            for lo in (0, 72):
                n = 72 if lo == 0 else 64
                f = 0 if lo == 0 else 8
                src = b4[:, 0:288].rearrange("p (c f) -> p c f", c=4)
                act.activation(wk[:, 0:4, lo:lo + n], src[:, :, f:72], ACT.Copy).then_inc(sem("act_step"), 1)
                act.activation(wk[0:NM, 4, lo:lo + n], b5[0:NM, f:72], ACT.Copy).then_inc(sem("act_step"), 1)
                act.activation(wk[0:NS, 5, lo:lo + n], b5[0:NS, 72 + f:144], ACT.Copy).then_inc(sem("act_step"), 1)
            ch.n += 6
            act.wait_ge(sem("act_step"), ch.n)
            act.sem_inc(sem("wk_ready"), 1)
            act.wait_ge(sem("idx_turned"), 2)
            act.activation(kiT[:, R0:NT], b6[:, :], ACT.Copy).then_inc(sem("act_step"), 1)
            act.activation(kiT[:, 0:R0], b7[:, 0:R0], ACT.Copy).then_inc(sem("act_step"), 1)
            act.wait_ge(sem("qS_clear"), 1)
            q4 = qiT[:, :, 0:NS].rearrange("p m b -> p b m")
            for dst in (0, 64):
                for src in (0, 64):
                    out = qS[dst:dst + 64, :, dst // 64, :].rearrange("p b (m e) -> p b m e", e=2)[:, :, :, src // 64]
                    act.activation(out, q4[src:src + 64], ACT.Copy).then_inc(sem("act_step"), 1)
            ch.n += 6
            act.wait_ge(sem("act_step"), ch.n)
            act.sem_inc(sem("ki_ready"), 1)

        def idx_relu(i, m):
            n = 4 * i + m
            act.wait_ge(sem("idx_scores"), n + 1)
            if n >= 1:
                act.wait_ge(sem("idx_summed"), n)
            w = P * (i + 1)
            for e, (real, meta) in enumerate(((b4, b6), (b5, b7))):
                act.activation(rel[:, e, NM:NM + w], real[:, 0:w], ACT.Relu, scale=IDX_SCALE)
                act.activation(rel[:, e, 0:NM], meta[:, 0:NM], ACT.Relu, scale=IDX_SCALE)\
                   .then_inc(sem("idx_relu"), 1)

        def idx_sample_relu():
            act.wait_ge(sem("sidx_scores"), NS)
            act.activation(rsc[:, :], b6[:, :], ACT.Relu, scale=IDX_SCALE).then_inc(sem("sidx_relu"), 1)
            act.wait_ge(sem("wbc_sum"), 1)
            act.activation(nsc[:], b5[0:NS, 0:NH], ACT.Relu, scale=IDX_SCALE).then_inc(sem("nsc_relu"), 1)

        def t_of(h4, j):
            return h4 + (S_C + j)

        def forget(h4, n):
            t = t_of(h4, 0)
            act.wait_ge(sem("mm"), (t + 1).v)
            act.wait_ge(sem("gate_ready"), n)
            act.activation(cut(t1[:, :]), whole(t), ACT.Exp, scale=-1.0).then_inc(sem("sig_exp"), 1)
            sigmoid_tail(3 * n)
            act.wait_ge(sem("sigmoid"), 3 * n + 1)
            if not isinstance(n, int):
                act.wait_ge(sem("mixed"), n)
            act.activation(t2[:, :], t1[:, :], ACT.Ln, scale=lbcol(h4, n, 1), bias=lbcol(h4, n, 0))\
               .then_inc(sem("logf"), 1)

        def lbcol(h4, n, which):
            return lb[:, 8 * which + n:8 * which + n + 1] if isinstance(n, int) else lb[:, bass.ds(n + 8 * which, 1)]

        def query(h4, n):
            t = t_of(h4, 1)
            act.wait_ge(sem("mm"), (t + 1).v)
            act.wait_ge(sem("kf_ready"), n + 1)
            act.activation(cut(t1[:, :]), whole(t), ACT.Exp, scale=-1.0).then_inc(sem("sig_exp"), 1)
            sigmoid_tail(3 * n + 1)

        def decays(h4, n):
            act.wait_ge(sem("b_ready"), n + 1)
            act.wait_ge(sem("intra_done"), n)
            off = 0
            for i in range(4):
                w = SUB * (i + 1)
                for c in range(NB):
                    lo = R0 + P * c
                    mid_ = lo + SUB * i + SUB // 2 - 1
                    act.activation(et[:, off + c * w:off + c * w + w], bcum[:, lo:lo + w], ACT.Exp, scale=-1.0,
                                   bias=bcum[:, mid_:mid_ + 1])
                off += NB * w
            act.activation(et[:, off:off + NM], bcum[:, M0:R0], ACT.Exp, scale=-1.0,
                           bias=bcum[:, M0 + 7:M0 + 8]).then_inc(sem("et_exp"), 1)
            for c in range(NB):
                lo = R0 + P * c
                act.activation(ke[:, lo:lo + P], bcum[:, lo:lo + P], ACT.Exp, scale=-1.0, bias=bcum[:, lo + P - 1:lo + P])
            act.activation(ke[:, M0:R0], bcum[:, M0:R0], ACT.Exp, scale=-1.0, bias=bcum[:, R0 - 1:R0])\
               .then_inc(sem("ke_exp"), 1)
            act.wait_ge(sem("ho_done"), n + 1)
            act.activation(qe[:, :], bcum[:, :], ACT.Exp).then_inc(sem("qe_exp"), 1)
            act.wait_ge(sem("st_ready"), n)
            act.activation(eb[:, :], bcum[:, R0 + P - 1:NT:P], ACT.Exp)
            act.wait_ge(sem("sstate_ready"), n)
            act.activation(fs[:, :], bcum[:, 0:NS], ACT.Exp).then_inc(sem("ends_exp"), 1)
            act.wait_ge(sem("qd_arg"), n + 1)
            act.activation(qd[:, M0:NT], qd[:, M0:NT], ACT.Exp).then_inc(sem("qd_exp"), 1)

        def inputs(h4, n):
            t = t_of(h4, 2)
            act.wait_ge(sem("mm"), (t + 1).v)
            act.wait_ge(sem("head_turned"), n)
            act.activation(cut(hiT[:, :]), whole(t), ACT.Copy).then_inc(sem("hi_ready"), 1)
            act.wait_ge(sem("hi_ready"), n + 1)
            act.sem_inc(sem(f"acc_read{t.odd}"), 1)

        def turned(h4, n):
            act.wait_ge(sem("head_turned"), n + 1)
            act.wait_ge(sem("ho_done"), n + 1)
            act.activation(itok[:, 0:4, :], b4[:, :].rearrange("p (c v) -> p c v", c=4), ACT.Copy)
            act.activation(ketok[:, 0:4, :], b6[:, :].rearrange("p (c v) -> p c v", c=4), ACT.Copy)
            act.activation(itok[0:NM, 4, :], b5[0:NM, 0:P], ACT.Copy)
            act.activation(itok[0:NS, 5, :], b5[0:NS, P:2 * P], ACT.Copy)
            act.activation(ketok[0:NM, 4, :], b5[0:NM, 2 * P:3 * P], ACT.Copy).then_inc(sem("tok_ready"), 1)

        def gating(h4, n):
            t = t_of(h4, 3)
            act.wait_ge(sem("mm"), (t + 1).v)
            act.wait_ge(sem("q_ready"), n + 1)
            act.activation(cut(t1[:, :]), whole(t), ACT.Exp, scale=-1.0).then_inc(sem("sig_exp"), 1)
            sigmoid_tail(3 * n + 2)

        def squares(n):
            act.wait_ge(sem("ho_done"), n + 2)
            if not isinstance(n, int):
                act.wait_ge(sem("b_ready"), n + 2)
            act.activation(t2[:, R0:NT], b4[:, :], ACT.Square)
            act.activation(t2[:, 0:R0], b5[:, 0:R0], ACT.Square).then_inc(sem("squared"), 1)

        def norm_scale(n):
            act.wait_ge(sem("norm_sum"), n + 1)
            act.activation(t2[:, R0:NT], b6[:, :], ACT.Ln, scale=1.0 / P, bias=NORM_EPS)
            act.activation(t2[:, 0:R0], b7[:, 0:R0], ACT.Ln, scale=1.0 / P, bias=NORM_EPS).then_inc(sem("norm_ln"), 1)
            act.wait_ge(sem("norm_ln"), n + 1)
            act.activation(t2[:, :], t2[:, :], ACT.Exp, scale=-0.5).then_inc(sem("norm_scale"), 1)

        def early(h4, n, j):
            if j == 1:
                forget(h4, n)
            if j == 2:
                query(h4, n)
                decays(h4, n)
            if j == 3:
                inputs(h4, n)

        def late(h4, n, j):
            if j == 0:
                turned(h4, n)
                gating(h4, n)
            if j == 2:
                squares(n)
            if j == 3:
                norm_scale(n)

        idx_setup()
        for j in range(4):
            split(At(S_C + j + 1))
            early(At(0), 0, j)
            if j == 0:
                idx_sample_relu()
            for i in IDX_BLOCKS[j]:
                for m in range(4):
                    idx_relu(i, m)
        with act.Fori(1, NH, 1) as h:
            for j in range(4):
                split(At(S_C + j + 1, 4, h))
                late(At(-4, 4, h), h - 1, j)
                early(At(0, 4, h), h, j)
        def take(g, j):
            t = At(S_B + 4 * g + j)
            act.wait_ge(sem("mm"), (t + 1).v)
            src = whole(t)
            dst = (kT[g % 2][:, :], vT[:, :], qT[g % 2][:, 0, :], qT[g % 2][:, 1, :])[j]
            if j == 0:
                ch(act.activation(knew[:, g, :], src[:, 0, 0:NS], ACT.Copy))
            if j >= 2:
                if j == 2 and g == 0:
                    act.wait_ge(sem("qpad_clear"), 1)
                ch(act.activation(qpad[:, g, :, 2 * g + j - 2], src[:, 0, 0:NS], ACT.Copy, scale=ATTN_SCALE))
            ch(act.activation(cut(dst), src, ACT.Copy))
            act.sem_inc(sem(f"acc_read{t.odd}"), 1)
            act.sem_inc(sem("qkv_in"), 1)

        def kv_rows(g, j):
            dst = ktok if j == 0 else vtok[g % 2]
            act.wait_ge(sem("kv_turned"), 4 * g + 2 * j + 1)
            if j == 0 and g >= 1:
                act.wait_ge(sem("k_out"), 48 * g)
            if j == 1 and g >= 2:
                act.wait_ge(sem("v_out"), 48 * (g - 1))
            act.activation(dst[:, 0:4, :], b7[:, :].rearrange("p (c d) -> p c d", c=4), ACT.Copy).then_inc(sem("kv_tok"), 1)
            act.wait_ge(sem("kv_turned"), 4 * g + 2 * j + 2)
            act.activation(dst[0:NM, 4, :], b7[0:NM, 0:P], ACT.Copy)
            act.activation(dst[0:NS, 5, :], b7[0:NS, P:2 * P], ACT.Copy).then_inc(sem("kv_tok"), 1)

        def att_exp(n):
            i = n % NB
            act.wait_ge(sem("att_max"), n + 1)
            for hd in range(2):
                last = act.activation(lg[:, hd, 0:WIDE[i]], lg[:, hd, 0:WIDE[i]], ACT.Exp, bias=nmx[:, 0, hd:hd + 1],
                                      accum_out=nmx[:, 1, hd:hd + 1])
                if i == 0:
                    last = act.activation(lgm[:, hd, :], lgm[:, hd, :], ACT.Exp, bias=nmxm[:, 0, hd:hd + 1],
                                   accum_out=nmxm[:, 1, hd:hd + 1])
            last.then_inc(sem("att_exp"), 1)

        def att_probs(n):
            i = n % NB
            act.wait_ge(sem("p_turned"), n + 1)
            w = P * (i + 1)
            act.activation(pT[:, 0, 0:w], b4[:, 0:w], ACT.Copy)
            act.activation(pT[:, 1, 0:w], b5[:, 0:w], ACT.Copy)
            m = 2 * P + (2 * NM if i == 0 else 0)
            act.activation(pTm[:, 0:m], b6[0:NM, 0:m], ACT.Copy).then_inc(sem("pT_out"), 1)

        def att_take(n):
            g, i = n // NB, n % NB
            act.wait_ge(sem("pv_done"), n + 1)
            if i == 0:
                ch(act.activation(attn_o[:, 2 * g:2 * g + 2, M0:R0],
                                  b7[:, 2 * P:2 * P + 2 * NM].rearrange("p (h q) -> p h q", h=2), ACT.Copy))
            act.activation(attn_o[:, 2 * g:2 * g + 2, R0 + P * i:R0 + P * i + P],
                           b7[:, 0:2 * P].rearrange("p (h q) -> p h q", h=2), ACT.Copy).then_inc(sem("pv_out"), 1)

        def keep_new(g):
            act.activation(vnew[:, g, :], vtok[g % 2][0:NS, 5, :], ACT.Copy).then_inc(sem("vnew_in"), 1)

        for g in range(NG):
            for j in range(4):
                split(At(S_B + 4 * g + j + 1))
                if j >= 1:
                    take(g, j - 1)
                elif g >= 1:
                    take(g - 1, 3)
                if g == 0:
                    if j != 2:
                        late(At(4 * NH - 4), NH - 1, j)
                    if j == 2:
                        kv_rows(0, 0)
                        squares(NH - 1)
                    if j == 3:
                        kv_rows(0, 1)
                else:
                    n = 4 * (g - 1) + j
                    if n >= 1:
                        att_take(n - 1)
                    att_exp(n)
                    if j == 0:
                        keep_new(g - 1)
                    if j in (1, 2):
                        kv_rows(g, j - 1)
                    att_probs(n)

        def mix_round(k):
            act.wait_ge(sem("x_sum"), k + 1)
            act.activation(xh[:, 8 + k, :], sacc[:, 8 + k, :], ACT.Copy).then_inc(sem("mix_h"), 1)

        def mix_resid(k):
            act.wait_ge(sem("mix_in"), k + 1)
            act.activation(sacc[:, 8 + k, :], tmp[:, k % 2, :], ACT.Copy, scale=ALPHA).then_inc(sem("resid"), 1)

        def sample_att(b):
            act.wait_ge(sem("sg_turned"), b + 1)
            act.wait_ge(sem("slog"), b)
            act.activation(kgT[:, 0], b4[:, :].rearrange("p (g k) -> p g k", g=NG), ACT.Copy)
            act.activation(kgT[:, 1], b5[:, :].rearrange("p (g k) -> p g k", g=NG), ACT.Copy).then_inc(sem("sgT"), 1)
            act.wait_ge(sem("smax"), b + 1)
            act.activation(ps[:, :], b6[0:NH, 0:KEEP_S + 1], ACT.Exp, bias=snm[:, 0:1], accum_out=snm[:, 1:2])\
               .then_inc(sem("sexp"), 1)
            act.wait_ge(sem("sp_turned"), b + 1)
            act.activation(pTs[:, 0:16], b7[:, 0:16], ACT.Copy)
            act.activation(pTs[0:NS, 16:24], b7[0:NS, 16:24], ACT.Copy).then_inc(sem("spT"), 1)
            act.wait_ge(sem("so_done"), b + 1)
            act.activation(attn_o[:, :, b], b7[:, 32:32 + NH], ACT.Copy).then_inc(sem("so_out"), 1)

        for n in range(8):
            if n == 0:
                act.wait_ge(sem("mm"), T_D1)
                mix_round(0)
                for k in range(1, 9):
                    if k < 8:
                        mix_round(k)
                    mix_resid(k - 1)
                    if k == 3:
                        take(3, 3)
            split(At(S_D1 + n + 1))
            if n <= 4:
                att_take(11 + n)
            if n == 1:
                act.wait_ge(sem("k_out"), 48 * NG)
                act.wait_ge(sem("v_out"), 48 * NG)
                for k in range(8):
                    act.activation(sacc[:, k, :], fr(xh[:, k, :]), ACT.Copy, scale=ALPHA).then_inc(sem("resid_h"), 1)
            if n < 4:
                att_exp(12 + n)
                if n == 0:
                    keep_new(3)
                att_probs(12 + n)
            else:
                sample_att(2 * (n - 4))
                sample_att(2 * (n - 4) + 1)

        def stat_square(m):
            k = m.const % KD
            act.wait_ge(sem("s_done"), (m + 1).v)
            if m.reg is not None or m.const >= 2:
                act.wait_ge(sem("q_sum"), (m - 1).v)
            src = sacc[:, k, :] if m.reg is None else sacc[:, bass.ds(m.v, 1), :].rearrange("p o n -> p (o n)")
            act.activation(sq[:, k % 2, :], src, ACT.Square).then_inc(sem("sq_done"), 1)

        act.wait_ge(sem("so_out"), NS)
        for k in range(NH):
            act.activation(xh[:, k, :], attn_o[:, k, :], ACT.Copy).then_inc(sem("att_h"), 1)

        def d2(n2):
            for i in range(2):
                s = At(S_D2 + i + 1, 2, n2) if not isinstance(n2, int) else At(S_D2 + i + 1 + 2 * n2)
                split(s, d2_before(i + 1, n2))
                for e in range(2):
                    stat_square(At(2 * i + e, 4, n2) if not isinstance(n2, int) else At(2 * i + e + 4 * n2))

        d2(0)
        with act.Fori(1, 4, 1) as n2:
            d2(n2)

        def scale_of(n):
            act.wait_ge(sem("ln_var"), n)
            ch(act.activation(rstd[:, :], rstd[:, :], ACT.Ln, bias=LN_EPS))
            act.activation(rstd[:, :], rstd[:, :], ACT.Exp, scale=-0.5).then_inc(sem("ln_rstd"), 1)

        split(At(S_E + 1), At(T_E))
        scale_of(1)
        for k in range(KD):
            act.wait_ge(sem("ln_norm"), k + 1)
            ch(act.activation(sacc[:, k, :], lnd[:, k % 4, :], ACT.Identity, scale=vec[:, 32 + k:33 + k],
                              bias=vec[:, 48 + k:49 + k]))
            act.activation(xh[:, k, :], sacc[:, k, :], ACT.Copy).then_inc(sem("x1_h"), 1)
        nc.scalar.preload_act_table_set("silu_and_others")

        def gate(u, t):
            act.wait_ge(sem("mm"), (t + 1).v)
            if u.reg is not None or u.const >= 2:
                act.wait_ge(sem("gated"), (u - 1).v)
            act.activation(cut(gbuf[:, u.const % 2, :]), whole(t), ACT.Silu).then_inc(sem("gate_done"), 1)
            act.wait_ge(sem("gate_done"), (u + 1).v)
            act.sem_inc(sem(f"acc_read{t.odd}"), 1)

        def hidden(u):
            act.wait_ge(sem("gated"), (u + 1).v)
            act.activation(hh[:, u.const % FC, :], hbuf[:, u.const % 2, :], ACT.Copy).then_inc(sem("hh_done"), 1)

        def mlp(c):
            u0 = At(FC * c) if isinstance(c, int) else At(0, FC, c)
            for p_, (kind, f, s, t) in enumerate(mlp_plan(c)):
                if p_ == 0 and isinstance(c, int) and c == NC:
                    hidden(u0 - 1)
                if not (p_ == 0 and isinstance(c, int) and c == 0) and not (kind == "down" and f == 3 and isinstance(c, int)):
                    split(s + 1, t)
                if p_ == 0 and not isinstance(c, int):
                    hidden(u0 - 1)
                if kind == "up" and f >= 1 or kind == "down" and f == 0 and not (isinstance(c, int) and c == NC):
                    gate(u0 + (f if kind == "up" else 0), t - 1)
                if kind == "up" and f == 0 and isinstance(c, int) and c == 0:
                    gate(u0, t - 1)
                if kind == "gate" and f >= 1:
                    hidden(u0 + (f - 1))
                if isinstance(c, int) and c == 0 and 2 <= p_ < 6:
                    if p_ == 2:
                        act.wait_ge(sem("x1_in"), KD)
                    for k in range(4 * p_ - 8, 4 * p_ - 4):
                        act.activation(sacc[:, k, :], sacc[:, k, :], ACT.Copy, scale=ALPHA).then_inc(sem("x1_resid"), 1)
                if kind == "down" and isinstance(c, int) and c == NC:
                    for i in range(4):
                        stat_square(At(16 + 4 * f + i))

        mlp(0)
        with act.Fori(1, NC, 1) as c:
            mlp(c)
        mlp(NC)
        nc.scalar.preload_act_table_set("natural_log_exp_and_others")
        scale_of(2)
        for k in range(KD + 4):
            if k < KD:
                act.wait_ge(sem("ln_norm"), KD + k + 1)
                act.activation(sacc[:, k, :], lnd[:, k % 4, :], ACT.Identity, scale=vec[:, 81 + k:82 + k],
                               bias=vec[:, 97 + k:98 + k]).then_inc(sem("y_ready"), 1)
            for u in y_after(k):
                if y_on_act(u):
                    act.wait_ge(sem("y_turned"), u + 1)
                    q, r = u // 5, P if u % 5 < 4 else NS
                    act.activation(ytok[0:r, u % 5, 512 * q:512 * q + 512], y_bank(u)[0:r], ACT.Copy)\
                       .then_inc(sem("y_act"), 1)

    @block.tensor
    def _(pe):
        mm = nc.tensor.matmul

        def turn(out, in_):
            k = in_.shape[0]
            b = in_.start_partition()
            return nc.tensor.transpose(out, in_, ident[b:b + k, b:b + k])

        def product(s, t, kt, width, sub, x, between, rows=P, kx0=0):
            if sub == 0:
                pe.wait_ge(sem("l_split"), (s + 1).v)
            if t.reg is not None or t.const >= 2:
                pe.wait_ge(sem(f"acc_read{t.odd}"), t.half().v)
            for k in range(kt):
                at_ = k * width + sub * P
                a_h, a_l = (w[:, s.odd, at_:at_ + rows] for w in (wh, wl))
                for n, (a, b) in enumerate(((a_h, x[0]), (a_h, x[1]), (a_l, x[0]))):
                    for half in range(2):
                        ins = mm(acc[0:rows, t.odd, half, 0:HALF], a, b[:, kx0 + k, half * HALF:half * HALF + HALF],
                                 start=(k == 0 and n == 0), stop=(k == kt - 1 and n == 2))
                if k == kt - 1:
                    ins.then_inc(sem("mm"), 1)
                for f in between.get(k, ()):
                    f()

        X = (xh, xl)

        def two_products(s, t, before):
            pe.wait_ge(sem("l_split"), (s + 2).v)
            if t.const >= 2:
                for i in range(2):
                    pe.wait_ge(sem(f"acc_read{(t + i).odd}"), (t + i).half().v)
            for k in range(KD):
                before(k)
                for i in range(2):
                    s_, t_ = s + i, t + i
                    a_h, a_l = (w[:, s_.odd, k * P:k * P + P] for w in (wh, wl))
                    for n, (a, b) in enumerate(((a_h, X[0]), (a_h, X[1]), (a_l, X[0]))):
                        for half in range(2):
                            ins = mm(acc[:, t_.odd, half, 0:HALF], a, b[:, k, half * HALF:half * HALF + HALF],
                                     start=(k == 0 and n == 0), stop=(k == KD - 1 and n == 2))
                    if k == KD - 1:
                        ins.then_inc(sem("mm"), 1)

        pe.wait_ge(sem("consts"), 1)
        pe.wait_ge(sem("vec_in"), 128)
        turn(b4[:, 0:113], vrows[0:113, :]).then_inc(sem("vec_turned"), 1)
        pe.wait_ge(sem("vec_ready"), 1)
        pe.wait_ge(sem("pt_ready"), 1)
        mm(b7[:, 64:72], pageof[:], ptT[:], start=True, stop=True).then_inc(sem("krow_sum"), 1)
        real, small = (b4, b6), (b5, b7)

        def x_turn(k):
            if k == 0:
                pe.wait_ge(sem("x_norm"), NB + 1)
            if k == 1:
                pe.wait_ge(sem("krow_ready"), 1)
            if k >= 2:
                pe.wait_ge(sem(f"x_lin{k % 2}"), k // 2)
            for c in range(NB):
                turn(real[k % 2][:, c * P:c * P + P], xtok[:, c, k * P:k * P + P])
            turn(small[k % 2][:, 0:R0], xtok_s[:, k * P:k * P + P]).then_inc(sem("x_turned"), 1)

        x_turn(0)
        x_turn(1)

        def x_step(k):
            if k + 2 < KD:
                x_turn(k + 2)
            pe.wait_ge(sem("xl_ready"), k + 1)

        def kx_turn(b):
            pe.wait_ge(sem(f"kx_in{b % 2}"), 16 * (b // 2 + 1))
            if b >= 2:
                pe.wait_ge(sem("kxT_ready"), b - 1)
            for r in range(4):
                last = turn((b4, b5)[b % 2][:, P * r:P * r + P], kx[:, b % 2, P * r:P * r + P])
            last.then_inc(sem("kx_turned"), 1)

        two_products(At(0), At(0), x_step)
        for i in (2, 3):
            product(At(i), At(i), KD, P, 0, X, {5 * q + 3: (lambda b=3 * i - 6 + q: kx_turn(b),) for q in range(3)})
        product(At(4), At(4), KD, 72, 0, X, {3: (lambda: kx_turn(6),), 8: (lambda: kx_turn(7),)}, rows=72)

        def wk_turn():
            pe.wait_ge(sem("wiki_ready"), 1)
            pe.wait_ge(sem("kxT_ready"), NS)
            for c in range(NB):
                turn(b4[:, 72 * c:72 * c + 72], wikiT[:, R0 + P * c:R0 + P * c + P])
            turn(b5[0:NM, 0:72], wikiT[:, M0:R0])
            turn(b5[0:NS, 72:144], wikiT[:, 0:NS]).then_inc(sem("idx_turned"), 1)

        def ki_back():
            pe.wait_ge(sem("wk_ready"), 1)
            for c in range(NB):
                turn(b6[:, P * c:P * c + P], wk[:, c, 8:136])
            turn(b7[:, M0:R0], wk[0:NM, 4, 8:136])
            turn(b7[:, 0:NS], wk[0:NS, 5, 8:136]).then_inc(sem("idx_turned"), 1)

        def kx_scores(b):
            pe.wait_ge(sem("kxT_ready"), b + 1)
            pe.wait_ge(sem("ki_ready"), 1)
            for r in range(4):
                at_ = (b * 4 + r) * 2 * NH
                last = mm(b6[:, at_:at_ + 2 * NH], kxT[:, b, P * r:P * r + P], qS[:, b, :, :].rearrange("p e h -> p (e h)"),
                          start=True, stop=True)
            last.then_inc(sem("sidx_scores"), 1)

        def kx_new():
            pe.wait_ge(sem("prod_ready"), 1)
            pe.wait_ge(sem("kxT_ready"), NS)
            for m in range(4):
                mm(b5[0:NS, 2 * m:2 * m + 2], prod[:, m, :], halfsel[:], start=True, stop=True)
            mm(b4[:, 0:64], ones[0:NS, :], wsel[:].rearrange("k b h -> k (b h)"), start=True, stop=True)\
                .then_inc(sem("wbc_sum"), 1)

        def is_turn():
            pe.wait_ge(sem("isc_ready"), 1)
            pe.wait_ge(sem("nsc_relu"), 1)
            for e in range(2):
                for r in range(4):
                    last = turn((b4, b5)[e][0:NS, P * r:P * r + P], isc[:, :, 2 * r + e])
            last.then_inc(sem("idx_turned"), 1)

        def idx_scores(i, m):
            n = 4 * i + m
            if n == 0:
                pe.wait_ge(sem("isc_read"), 2)
            else:
                pe.wait_ge(sem("idx_relu"), 2 * n)
            w = P * (i + 1)
            lo = R0 + P * i
            for e, (real_, meta) in enumerate(((b4, b6), (b5, b7))):
                a = qiT[64 * e:64 * e + 64, m, lo:lo + P]
                mm(real_[:, 0:w], a, kiT[64 * e:64 * e + 64, R0:R0 + w], start=True, stop=True)
                last = mm(meta[:, 0:NM], a, kiT[64 * e:64 * e + 64, M0:R0], start=True, stop=True)
            last.then_inc(sem("idx_scores"), 1)

        def head_turn(n):
            pe.wait_ge(sem("idx_relu"), 32)
            pe.wait_ge(sem("hi_ready"), n + 1)
            pe.wait_ge(sem("qd_ready"), n + 1)
            pe.wait_ge(sem("decayed"), n + 1)
            for c in range(NB):
                lo = R0 + P * c
                turn(b4[:, P * c:P * c + P], hiT[:, lo:lo + P])
                turn(b6[:, P * c:P * c + P], ke[:, lo:lo + P])
            turn(b5[0:NM, 0:P], hiT[:, M0:R0])
            turn(b5[0:NS, P:2 * P], hiT[:, 0:NS])
            turn(b5[0:NM, 2 * P:3 * P], ke[:, M0:R0])
            off = NB * (32 + 64 + 96 + 128)
            mm(b5[0:NM, 3 * P:3 * P + NM], et[:, off:off + NM], qd[:, M0:R0], start=True, stop=True)\
                .then_inc(sem("head_turned"), 1)
            off = 0
            for i in range(4):
                w = SUB * (i + 1)
                for c in range(NB):
                    last = mm(b7[0:w, P * c + SUB * i:P * c + SUB * i + SUB], et[:, off + c * w:off + c * w + w],
                              qd[:, R0 + P * c + SUB * i:R0 + P * c + SUB * i + SUB], start=True, stop=True)
                off += NB * w
            last.then_inc(sem("intra_done"), 1)

        def outer(n):
            pe.wait_ge(sem("tok_ready"), n + 1)
            pe.wait_ge(sem("aT_ready"), n + 1)
            for c in range(NB):
                mm(b4[:, P * c:P * c + P], ketok[:, c, :], itok[:, c, :], start=True, stop=True)
            mm(b5[:, 0:P], ketok[0:NM, 4, :], itok[0:NM, 4, :], start=True, stop=True).then_inc(sem("outer_done"), 1)

        def spread(n):
            for b in range(NS):
                last = mm((b6, b7)[b // 4][:, P * (b % 4):P * (b % 4) + P], ident[0:NS, b:b + 1].to_broadcast([NS, P]),
                          itok[0:NS, 5, :], start=True, stop=True)
            last.then_inc(sem("spread_done"), 1)

        def head_out(n):
            pe.wait_ge(sem("st_ready"), n + 1)
            for c in range(NB):
                lo = R0 + P * c
                mm(b4[:, P * c:P * c + P], itok[:, c, :], aT[:, c, :], start=True, stop=False)
                mm(b4[:, P * c:P * c + P], st[:, c, :], qe[:, lo:lo + P], start=False, stop=True)
            mm(b5[:, M0:R0], itok[0:NM, 4, :], aTm[:], start=True, stop=True)
            pe.wait_ge(sem("sstate_ready"), n + 1)
            for b in range(NS):
                last = mm(b5[:, b:b + 1], ss[:, b, :], hq[:, b:b + 1], start=True, stop=True)
            last.then_inc(sem("ho_done"), 1)

        def norm_sum(n):
            pe.wait_ge(sem("squared"), n + 1)
            mm(b6[:, :], ones[:], t2[:, R0:NT], start=True, stop=True)
            mm(b7[:, 0:R0], ones[:], t2[:, 0:R0], start=True, stop=True).then_inc(sem("norm_sum"), 1)

        def late(n, j):
            if j == 0:
                return {2: (lambda: head_turn(n),), 12: (lambda: outer(n),), 15: (lambda: spread(n),)}
            if j == 1:
                return {11: (lambda: head_out(n),)}
            if j == 2:
                return {11: (lambda: norm_sum(n),)}
            return {}

        for j in range(4):
            side = {}
            if j == 0:
                side = {1: (wk_turn,), 4: (ki_back,), 9: (lambda: [kx_scores(b) for b in range(NS)], kx_new)}
            if j == 1:
                side = {2: (is_turn,)}
            steps = [(i, m) for i in IDX_BLOCKS[j] for m in range(4)]
            for q, (i, m) in enumerate(steps):
                at_ = (4, 3)[j // 2] + (3 * q + 1) // 2
                side[at_] = side.get(at_, ()) + (lambda i=i, m=m: idx_scores(i, m),)
            product(At(S_C + j), At(S_C + j), KD, P, 0, X, side)
        with pe.Fori(1, NH, 1) as h:
            for j in range(4):
                s = At(S_C + j, 4, h)
                product(s, s, KD, P, 0, X, late(h - 1, j))

        def kv_turn(g, j, small):
            c = 4 * g + 2 * j + small
            src = (kT[g % 2], vT)[j]
            pe.wait_ge(sem("qkv_in"), 4 * g + j + 1)
            if g == 0:
                pe.wait_ge(sem("sstate_ready"), NH) if j == 0 else pe.wait_ge(sem("norm_ln"), NH)
            else:
                pe.wait_ge(sem("pv_out"), 4 * (g - 1) + j + 1)
            if c >= 1:
                pe.wait_ge(sem("kv_tok"), c)
            if small:
                turn(b7[0:NM, 0:P], src[:, M0:R0])
                last = turn(b7[0:NS, P:2 * P], src[:, 0:NS])
            else:
                for q in range(NB):
                    last = turn(b7[:, P * q:P * q + P], src[:, R0 + P * q:R0 + P * q + P])
            last.then_inc(sem("kv_turned"), 1)

        def att_scores(n):
            g, i = n // NB, n % NB
            pe.wait_ge(sem("qkv_in"), 4 * g + 4)
            if n == 0:
                pe.wait_ge(sem("mixed"), NH + 1)
            else:
                pe.wait_ge(sem("pT_out"), n)
            q, k = qT[g % 2], kT[g % 2]
            w, lo = P * (i + 1), R0 + P * i
            for hd in range(2):
                mm((b4, b5)[hd][:, 0:w], q[:, hd, lo:lo + P], k[:, R0:R0 + w], start=True, stop=True)
                last = mm(b6[:, NM * hd:NM * hd + NM], q[:, hd, lo:lo + P], k[:, M0:R0], start=True, stop=True)
                if i == 0:
                    last = mm(b6[0:NM, 2 * NM + NM * hd:3 * NM + NM * hd], q[:, hd, M0:R0], k[:, M0:R0],
                              start=True, stop=True)
            last.then_inc(sem("att_scores"), 1)

        def p_turn(n):
            i = n % NB
            pe.wait_ge(sem("att_p"), n + 1)
            for hd in range(2):
                for c in range(i + 1):
                    turn((b4, b5)[hd][:, P * c:P * c + P], lg[:, hd, NM + P * c:NM + P * c + P])
                last = turn(b6[0:NM, P * hd:P * hd + P], lg[:, hd, 0:NM])
                if i == 0:
                    last = turn(b6[0:NM, 2 * P + NM * hd:2 * P + NM * hd + NM], lgm[:, hd, :])
            last.then_inc(sem("p_turned"), 1)

        def pv(n):
            g, i = n // NB, n % NB
            v = vtok[g % 2]
            pe.wait_ge(sem("pT_out"), n + 1)
            pe.wait_ge(sem("kv_tok"), min(16, 4 * g + 4 + (0, 2, 4, 4)[i]))
            if n == 11:
                pe.wait_ge(sem("grow_ready"), 1)
            for hd in range(2):
                out = b7[:, P * hd:P * hd + P]
                for c in range(i + 1):
                    mm(out, v[:, c, :], pT[:, hd, P * c:P * c + P], start=(c == 0), stop=False)
                last = mm(out, v[0:NM, 4, :], pTm[:, P * hd:P * hd + P], start=False, stop=True)
            if i == 0:
                for hd in range(2):
                    last = mm(b7[:, 2 * P + NM * hd:2 * P + NM * hd + NM], v[0:NM, 4, :],
                              pTm[:, 2 * P + NM * hd:2 * P + NM * hd + NM], start=True, stop=True)
            last.then_inc(sem("pv_done"), 1)

        def row_turn():
            pe.wait_ge(sem("rows_ready"), 1)
            pe.wait_ge(sem("pv_out"), 11)
            for blk in range(NBLK):
                last = turn(b7[:, NS * blk:NS * blk + NS], work[:, 3, P * blk:P * blk + P])
            last.then_inc(sem("rows_turned"), 1)

        for g in range(NG):
            for j in range(4):
                side = {}
                if g == 0:
                    side = late(NH - 1, j)
                    if j == 2:
                        side = {2: (lambda: kv_turn(0, 0, 0),), 5: (lambda: kv_turn(0, 0, 1),), 11: side[11]}
                    if j == 3:
                        side = {12: (lambda: kv_turn(0, 1, 0),), 15: (lambda: kv_turn(0, 1, 1),)}
                else:
                    n = 4 * (g - 1) + j
                    if n >= 1:
                        side[3] = (lambda n=n: pv(n - 1),)
                    side[5] = (lambda n=n: att_scores(n),)
                    if j in (1, 2):
                        side[8] = (lambda g=g, j=j: kv_turn(g, j - 1, 0),)
                        side[11] = (lambda g=g, j=j: kv_turn(g, j - 1, 1),)
                    if n == 11:
                        side[8] = (row_turn,)
                    side[15] = (lambda n=n: p_turn(n),)
                s = At(S_B + 4 * g + j)
                product(s, s, KD, P, 0, X, side)

        def mix_in(k):
            return lambda: pe.wait_ge(sem("mix_in"), k + 1)

        def sg_turn(b):
            pe.wait_ge(sem(f"gk{b % 2}"), 16 * NBLK * (b // 2 + 1))
            pe.wait_ge(sem("sgT"), b) if b >= 1 else pe.wait_ge(sem("pT_out"), 16)
            for blk in range(NBLK):
                for g in range(NG):
                    last = turn((b4, b5)[blk][:, P * g:P * g + P], kgs[:, b % 2, blk, P * g:P * g + P])
            last.then_inc(sem("sg_turned"), 1)

        def s_scores(b):
            pe.wait_ge(sem("sgT"), b + 1)
            if b >= 1:
                pe.wait_ge(sem("sexp"), b)
            out = b6[0:NH, 0:KEEP_S + 1]
            mm(out, ident[0:NS, b:b + 1].to_broadcast([NS, NH]), maskS[:], start=True, stop=False)
            mm(out, nsl[:, b, :], distS[:], start=False, stop=False)
            for g in range(NG):
                mm(b6[0:NH, 0:KEEP_S], qpad[:, g, b, :], kgT[:, :, g, :], start=False, stop=False)
            for g in range(NG):
                last = mm(b6[0:NH, KEEP_S:KEEP_S + 1], qpad[:, g, b, :], knew[:, g, b:b + 1], start=False, stop=(g == NG - 1))
            last.then_inc(sem("slog"), 1)

        def sp_turn(b):
            pe.wait_ge(sem("sp_ready"), b + 1)
            pe.wait_ge(sem("so_out"), b) if b >= 1 else pe.wait_ge(sem("pv_out"), 16)
            for blk in range(NBLK):
                turn(b7[:, 8 * blk:8 * blk + 8], ps[:, P * blk:P * blk + P])
            mm(b7[0:NS, 16:24], pz[:, NS - 1 - b:2 * NS - 1 - b], ident[0:NH, 0:NH], start=True, stop=True)\
                .then_inc(sem("sp_turned"), 1)

        def s_pv(b):
            pe.wait_ge(sem("spT"), b + 1)
            pe.wait_ge(sem(f"gv{b % 2}"), 16 * NBLK * (b // 2 + 1))
            if b == 0:
                pe.wait_ge(sem("vnew_in"), NG)
            for g in range(NG):
                out = b7[:, 32 + 2 * g:34 + 2 * g]
                for blk in range(NBLK):
                    mm(out, vgs[:, b % 2, blk, P * g:P * g + P], pTs[:, 8 * blk + 2 * g:8 * blk + 2 * g + 2],
                       start=(blk == 0), stop=False)
                last = mm(out, vnew[:, g, :], pTs[0:NS, 16 + 2 * g:18 + 2 * g], start=False, stop=True)
            last.then_inc(sem("so_done"), 1)

        mix_in(0)()
        for n in range(8):
            for i in range(2):
                side = {}
                if n == 0 and i == 0:
                    side = {k: (mix_in(k + 1),) for k in range(7)}
                if n <= 3:
                    if i == 0:
                        side[3] = side.get(3, ()) + (lambda n=n: pv(11 + n),)
                        side[5] = side.get(5, ()) + (lambda n=n: att_scores(12 + n),)
                    else:
                        side[7] = (lambda n=n: p_turn(12 + n),)
                else:
                    b = 2 * (n - 4) + i
                    side = {0: (lambda b=b: sg_turn(b),), 2: (lambda b=b: s_scores(b),),
                            6: (lambda b=b: sp_turn(b),), 7: (lambda b=b: s_pv(b),)}
                    if b == 0:
                        side[0] = (lambda: pv(15),) + side[0]
                product(At(S_D1 + n), At(T_D1 + 2 * n + i), 8, 256, i, X, side, kx0=8)

        def att_in(k):
            return lambda: pe.wait_ge(sem("att_in"), k + 1)

        def d2(n2):
            for i in range(2):
                for e in range(2):
                    if isinstance(n2, int):
                        s, t = At(S_D2 + i + 2 * n2), At(T_D2 + 2 * i + e + 4 * n2)
                    else:
                        s, t = At(S_D2 + i, 2, n2), At(T_D2 + 2 * i + e, 4, n2)
                    side = {k: (att_in(k + 1),) for k in range(7)} if isinstance(n2, int) and i == e == 0 else {}
                    product(s, t, 8, 256, e, X, side)

        att_in(0)()
        d2(0)
        with pe.Fori(1, 4, 1) as n2:
            d2(n2)

        def ln_sums(n):
            pe.wait_ge(sem("s_sum"), 16 * n)
            pe.wait_ge(sem("q_sum"), 16 * n)
            if n == 1:
                pe.wait_ge(sem("so_out"), NS)
            mm(b4[:, :], ones[:], ssum[:, 0, R0:NT], start=True, stop=True)
            mm(b5[:, 0:R0], ones[:], ssum[:, 0, 0:R0], start=True, stop=True)
            mm(b6[:, :], ones[:], ssum[:, 1, R0:NT], start=True, stop=True)
            mm(b7[:, 0:R0], ones[:], ssum[:, 1, 0:R0], start=True, stop=True).then_inc(sem("ln_sums"), 1)

        ln_sums(1)

        def mlp(c, plan):
            for kind, n, s, t in plan:
                if kind == "down":
                    if n == 0:
                        pe.wait_ge(sem("hl_done"), FC * c)
                    for i in range(4):
                        product(s, t + i, FC, 512, i, (hh, hl), {})
                else:
                    product(s, t, KD, P, 0, X, {})

        two_products(At(S_E), At(T_E), lambda k: pe.wait_ge(sem("x1_in"), k + 1))
        mlp(0, mlp_plan(0)[2:])
        with pe.Fori(1, NC, 1) as c:
            mlp(c, mlp_plan(c))
        mlp(NC, mlp_plan(NC))
        ln_sums(2)
        for q in range(4):
            pe.wait_ge(sem("y_ready"), 4 * q + 4)
            if q == 0:
                pe.wait_ge(sem("s_done"), 32)
            for c in range(NB + 1):
                u = 5 * q + c
                if u >= 8:
                    name, n = y_copied(u - 8)
                    pe.wait_ge(sem(name), n)
                for k in range(4):
                    out = y_bank(u)[:, P * k:P * k + P]
                    if c < NB:
                        last = turn(out, sacc[:, 4 * q + k, R0 + P * c:R0 + P * c + P])
                    else:
                        last = turn(out[0:NS], sacc[:, 4 * q + k, 0:NS])
                last.then_inc(sem("y_turned"), 1)

    @block.vector
    def _(dve):
        V = nc.vector
        ch = Chain(dve, sem("dve_step"))

        def split(s, n=2048):
            dve.wait_ge(sem("h_split"), (s + 1).v)
            V.tensor_tensor(wl[:, s.odd, 0:n], raw[:, s.odd, 0:n], fr(wh[:, s.odd, 0:n]), ALU.subtract)\
                .then_inc(sem("l_split"), 1)

        for c in (NB, 0, 1, 2, 3):
            n, src = (R0, xtok_s) if c == NB else (P, xtok[:, c, :])
            dve.wait_ge(sem(f"x_in{c}"), 32 if c == NB else 16)
            for q in range(4):
                last = V.bn_stats(bn[0:n, c, q, :], src[0:n, q * 512:q * 512 + 512])
            ch(last)
            V.bn_aggr(mv[0:n, c, 0:2], bn[0:n, c, :, :].rearrange("p a b -> p (a b)")).then_inc(sem("var"), 1)
        dve.wait_ge(sem("pt_in"), 32)
        V.tensor_copy(ptT[:], pt_i[:, 0, :])
        V.tensor_copy(ptB[:], pt_i[:, 1, :]).then_inc(sem("pt_ready"), 1)
        dve.wait_ge(sem("vec_ready"), 1)
        ch(V.tensor_tensor(lb[:, 16:24], vec[:, 64:72], vec[:, 72:80], ALU.max))
        V.tensor_tensor(lb[:, 8:16], vec[:, 72:80], lb[:, 16:24], ALU.subtract)
        V.tensor_tensor(lb[:, 0:8], vec[:, 64:72], lb[:, 16:24], ALU.subtract).then_inc(sem("lb_shifted"), 1)
        dve.wait_ge(sem("consts"), 1)
        ch(V.tensor_scalar(pmod[:].bitcast(I32), pmod[:].bitcast(I32), 15, None, ALU.bitwise_and))
        ch(V.tensor_copy(pmod[:], pmod[:].bitcast(I32)))
        dve.wait_ge(sem("krow_sum"), 1)
        V.tensor_tensor(krow[:], b7[:, 64:72], pmod[:], ALU.add).then_inc(sem("krow_ready"), 1)
        dve.wait_ge(sem("lb_exp"), 1)
        ch(V.tensor_tensor(lb[:, 16:24], lb[:, 0:8], lb[:, 8:16], ALU.add))
        ch(V.reciprocal(lb[:, 16:24], lb[:, 16:24]))
        ch(V.tensor_tensor(lb[:, 0:8], lb[:, 0:8], lb[:, 16:24], ALU.mult))
        V.tensor_scalar(lb[:, 16:24], lb[:, 0:8], 1.0, None, ALU.subtract)
        ch(V.tensor_scalar(lb[:, 8:16], lb[:, 0:8], -1.0, 1.0, ALU.mult, ALU.add))
        real, small = (b4, b6), (b5, b7)
        split(At(0))
        split(At(1))
        for k in range(KD):
            if k % 2 == 0:
                dve.wait_ge(sem("x_turned"), k + 1)
                if k >= 2:
                    dve.wait_ge(sem("xl_ready"), k - 1)
                g, b = vec[:, k:k + 1], vec[:, 16 + k:17 + k]
                V.tensor_scalar(lnt[:, 0, R0:NT], b4[:, :], g, b, ALU.mult, ALU.add)
                V.tensor_scalar(lnt[:, 0, 0:R0], b5[:, 0:R0], g, b, ALU.mult, ALU.add).then_inc(sem("x_lin0"), 1)
            dve.wait_ge(sem("xh_ready"), k + 1)
            V.tensor_tensor(xl[:, k, :], lnt[:, k % 2, :], fr(xh[:, k, :]), ALU.subtract).then_inc(sem("xl_ready"), 1)
        for i in range(2, 5):
            split(At(i), KD * 72 if i == 4 else 2048)
        split(At(S_C))

        def idx_setup():
            V.memset(qS[:], 0.0).then_inc(sem("qS_clear"), 1)
            dve.wait_ge(sem("wk_ready"), 1)
            ch(V.tensor_scalar(wk[:, 0:4, 0:8], wk[:, 0:4, 0:8], IDX_W_SCALE, None, ALU.mult))
            ch(V.tensor_scalar(wk[0:NS, 5, 0:8], wk[0:NS, 5, 0:8], IDX_W_SCALE, None, ALU.mult))
            ch(V.tensor_tensor(wsel[:], wk[0:NS, 5, 0:8].unsqueeze(1).to_broadcast([NS, NS, NH]),
                               ident[0:NS, 0:NS].unsqueeze(2).to_broadcast([NS, NS, NH]), ALU.mult))
            dve.wait_ge(sem("ki_ready"), 1)
            V.tensor_tensor(prod[:], qiT[:, :, 0:NS], kiT[:, 0:NS].unsqueeze(1).to_broadcast([P, 4, NS]), ALU.mult)\
                .then_inc(sem("prod_ready"), 1)

        def idx_samples():
            dve.wait_ge(sem("wbc_sum"), 1)
            ch(V.tensor_copy(wbc[:], b4[:, 0:64].rearrange("p (b h) -> p b h", b=NS)))
            dve.wait_ge(sem("sidx_relu"), 1)
            v = rsc[:, :].rearrange("p (b r h) -> p b r h", b=NS, r=8)
            ch(V.tensor_tensor(v, v, wbc[:].unsqueeze(2).to_broadcast([P, NS, 8, NH]), ALU.mult))
            ch(V.tensor_reduce(isc[:], v, AX, ALU.add))
            dve.sem_inc(sem("isc_ready"), 1)
            dve.wait_ge(sem("nsc_relu"), 1)
            ch(V.tensor_tensor(nsc[:], nsc[:], wk[0:NS, 5, 0:8], ALU.mult))
            ch(V.tensor_reduce(curs[:, PAST:PAST + 1], nsc[:], AX, ALU.add))

        def idx_sample_rows():
            dve.wait_ge(sem("idx_turned"), 3)
            rows = curs[:, 0:PAST].rearrange("b (p r e) -> b e r p", r=4, e=2)
            for e in range(2):
                V.tensor_copy(rows[:, e], (b4, b5)[e][0:NS, :].rearrange("b (r p) -> b r p", r=4))\
                    .then_inc(sem("isc_read"), 1)
            dve.wait_ge(sem("isc_read"), 2)

        def idx_sum(i, m):
            n = 4 * i + m
            out = cur[:, WOFF[i]:WOFF[i] + WIDE[i]]
            for e in range(2):
                w = wk[:, i, 2 * m + e:2 * m + e + 1]
                dve.wait_ge(sem("idx_relu"), 2 * n + e + 1)
                if m == 0 and e == 0:
                    ch(V.tensor_scalar(out, rel[:, e, 0:WIDE[i]], w, None, ALU.mult))
                else:
                    ch(V.scalar_tensor_tensor(out=out, in0=rel[:, e, 0:WIDE[i]], scalar=w, in1=out,
                                              op0=ALU.mult, op1=ALU.add))
            dve.sem_inc(sem("idx_summed"), 1)
            if m == 3:
                ch(V.tensor_tensor(out[:, WIDE[i] - P:WIDE[i]], out[:, WIDE[i] - P:WIDE[i]], causal[:], ALU.add))

        def take_prompt(c2):
            for i in range(NB):
                V.max(top8[:, i, :], cur[:, WOFF[i]:WOFF[i] + WIDE[i]]).then_inc(sem("dve_top"), 1)
            wait_apart(dve, sem("dve_top"), c2 + 4, sem("seen"))
            for i in range(NB):
                row = cur[:, WOFF[i]:WOFF[i] + WIDE[i]]
                V.match_replace(row, top8[:, i, :], row, TAKEN).then_inc(sem("dve_top"), 1)
            wait_apart(dve, sem("dve_top"), c2 + 8, sem("seen"))

        def take_sample(c3, slot):
            V.max(tops[:], curs[:]).then_inc(sem("dve_tops"), 1)
            wait_apart(dve, sem("dve_tops"), c3 + 1, sem("seen"))
            V.max_index(topi[:], tops[:], curs[:]).then_inc(sem("dve_tops"), 1)
            V.match_replace(curs[:], tops[:], curs[:], TAKEN).then_inc(sem("dve_tops"), 1)
            dve.wait_ge(sem("dve_tops"), c3 + 3)
            V.tensor_copy(slot, topi[:]).then_inc(sem("dve_tops"), 1)
            dve.wait_ge(sem("dve_tops"), c3 + 4)

        def t_of(h4, j):
            return h4 + (S_C + j)

        def lbcol(n, which):
            return lb[:, 8 * which + n:8 * which + n + 1] if isinstance(n, int) else lb[:, bass.ds(n + 8 * which, 1)]

        def cap(u):
            dve.wait_ge(sem("sig_exp"), u + 1)
            V.tensor_scalar(t1[:, :], t1[:, :], SIG_CAP, None, ALU.min).then_inc(sem("sig_capped"), 1)

        SCAN = 8

        def forget(h4, n):
            t = t_of(h4, 0)
            cap(3 * n)
            V.sem_inc(sem(f"acc_read{t.odd}"), 1)
            dve.wait_ge(sem("sigmoid"), 3 * n + 1)
            dve.wait_ge(sem("head_turned"), n)
            V.tensor_scalar(kf[:, :], t1[:, :], lbcol(n, 2), lbcol(n, 1), ALU.mult, ALU.add).then_inc(sem("kf_ready"), 1)
            dve.wait_ge(sem("logf"), n + 1)
            for c in range(NB):
                lo = R0 + P * c
                V.tensor_tensor_scan(bcum[:, lo:lo + P], ones[:], t2[:, lo:lo + P], 0.0, ALU.mult, ALU.add)
            V.tensor_tensor_scan(bcum[:, M0:R0], ones[:, 0:NM], t2[:, M0:R0], 0.0, ALU.mult, ALU.add)
            V.tensor_copy(bcum[:, 0:NS], t2[:, 0:NS]).then_inc(sem("b_ready"), 1)

        def query(h4, n):
            t = t_of(h4, 1)
            cap(3 * n + 1)
            dve.wait_ge(sem("sigmoid"), 3 * n + 2)
            dve.wait_ge(sem("ho_done"), n + 1)
            V.tensor_tensor(cut(hq[:, :]), whole(t), cut(t1[:, :]), ALU.mult).then_inc(sem("q_ready"), 1)
            dve.wait_ge(sem("q_ready"), n + 1)
            V.sem_inc(sem(f"acc_read{t.odd}"), 1)
            dve.wait_ge(sem("b_ready"), n + 1)
            dve.wait_ge(sem("intra_done"), n)
            v = bcum[:, R0:NT].rearrange("p (s x) -> p s x", x=SUB)
            V.tensor_tensor(qd[:, R0:NT].rearrange("p (s x) -> p s x", x=SUB), v,
                            v[:, :, SUB // 2 - 1:SUB // 2].to_broadcast([P, NR // SUB, SUB]), ALU.subtract)
            V.tensor_scalar(qd[:, M0:R0], bcum[:, M0:R0], bcum[:, M0 + 7:M0 + 8], None, ALU.subtract).then_inc(sem("qd_arg"), 1)

        def decays(h4, n):
            dve.wait_ge(sem("qd_exp"), n + 1)
            V.tensor_tensor(qd[:, M0:NT], qd[:, M0:NT], hq[:, M0:NT], ALU.mult).then_inc(sem("qd_ready"), 1)

        def triangle(n):
            dve.wait_ge(sem("intra_done"), n + 1)
            dve.wait_ge(sem("ho_done"), n + 1)
            v = b7[:, :].rearrange("p (c x) -> p c x", c=NB)
            for i in range(4):
                w, lo = SUB * (i + 1), SUB * i
                V.tensor_tensor(aT[0:w, :, lo:lo + SUB], v[0:w, :, lo:lo + SUB],
                                tri[0:w, lo:lo + SUB].unsqueeze(1).to_broadcast([w, NB, SUB]), ALU.mult)
            dve.wait_ge(sem("tok_ready"), n + 1)
            V.tensor_tensor(aTm[:], b5[0:NM, 3 * P:3 * P + NM], tri[0:NM, 0:NM], ALU.mult).then_inc(sem("aT_ready"), 1)

        def gating(h4, n):
            t = t_of(h4, 3)
            cap(3 * n + 2)
            dve.wait_ge(sem("sigmoid"), 3 * n + 3)
            dve.wait_ge(sem("mixed"), n + 1)
            V.tensor_tensor(cut(gate[:, :]), whole(t), cut(t1[:, :]), ALU.mult).then_inc(sem("gate_ready"), 1)
            dve.wait_ge(sem("gate_ready"), n + 1)
            V.sem_inc(sem(f"acc_read{t.odd}"), 1)

        def states(n, cst):
            dve.wait_ge(sem("outer_done"), n + 1)
            dve.wait_ge(sem("ends_exp"), n + 1)
            dve.wait_ge(sem("ho_done"), n + 1)
            dve.wait_ge(sem("state_left"), n + 1)
            V.tensor_copy(st[:, 0, :], b5[:, 0:P]).then_inc(sem("dve_st"), 1)
            for c in range(NB):
                dve.wait_ge(sem("dve_st"), cst + c + 1)
                ins = V.scalar_tensor_tensor(out=st[:, c + 1, :], in0=st[:, c, :], scalar=eb[:, c:c + 1],
                                             in1=b4[:, P * c:P * c + P], op0=ALU.mult, op1=ALU.add)
                ins.then_inc(sem("dve_st"), 1)
            dve.wait_ge(sem("dve_st"), cst + 5)
            dve.sem_inc(sem("st_ready"), 1)
            dve.wait_ge(sem("spread_done"), n + 1)
            dve.wait_ge(sem("state_in"), (n + 1) * 16)
            for b in range(NS):
                V.tensor_scalar(ss[:, b, :], ss[:, b, :], fs[:, b:b + 1], None, ALU.mult).then_inc(sem("dve_st"), 1)
            dve.wait_ge(sem("dve_st"), cst + 5 + NS)
            for b in range(NS):
                ins = V.scalar_tensor_tensor(out=ss[:, b, :], in0=(b6, b7)[b // 4][:, P * (b % 4):P * (b % 4) + P],
                                             scalar=kf[:, b:b + 1], in1=ss[:, b, :], op0=ALU.mult, op1=ALU.add)
            ins.then_inc(sem("sstate_ready"), 1)
            return 5 + NS

        def mix(n, cm):
            dve.wait_ge(sem("norm_scale"), n + 1)
            V.tensor_tensor(t2[:, R0:NT], b4[:, :], t2[:, R0:NT], ALU.mult).then_inc(sem("dve_mix"), 1)
            V.tensor_tensor(t2[:, 0:R0], b5[:, 0:R0], t2[:, 0:R0], ALU.mult).then_inc(sem("dve_mix"), 1)
            dve.wait_ge(sem("dve_mix"), cm + 2)
            dst = sacc[:, NH + n, :] if isinstance(n, int) else sacc[:, bass.ds(n + NH, 1), :].rearrange("p o n -> p (o n)")
            V.scalar_tensor_tensor(out=dst, in0=t2[:, :], scalar=vec[:, 80:81], in1=gate[:, :],
                                   op0=ALU.mult, op1=ALU.mult).then_inc(sem("mixed"), 1)

        def early(h4, n, j):
            if j == 1:
                forget(h4, n)
            if j == 2:
                query(h4, n)
            if j == 3:
                decays(h4, n)

        def late(h4, n, j):
            if j == 0:
                triangle(n)
                gating(h4, n)
            if j == 1:
                states(n, n * (5 + NS))
            if j == 3:
                mix(n, n * 2)

        idx_setup()
        for j in range(4):
            split(At(S_C + j + 1))
            if j == 1:
                idx_sample_rows()
            early(At(0), 0, j)
            if j == 0:
                idx_samples()
                V.memset(aT[:], 0.0)
            for i in IDX_BLOCKS[j]:
                for m in range(4):
                    idx_sum(i, m)
        with dve.Fori(1, NH, 1) as h:
            for j in range(4):
                split(At(S_C + j + 1, 4, h))
                late(At(-4, 4, h), h - 1, j)
                early(At(0, 4, h), h, j)
                if j < 2:
                    take_prompt((h - 1) * 16 + 8 * j)
                if j >= 1:
                    take_sample((h - 1) * 12 + 4 * (j - 1), idx[:, bass.ds((h - 1) * 24 + 8 * (j - 1), 8)])

        def keep_prompt(i):
            row = cur[:, WOFF[i]:WOFF[i] + WIDE[i]]
            w = WIDE[i]
            eq, rank, cnt = et[:, 0:w], et[:, 528:528 + w], et[:, 1060:1064]
            km = keepmask[:, WOFF[i]:WOFF[i] + w]
            top = top8[:, i, :]
            ch(V.max(top, row))
            least = top8[:, i, 3:4]
            V.tensor_scalar(cnt[:, 0:3], top8[:, i, 0:3], least, None, ALU.is_gt)
            ch(V.tensor_scalar(eq, row, least, None, ALU.is_equal))
            V.tensor_tensor_scan(rank, eq, eq, 0.0, ALU.add, ALU.max)
            ch(V.tensor_reduce(cnt[:, 3:4], cnt[:, 0:3], AX, ALU.add))
            ch(V.tensor_scalar(cnt[:, 3:4], cnt[:, 3:4], -1.0, 4.0, ALU.mult, ALU.add))
            ch(V.scalar_tensor_tensor(out=rank, in0=rank, scalar=cnt[:, 3:4], in1=eq, op0=ALU.is_le, op1=ALU.mult))
            ch(V.scalar_tensor_tensor(out=rank, in0=row, scalar=least, in1=rank, op0=ALU.is_gt, op1=ALU.add))
            ch(V.scalar_tensor_tensor(out=rank, in0=row, scalar=TAKEN, in1=rank, op0=ALU.is_equal, op1=ALU.add))
            ch(V.tensor_scalar(km, rank, -OFF, OFF, ALU.mult, ALU.add))
            ch(V.tensor_tensor(km[:, w - P:w], km[:, w - P:w], causal[:], ALU.add))

        def sample_rows():
            page, pos, rows = work[:, 0, :], work[:, 1, :], work[:, 3, :]
            ch(V.tensor_scalar(page.bitcast(I32), idx[:].bitcast(I32), 7, None, ALU.logical_shift_right))
            ch(V.tensor_scalar(pos.bitcast(I32), idx[:].bitcast(I32), P - 1, None, ALU.bitwise_and))
            ch(V.tensor_copy(page, page.bitcast(I32)))
            ch(V.tensor_copy(rows, pos.bitcast(I32)))
            ch(V.tensor_copy(pos, idx[:].bitcast(I32)))
            ch(V.tensor_scalar(distS[:, 0:KEEP_S], pos, -1.0, float(PAST), ALU.mult, ALU.add))
            ch(V.memset(distS[:, KEEP_S:KEEP_S + 1], 0.0))
            ch(V.tensor_scalar(maskS[:, 0:KEEP_S], pos, float(PAST), None, ALU.is_ge))
            ch(V.tensor_reduce(maskS[:, KEEP_S:KEEP_S + 1], maskS[:, 0:KEEP_S], AX, ALU.add))
            ch(V.tensor_scalar(maskS[:, 0:KEEP_S], maskS[:, 0:KEEP_S], OFF, None, ALU.mult))
            ch(V.tensor_scalar(maskS[:, KEEP_S:KEEP_S + 1], maskS[:, KEEP_S:KEEP_S + 1], -OFF, OFF, ALU.mult, ALU.add))
            for q in range(PAST // P):
                ch(V.tensor_scalar(work[:, 2, :], page, float(q), ptB[:, q:q + 1], ALU.is_equal, ALU.mult))
                ch(V.scalar_tensor_tensor(out=rows, in0=work[:, 2, :], scalar=float(P), in1=rows,
                                          op0=ALU.mult, op1=ALU.add))
            V.tensor_tensor(nsl[:], ident[0:NS, 0:NS].unsqueeze(2).to_broadcast([NS, NS, NH]),
                            slope8[:].unsqueeze(1).to_broadcast([NS, NS, NH]), ALU.mult).then_inc(sem("rows_ready"), 1)

        def attend(n):
            g, i = n // NB, n % NB
            w = WIDE[i]
            if n >= 1:
                dve.wait_ge(sem("p_turned"), n)
            for hd in range(2):
                slope = -(2.0 ** -(2 * g + hd + 1))
                ch(V.scalar_tensor_tensor(out=lg[:, hd, 0:w], in0=dist[:, 384 - P * i:384 - P * i + w], scalar=slope,
                                          in1=keepmask[:, WOFF[i]:WOFF[i] + w], op0=ALU.mult, op1=ALU.add))
                if i == 0:
                    ch(V.scalar_tensor_tensor(out=lgm[:, hd, :], in0=dist[0:NM, 400:400 + NM], scalar=slope,
                                              in1=causal[0:NM, 0:NM], op0=ALU.mult, op1=ALU.add))
            dve.wait_ge(sem("att_scores"), n + 1)
            for hd in range(2):
                V.scalar_tensor_tensor(out=lg[:, hd, NM:w], in0=(b4, b5)[hd][:, 0:w - NM], scalar=ATTN_SCALE,
                                       in1=lg[:, hd, NM:w], op0=ALU.mult, op1=ALU.add)
                last = V.scalar_tensor_tensor(out=lg[:, hd, 0:NM], in0=b6[:, NM * hd:NM * hd + NM], scalar=ATTN_SCALE,
                                              in1=lg[:, hd, 0:NM], op0=ALU.mult, op1=ALU.add)
                if i == 0:
                    last = V.scalar_tensor_tensor(out=lgm[:, hd, :], in0=b6[0:NM, 2 * NM + NM * hd:3 * NM + NM * hd],
                                                  scalar=ATTN_SCALE, in1=lgm[:, hd, :], op0=ALU.mult, op1=ALU.add)
            ch(last)
            last = V.tensor_reduce(nmx[:, 0, :], lg[:, :, 0:w], AX, ALU.max)
            if i == 0:
                last = V.tensor_reduce(nmxm[:, 0, :], lgm[:], AX, ALU.max)
            ch(last)
            if i == 0:
                ch(V.tensor_scalar(nmxm[:, 0, :], nmxm[:, 0, :], -1.0, None, ALU.mult))
            V.tensor_scalar(nmx[:, 0, :], nmx[:, 0, :], -1.0, None, ALU.mult).then_inc(sem("att_max"), 1)
            dve.wait_ge(sem("att_exp"), n + 1)
            last = V.reciprocal(nmx[:, 1, :], nmx[:, 1, :])
            if i == 0:
                last = V.reciprocal(nmxm[:, 1, :], nmxm[:, 1, :])
            ch(last)
            for hd in range(2):
                if i == 0:
                    V.tensor_scalar(lgm[:, hd, :], lgm[:, hd, :], nmxm[:, 1, hd:hd + 1], None, ALU.mult)
                last = V.tensor_scalar(lg[:, hd, 0:w], lg[:, hd, 0:w], nmx[:, 1, hd:hd + 1], None, ALU.mult)
            last.then_inc(sem("att_p"), 1)

        q = 3 * (NH - 1)
        for g in range(NG):
            for j in range(4):
                split(At(S_B + 4 * g + j + 1))
                if g == 0:
                    late(At(4 * NH - 4), NH - 1, j)
                    if j == 0:
                        V.memset(qpad[:], 0.0).then_inc(sem("qpad_clear"), 1)
                    if j < 2:
                        take_prompt(112 + 8 * j)
                    if j >= 2:
                        keep_prompt(2 * j - 4)
                        keep_prompt(2 * j - 3)
                else:
                    attend(4 * (g - 1) + j)
                    rounds = 1 if 4 * g + j <= 11 else 2 if j == 0 else 1
                    for r in range(rounds):
                        if q < KEEP_S // 8:
                            take_sample(4 * q, idx[:, 8 * q:8 * q + 8])
                            q += 1
                    if g == 3 and j == 2:
                        dve.wait_ge(sem("sstate_out"), 16 * NH)
                        dve.wait_ge(sem("state_out"), 16 * NH)
                        sample_rows()
                    if g == 3 and j == 3:
                        dve.wait_ge(sem("rows_turned"), 1)
                        V.tensor_copy(grow[:].rearrange("p k b -> p (k b)"), b7[:, 0:16]).then_inc(sem("grow_ready"), 1)

        def x_sum(k):
            if k >= 2:
                dve.wait_ge(sem("resid"), k - 1)
            V.tensor_tensor(tmp[:, k % 2, :], fr(xh[:, 8 + k, :]), fr(xl[:, 8 + k, :]), ALU.add).then_inc(sem("x_sum"), 1)

        def mix_rest(k):
            dve.wait_ge(sem("mix_h"), k + 1)
            V.tensor_tensor(xl[:, 8 + k, :], sacc[:, 8 + k, :], fr(xh[:, 8 + k, :]), ALU.subtract).then_inc(sem("mix_in"), 1)

        def add_mix(n, i):
            t = At(T_D1 + 2 * n + i)
            m = (2 * n + i + 8) % KD
            dve.wait_ge(sem("mm"), (t + 1).v)
            V.tensor_tensor(cut(sacc[:, m, :]), cut(sacc[:, m, :]), whole(t), ALU.add).then_inc(sem(f"acc_read{t.odd}"), 1)

        def sample_att(b):
            dve.wait_ge(sem("slog"), b + 1)
            ch(V.tensor_reduce(snm[:, 0:1], b6[0:NH, 0:KEEP_S + 1], AX, ALU.max))
            V.tensor_scalar(snm[:, 0:1], snm[:, 0:1], -1.0, None, ALU.mult).then_inc(sem("smax"), 1)
            dve.wait_ge(sem("sexp"), b + 1)
            ch(V.reciprocal(snm[:, 1:2], snm[:, 1:2]))
            ch(V.tensor_scalar(ps[:, :], ps[:, :], snm[:, 1:2], None, ALU.mult))
            V.tensor_scalar(pz[:], zt[:], ps[:, KEEP_S:KEEP_S + 1], None, ALU.mult).then_inc(sem("sp_ready"), 1)

        for n in range(8):
            if n == 0:
                x_sum(0)
                for k in range(8):
                    if k < 7:
                        x_sum(k + 1)
                    mix_rest(k)
            split(At(S_D1 + n + 1))
            if n >= 1:
                add_mix(n - 1, 1)
            if n == 1:
                for k in range(8):
                    dve.wait_ge(sem("resid_h"), k + 1)
                    V.scalar_tensor_tensor(out=sacc[:, k, :], in0=fr(xl[:, k, :]), scalar=ALPHA, in1=sacc[:, k, :],
                                           op0=ALU.mult, op1=ALU.add).then_inc(sem("resid_lo"), 1)
            if n < 4:
                attend(12 + n)
                add_mix(n, 0)
            else:
                sample_att(2 * (n - 4))
                add_mix(n, 0)
                sample_att(2 * (n - 4) + 1)

        dve.wait_ge(sem("so_out"), NS)
        for k in range(NH):
            dve.wait_ge(sem("att_h"), k + 1)
            V.tensor_tensor(xl[:, k, :], attn_o[:, k, :], fr(xh[:, k, :]), ALU.subtract).then_inc(sem("att_in"), 1)
        add_mix(7, 1)

        def tile_of(buf, m):
            k = m.const % KD
            return buf[:, k, :] if m.reg is None else buf[:, bass.ds(m.v, 1), :].rearrange("p o n -> p (o n)")

        def finish(m, t):
            dve.wait_ge(sem("mm"), (t + 1).v)
            dst = tile_of(sacc, m)
            V.tensor_tensor(cut(dst), cut(dst), whole(t), ALU.add).then_inc(sem("s_done"), 1)
            dve.wait_ge(sem("s_done"), (m + 1).v)
            dve.sem_inc(sem(f"acc_read{t.odd}"), 1)
            dve.wait_ge(sem("s_sum"), m.v)
            V.tensor_tensor(ssum[:, 0, :], ssum[:, 0, :], dst, ALU.add).then_inc(sem("s_sum"), 1)

        def finish_square(m):
            dve.wait_ge(sem("sq_done"), (m + 1).v)
            dve.wait_ge(sem("q_sum"), m.v)
            V.tensor_tensor(ssum[:, 1, :], ssum[:, 1, :], sq[:, m.const % 2, :], ALU.add).then_inc(sem("q_sum"), 1)

        ch(V.memset(ssum[:], 0.0))

        def d2(n2):
            for i in range(2):
                split(At(S_D2 + i + 1, 2, n2) if not isinstance(n2, int) else At(S_D2 + i + 1 + 2 * n2))
                for e in range(2):
                    m = At(2 * i + e, 4, n2) if not isinstance(n2, int) else At(2 * i + e + 4 * n2)
                    finish(m, m + T_D2)
                    finish_square(m)

        d2(0)
        with dve.Fori(1, 4, 1) as n2:
            d2(n2)

        def ln_stats(n):
            dve.wait_ge(sem("ln_sums"), n)
            for src, part in ((b4, slice(R0, NT)), (b5, slice(0, R0))):
                last = V.tensor_scalar(mu[:, part], src[:, 0:part.stop - part.start], 1.0 / D, None, ALU.mult)
            last.then_inc(sem("mu_ready"), 1)
            dve.wait_ge(sem("mu_ready"), n)
            ch(V.tensor_tensor(rstd[:, :], mu[:, :], mu[:, :], ALU.mult))
            for src, part in ((b6, slice(R0, NT)), (b7, slice(0, R0))):
                last = V.scalar_tensor_tensor(out=rstd[:, part], in0=src[:, 0:part.stop - part.start], scalar=1.0 / D,
                                              in1=rstd[:, part], op0=ALU.mult, op1=ALU.subtract)
            last.then_inc(sem("ln_var"), 1)

        def scaled(n, k):
            if n == 1 and k % 4 == 3:
                if k >= 4:
                    dve.wait_ge(sem("y_ready"), k - 3)
                ch(V.tensor_tensor(lnd[:, k % 4, :], sacc[:, k, :], mu[:, :], ALU.subtract))
            else:
                dve.wait_ge(sem("centered"), KD + 3 * (k // 4) + k % 4 + 1 if n else k + 1)
            if k == 0:
                dve.wait_ge(sem("ln_rstd"), n + 1)
            V.tensor_tensor(lnd[:, k % 4, :], lnd[:, k % 4, :], rstd[:, :], ALU.mult).then_inc(sem("ln_norm"), 1)

        split(At(S_E + 1))
        ln_stats(1)
        for k in range(KD):
            scaled(0, k)
            if k >= 1:
                dve.wait_ge(sem("x1_h"), k)
                V.tensor_tensor(xl[:, k - 1, :], sacc[:, k - 1, :], fr(xh[:, k - 1, :]), ALU.subtract).then_inc(sem("x1_in"), 1)
        dve.wait_ge(sem("x1_h"), KD)
        V.tensor_tensor(xl[:, KD - 1, :], sacc[:, KD - 1, :], fr(xh[:, KD - 1, :]), ALU.subtract).then_inc(sem("x1_in"), 1)
        ch(V.memset(ssum[:], 0.0))

        def hidden(u, t):
            dve.wait_ge(sem("mm"), (t + 1).v)
            dve.wait_ge(sem("gate_done"), (u + 1).v)
            if u.reg is not None or u.const >= 2:
                dve.wait_ge(sem("hl_done"), (u - 1).v)
            hb = hbuf[:, u.const % 2, :]
            V.tensor_tensor(cut(hb), whole(t), cut(gbuf[:, u.const % 2, :]), ALU.mult).then_inc(sem("gated"), 1)
            dve.wait_ge(sem("gated"), (u + 1).v)
            dve.sem_inc(sem(f"acc_read{t.odd}"), 1)
            dve.wait_ge(sem("hh_done"), (u + 1).v)
            V.tensor_tensor(hl[:, u.const % FC, :], hb, fr(hh[:, u.const % FC, :]), ALU.subtract).then_inc(sem("hl_done"), 1)

        def mlp(c):
            u0 = At(FC * c) if isinstance(c, int) else At(0, FC, c)
            for p_, (kind, f, s, t) in enumerate(mlp_plan(c)):
                if p_ == 0 and isinstance(c, int) and c == NC:
                    hidden(u0 - 1, t - 1)
                if not (p_ == 0 and isinstance(c, int) and c == 0) and not (kind == "down" and f == 3 and isinstance(c, int)):
                    split(s + 1)
                if p_ == 0 and not isinstance(c, int):
                    hidden(u0 - 1, t - 1)
                if kind == "gate" and f >= 1:
                    hidden(u0 + (f - 1), t - 1)
                if kind == "down":
                    for i in range(4):
                        m = 4 * f + i
                        if isinstance(c, int):
                            finish(At(16 + m), t + i)
                            finish_square(At(16 + m))
                        else:
                            t_ = t + i
                            dve.wait_ge(sem("mm"), (t_ + 1).v)
                            V.tensor_tensor(cut(sacc[:, m, :]), cut(sacc[:, m, :]), whole(t_), ALU.add)\
                                .then_inc(sem(f"acc_read{t_.odd}"), 1)

        mlp(0)
        dve.wait_ge(sem("x1_resid"), KD)
        with dve.Fori(1, NC, 1) as c:
            mlp(c)
        mlp(NC)
        ln_stats(2)
        for k in range(KD + 4):
            if k < KD:
                scaled(1, k)
            for u in y_after(k):
                if not y_on_act(u):
                    dve.wait_ge(sem("y_turned"), u + 1)
                    q, r = u // 5, P if u % 5 < 4 else NS
                    V.tensor_copy(ytok[0:r, u % 5, 512 * q:512 * q + 512], y_bank(u)[0:r]).then_inc(sem("y_dve"), 1)


OUTPUTS = (
    (1, NR, D), (NS, 1, D),
    (1, 1, NM + NR, NG, HD), (1, 1, NM + NR, NG, HD), (1, 1, NM + NR, 64), (1, 1, NH, HD, HD),
    (1, NS, 1, NG, HD), (1, NS, 1, NG, HD), (1, NS, 1, 64), (1, NS, NH, HD, HD),
)
INPUTS = (
    "x_prompt", "x_sample", "cache_k", "cache_v", "cache_kidx", "state_hgrn", "page_table", "meta_tokens",
    "ln_in_g", "ln_in_b", "w_in", "hg_lb_logits", "hg_norm_g", "w_out", "ln1_g", "ln1_b",
    "w_gate", "w_up", "w_down", "ln2_g", "ln2_b",
)


def kernel(**inputs):
    import numpy as _np
    import concourse.bacc as _bacc
    from concourse import mybir as _mybir
    from concourse.bass_utils import run_bass_kernel_spmd as _run

    nc = _bacc.Bacc("TRN2", target_bir_lowering=False, num_devices=1)
    arrays, args = {}, []
    for name in INPUTS:
        a = _np.ascontiguousarray(inputs[name])
        arrays[f"in_{name}_dram"] = a
        args.append(nc.dram_tensor(f"in_{name}_dram", a.shape, _mybir.dt.from_np(a.dtype), kind="ExternalInput").ap())
    for i, shape in enumerate(OUTPUTS):
        args.append(nc.dram_tensor(f"out_{i}_dram", shape, _mybir.dt.float32, kind="ExternalOutput").ap())
    hymba_kernel(nc, *args)
    r = _run(nc, [arrays], core_ids=[0])
    return tuple(r.results[0][f"out_{i}_dram"] for i in range(len(OUTPUTS)))
```
